# Optimizing a Trainium2 kernel written in Bass

```python
import jax, jax.numpy as jnp
from jax import lax
import numpy as np
import jax
import jax.numpy as jnp

D_MODEL = 1024
BATCH = 1
SEQ = 512
DEPTH = 1

CHUNK = 64
EPS = 1e-6
N_BRANCH = 2
CONV_DIM = D_MODEL
CONV_WIDTH = 3
SSM_EXPAND = 2
D_SSM = SSM_EXPAND * D_MODEL
SSM_HEAD_DIM = 64
SSM_HEADS = D_SSM // SSM_HEAD_DIM
SSM_GROUPS = 8
SSM_STATE = 128
SSM_CONV_WIDTH = 4
SSM_CONV_DIM = D_SSM + 2 * SSM_GROUPS * SSM_STATE
DT_MIN = 1e-3
DT_MAX = 1e-1
D_FF = 4 * D_MODEL
N_MOD = 6


def proj_sizes():
    return (N_BRANCH * D_MODEL,
            CONV_DIM, CONV_DIM, CONV_DIM,
            D_SSM,
            SSM_CONV_DIM,
            SSM_HEADS)

def rms_norm(x, w):
    xf = x.astype(jnp.float32)
    y = xf * lax.rsqrt(jnp.mean(xf * xf, axis=-1, keepdims=True) + EPS)
    return (y * w.astype(jnp.float32)).astype(x.dtype)

def causal_depthwise_conv(x, w):
    k = w.shape[0]
    return lax.conv_general_dilated(
        x, w[:, None, :].astype(x.dtype), window_strides=(1,), padding=((k - 1, 0),),
        dimension_numbers=('NWC', 'WIO', 'NWC'), feature_group_count=x.shape[-1])

def ssd_scan(x, a, b, c):
    bsz, seqlen, h, p = x.shape
    g, n = b.shape[-2:]
    r = h // g
    nc = seqlen // CHUNK

    def to_chunks(t):
        return jnp.moveaxis(t.reshape(bsz, nc, CHUNK, *t.shape[2:]), 1, 0)

    xs = (to_chunks(x.reshape(bsz, seqlen, g, r, p)),
          to_chunks(a.reshape(bsz, seqlen, g, r)),
          to_chunks(b), to_chunks(c))
    tril = jnp.tril(jnp.ones((CHUNK, CHUNK), dtype=bool))[None, :, :, None, None]

    def step(state, inp):
        xq, aq, bq, cq = inp
        a_cum = jnp.cumsum(aq, axis=1)
        seg = a_cum[:, :, None] - a_cum[:, None, :]
        decay = jnp.exp(jnp.where(tril, seg, -jnp.inf))
        scores = jnp.einsum('btgn,bsgn->btsg', cq, bq)
        y_diag = jnp.einsum('btsg,btsgr,bsgrp->btgrp', scores, decay, xq)
        y_off = jnp.einsum('btgn,bgrpn->btgrp', cq, state) * jnp.exp(a_cum)[..., None]
        to_end = jnp.exp(a_cum[:, -1:] - a_cum)
        new_state = (state * jnp.exp(a_cum[:, -1])[..., None, None]
                     + jnp.einsum('bsgn,bsgr,bsgrp->bgrpn', bq, to_end, xq))
        return new_state, y_diag + y_off

    state0 = jnp.zeros((bsz, g, r, p, n), jnp.float32)
    _, y = lax.scan(step, state0, xs)
    return jnp.moveaxis(y, 0, 1).reshape(bsz, seqlen, h, p)

def mixer_sublayer(u, w_in, conv_w, ssm_conv_w, ssm_conv_b, dt_bias, a_log, d_skip,
                   ssm_norm_w, w_conv_out, w_ssm_out, w_o):
    bsz, seqlen, _ = u.shape
    proj = u @ w_in
    split_at = [int(v) for v in np.cumsum(proj_sizes())[:-1]]
    gl, cb, cc, cx, z, xbc, dt = jnp.split(proj, split_at, axis=-1)

    y_conv = cb * causal_depthwise_conv(cc * cx, conv_w)
    p_conv = y_conv @ w_conv_out

    xbc = jax.nn.silu(causal_depthwise_conv(xbc, ssm_conv_w) + ssm_conv_b.astype(xbc.dtype))
    xbc = xbc.astype(jnp.float32)
    xs, bs, cs = jnp.split(xbc, [D_SSM, D_SSM + SSM_GROUPS * SSM_STATE], axis=-1)
    xs = xs.reshape(bsz, seqlen, SSM_HEADS, SSM_HEAD_DIM)
    bs = bs.reshape(bsz, seqlen, SSM_GROUPS, SSM_STATE)
    cs = cs.reshape(bsz, seqlen, SSM_GROUPS, SSM_STATE)
    dt = jax.nn.softplus(dt.astype(jnp.float32) + dt_bias.astype(jnp.float32))
    a = -jnp.exp(a_log.astype(jnp.float32))
    y = ssd_scan(xs * dt[..., None], dt * a, bs, cs)
    y = y + d_skip.astype(jnp.float32)[:, None] * xs
    y = y.reshape(bsz, seqlen, D_SSM) * jax.nn.silu(z.astype(jnp.float32))
    yg = y.reshape(bsz, seqlen, SSM_GROUPS, D_SSM // SSM_GROUPS)
    yg = yg * lax.rsqrt(jnp.mean(yg * yg, axis=-1, keepdims=True) + EPS)
    y = (yg.reshape(bsz, seqlen, D_SSM) * ssm_norm_w.astype(jnp.float32)).astype(u.dtype)
    p_ssm = y @ w_ssm_out

    g_conv, g_ssm = jnp.split(jax.nn.sigmoid(gl), 2, axis=-1)
    merged = g_conv * p_conv + g_ssm * p_ssm
    return merged @ w_o

def first_inputs(seed: int = 0) -> dict:
    key = jax.random.key(seed)
    ks = jax.random.split(key, 24)
    d_proj = sum(proj_sizes())
    f32 = jnp.float32

    def nrm(k, shape, scale):
        return jax.random.normal(k, shape, f32) * scale

    dt0 = jnp.exp(jax.random.uniform(ks[10], (DEPTH, SSM_HEADS), f32,
                                     np.log(DT_MIN), np.log(DT_MAX)))
    dt_bias = dt0 + jnp.log(-jnp.expm1(-dt0))
    return {
        "x": nrm(ks[0], (BATCH, SEQ, D_MODEL), 1.0),
        "c": nrm(ks[1], (BATCH, D_MODEL), 1.0),
        "w_ada": nrm(ks[2], (DEPTH, D_MODEL, N_MOD * D_MODEL), 0.5 * D_MODEL ** -0.5),
        "b_ada": nrm(ks[3], (DEPTH, N_MOD * D_MODEL), 0.02),
        "ln1": 1.0 + nrm(ks[4], (DEPTH, D_MODEL), 0.1),
        "ln2": 1.0 + nrm(ks[5], (DEPTH, D_MODEL), 0.1),
        "w_in": nrm(ks[6], (DEPTH, D_MODEL, d_proj), D_MODEL ** -0.5),
        "conv_w": nrm(ks[7], (DEPTH, CONV_WIDTH, CONV_DIM), CONV_WIDTH ** -0.5),
        "ssm_conv_w": nrm(ks[8], (DEPTH, SSM_CONV_WIDTH, SSM_CONV_DIM), SSM_CONV_WIDTH ** -0.5),
        "ssm_conv_b": nrm(ks[9], (DEPTH, SSM_CONV_DIM), 0.01),
        "dt_bias": dt_bias,
        "a_log": jnp.log(jax.random.uniform(ks[11], (DEPTH, SSM_HEADS), f32, 1.0, 16.0)),
        "d_skip": 1.0 + nrm(ks[12], (DEPTH, SSM_HEADS), 0.1),
        "ssm_norm_w": 1.0 + nrm(ks[13], (DEPTH, D_SSM), 0.1),
        "w_conv_out": nrm(ks[14], (DEPTH, CONV_DIM, D_MODEL), CONV_DIM ** -0.5),
        "w_ssm_out": nrm(ks[15], (DEPTH, D_SSM, D_MODEL), D_SSM ** -0.5),
        "w_o": nrm(ks[16], (DEPTH, D_MODEL, D_MODEL), D_MODEL ** -0.5),
        "w_up": nrm(ks[17], (DEPTH, D_MODEL, D_FF), D_MODEL ** -0.5),
        "w_down": nrm(ks[18], (DEPTH, D_FF, D_MODEL), D_FF ** -0.5),
        "final_norm": 1.0 + nrm(ks[19], (D_MODEL,), 0.1),
    }

def first_block(x, c, w_ada, b_ada, ln1, ln2, w_in, conv_w, ssm_conv_w, ssm_conv_b,
              dt_bias, a_log, d_skip, ssm_norm_w, w_conv_out, w_ssm_out, w_o,
              w_up, w_down, final_norm):
    bsz = x.shape[0]
    c_act = jax.nn.silu(c)
    for i in range(DEPTH):
        mod = (c_act @ w_ada[i] + b_ada[i]).reshape(bsz, N_MOD, D_MODEL)[:, :, None, :]
        shift1, scale1, gate1 = mod[:, 0], mod[:, 1], mod[:, 2]
        shift2, scale2, gate2 = mod[:, 3], mod[:, 4], mod[:, 5]

        u = rms_norm(x, ln1[i]) * (1.0 + scale1) + shift1
        mix = mixer_sublayer(u, w_in[i], conv_w[i], ssm_conv_w[i], ssm_conv_b[i], dt_bias[i],
                             a_log[i], d_skip[i], ssm_norm_w[i], w_conv_out[i],
                             w_ssm_out[i], w_o[i])
        x = x + gate1 * mix

        u2 = rms_norm(x, ln2[i]) * (1.0 + scale2) + shift2
        hid = jnp.square(jax.nn.relu(u2 @ w_up[i]))
        x = x + gate2 * (hid @ w_down[i])
    return rms_norm(x, final_norm)


GRID_W = 64
CTX_LEN = 256
N_MIXERS = 3
D_FF_2 = 4 * D_MODEL
N_DIRS = 2

GLA_HEADS = 4
GLA_DK = D_MODEL // 2
GLA_DV = D_MODEL
GLA_HK = GLA_DK // GLA_HEADS
GLA_HV = GLA_DV // GLA_HEADS
GLA_IN = 2 * GLA_DK + 2 * GLA_DV
GLA_GATE_RANK = 16
GLA_TAU = 16.0
GLA_CHUNK = 64

MLSTM_HEADS = 4
MLSTM_INNER = 2 * D_MODEL
MLSTM_HD = MLSTM_INNER // MLSTM_HEADS
MLSTM_QKV_BLOCK = 4
MLSTM_N_BLOCKS = MLSTM_INNER // MLSTM_QKV_BLOCK
MLSTM_CONV = 4
MLSTM_CHUNK = 64

POOL_WINDOWS = (2, 4, 8, 16)
POOL_GROUP = D_MODEL // len(POOL_WINDOWS)


def rmsnorm(x, g):
    xf = x.astype(jnp.float32)
    y = xf * lax.rsqrt(jnp.mean(xf * xf, axis=-1, keepdims=True) + EPS)
    return (y * g.astype(jnp.float32)).astype(x.dtype)

def modulate(h, shift, scale):
    return h * (1 + scale) + shift

def head_rmsnorm(o, g):
    return o * lax.rsqrt(jnp.mean(o * o, axis=-1, keepdims=True) + EPS) * g.astype(jnp.float32)

def head_layernorm(o, g):
    mu = jnp.mean(o, axis=-1, keepdims=True)
    oc = o - mu
    return oc * lax.rsqrt(jnp.mean(oc * oc, axis=-1, keepdims=True) + EPS) * g.astype(jnp.float32)

def to_chunks(t, size):
    b, n = t.shape[0], t.shape[1] // size
    t = t.reshape((b, n, size) + t.shape[2:])
    return t.transpose((1, 0, 3, 2) + tuple(range(4, t.ndim)))

def from_chunks(t):
    n, b, h, c, d = t.shape
    return t.transpose(1, 0, 3, 2, 4).reshape(b, n * c, h, d)

def gla_chunk_scan(q, k, v, log_a, s0):
    f32 = jnp.float32
    qc, kc, vc, gc = (to_chunks(t.astype(f32), GLA_CHUNK) for t in (q, k, v, log_a))
    tri = jnp.tril(jnp.ones((GLA_CHUNK, GLA_CHUNK), dtype=bool))

    def step(s, blk):
        qb, kb, vb, gb = blk
        b = jnp.cumsum(gb, axis=2)
        b_last = b[:, :, -1:, :]
        q_dec = qb * jnp.exp(b)
        att = jnp.where(tri, jnp.einsum('bhtd,bhsd->bhts', q_dec, kb * jnp.exp(-b)), 0.0)
        o = jnp.einsum('bhts,bhsv->bhtv', att, vb) + jnp.einsum('bhtd,bhdv->bhtv', q_dec, s)
        s_new = (jnp.exp(b_last[:, :, 0, :])[..., None] * s
                 + jnp.einsum('bhsd,bhsv->bhdv', kb * jnp.exp(b_last - b), vb))
        return s_new, o

    s_fin, o = lax.scan(step, s0, (qc, kc, vc, gc))
    return from_chunks(o), s_fin

def mlstm_chunk_scan(q, k, v, log_i, log_f, state):
    f32 = jnp.float32
    qc, kc, vc = (to_chunks(t.astype(f32), MLSTM_CHUNK) for t in (q, k, v))
    ic, fc = (to_chunks(t.astype(f32), MLSTM_CHUNK) for t in (log_i, log_f))
    tri = jnp.tril(jnp.ones((MLSTM_CHUNK, MLSTM_CHUNK), dtype=bool))

    def step(carry, blk):
        c_bar, n_bar, m_prev = carry
        qb, kb, vb, ib, fb = blk
        b = jnp.cumsum(fb, axis=-1)
        d_mat = jnp.where(tri, b[..., :, None] - b[..., None, :] + ib[..., None, :], -jnp.inf)
        inter = b + m_prev[..., None]
        m_row = jnp.maximum(jnp.max(d_mat, axis=-1), inter)
        w_qk = jnp.einsum('bhtd,bhsd->bhts', qb, kb) * jnp.exp(d_mat - m_row[..., None])
        w_inter = jnp.exp(inter - m_row)
        num = (jnp.einsum('bhts,bhsv->bhtv', w_qk, vb)
               + w_inter[..., None] * jnp.einsum('bhtd,bhdv->bhtv', qb, c_bar))
        den = jnp.sum(w_qk, axis=-1) + w_inter * jnp.einsum('bhtd,bhd->bht', qb, n_bar)
        h = num / jnp.maximum(jnp.abs(den), jnp.exp(-m_row))[..., None]
        carry_log = b[..., -1] + m_prev
        tok_log = b[..., -1:] - b + ib
        m_new = jnp.maximum(carry_log, jnp.max(tok_log, axis=-1))
        w_tok = jnp.exp(tok_log - m_new[..., None])
        w_carry = jnp.exp(carry_log - m_new)
        k_w = kb * w_tok[..., None]
        c_new = w_carry[..., None, None] * c_bar + jnp.einsum('bhsd,bhsv->bhdv', k_w, vb)
        n_new = w_carry[..., None] * n_bar + jnp.sum(k_w, axis=2)
        return (c_new, n_new, m_new), h

    state_fin, h = lax.scan(step, state, (qc, kc, vc, ic, fc))
    return from_chunks(h), state_fin

def bidirectional_scan(scan_fn, ctx_dirs, lat_dirs, init):
    rev = lambda t: jnp.flip(t, axis=1)
    out_ctx, out_lat = [], []
    for direction in range(N_DIRS):
        ca, la = ctx_dirs[direction], lat_dirs[direction]
        if direction == 1:
            ca = tuple(rev(t) for t in ca)
            la = tuple(rev(t) for t in la)
        o_c, state = scan_fn(*ca, init)
        o_l, _ = scan_fn(*la, state)
        if direction == 1:
            o_c, o_l = rev(o_c), rev(o_l)
        out_ctx.append(o_c)
        out_lat.append(o_l)
    return out_ctx[0] + out_ctx[1], out_lat[0] + out_lat[1]

def gla_mixer(a_ctx, a_lat, w_in, w_a1, w_a2, b_a, g_head, w_o, need_ctx):
    def project(a):
        B, T, _ = a.shape
        q, k, v, r = jnp.split(a @ w_in, [GLA_DK, 2 * GLA_DK, 2 * GLA_DK + GLA_DV], axis=-1)
        q = q.reshape(B, T, GLA_HEADS, GLA_HK) * GLA_HK ** -0.5
        k = k.reshape(B, T, GLA_HEADS, GLA_HK)
        v = v.reshape(B, T, GLA_HEADS, GLA_HV)
        dirs = []
        for d in range(N_DIRS):
            z = (a @ w_a1[d]) @ w_a2[d] + b_a[d]
            log_a = jax.nn.log_sigmoid(z.astype(jnp.float32)) / GLA_TAU
            dirs.append((q, k, v, log_a.reshape(B, T, GLA_HEADS, GLA_HK)))
        return dirs, r

    def finish(o, r):
        B, T = o.shape[:2]
        o = head_rmsnorm(o, g_head).reshape(B, T, GLA_DV).astype(r.dtype)
        return (o * jax.nn.silu(r)) @ w_o

    ctx_dirs, r_ctx = project(a_ctx)
    lat_dirs, r_lat = project(a_lat)
    s0 = jnp.zeros((a_lat.shape[0], GLA_HEADS, GLA_HK, GLA_HV), jnp.float32)
    o_ctx, o_lat = bidirectional_scan(gla_chunk_scan, ctx_dirs, lat_dirs, s0)
    out_ctx = finish(o_ctx, r_ctx) if need_ctx else None
    return out_ctx, finish(o_lat, r_lat)

def centred_conv(x, w, b):
    K = w.shape[0]
    y = lax.conv_general_dilated(x, w[:, None, :], window_strides=(1,),
                                 padding=[(K // 2, K - 1 - K // 2)],
                                 dimension_numbers=('NWC', 'WIO', 'NWC'),
                                 feature_group_count=x.shape[-1])
    return y + b

def headwise(t, w):
    B, T, _ = t.shape
    t = t.reshape(B, T, MLSTM_N_BLOCKS, MLSTM_QKV_BLOCK)
    return jnp.einsum('btni,nij->btnj', t, w).reshape(B, T, MLSTM_INNER)

def mlstm_mixer(a_ctx, a_lat, w_up, conv_w, conv_b, w_qkv, w_gate, b_gate, g_norm, skip, w_down, need_ctx):
    H = MLSTM_HEADS

    def project(a):
        B, T, _ = a.shape
        xm, z = jnp.split(a @ w_up, 2, axis=-1)
        xc = jax.nn.silu(centred_conv(xm, conv_w, conv_b))
        q = headwise(xc, w_qkv[0])
        k = headwise(xc, w_qkv[1])
        v = headwise(xm, w_qkv[2])
        gin = jnp.concatenate([q, k, v], axis=-1)
        heads = lambda t: t.reshape(B, T, H, MLSTM_HD)
        qh, kh, vh = heads(q), heads(k) * MLSTM_HD ** -0.5, heads(v)
        dirs = []
        for d in range(N_DIRS):
            g = (gin @ w_gate[d] + b_gate[d]).astype(jnp.float32)
            dirs.append((qh, kh, vh, g[..., :H], jax.nn.log_sigmoid(g[..., H:])))
        return dirs, xc, z

    def finish(h, xc, z):
        B, T = h.shape[:2]
        hn = head_layernorm(h, g_norm).reshape(B, T, MLSTM_INNER).astype(xc.dtype)
        return ((hn + skip * xc) * jax.nn.silu(z)) @ w_down

    ctx_dirs, xc_ctx, z_ctx = project(a_ctx)
    lat_dirs, xc_lat, z_lat = project(a_lat)
    B = a_lat.shape[0]
    init = (jnp.zeros((B, H, MLSTM_HD, MLSTM_HD), jnp.float32),
            jnp.zeros((B, H, MLSTM_HD), jnp.float32),
            jnp.zeros((B, H), jnp.float32))
    h_ctx, h_lat = bidirectional_scan(mlstm_chunk_scan, ctx_dirs, lat_dirs, init)
    out_ctx = finish(h_ctx, xc_ctx, z_ctx) if need_ctx else None
    return out_ctx, finish(h_lat, xc_lat, z_lat)

def box_mean(x, axis, window):
    length = x.shape[axis]
    pad = [(0, 0)] * x.ndim
    pad[axis] = (1, 0)
    cs = jnp.pad(jnp.cumsum(x.astype(jnp.float32), axis=axis), pad)
    pos = jnp.arange(length)
    lo = jnp.maximum(pos - window // 2, 0)
    hi = jnp.minimum(pos + (window - window // 2), length)
    total = jnp.take(cs, hi, axis=axis) - jnp.take(cs, lo, axis=axis)
    shape = [1] * x.ndim
    shape[axis] = length
    return total / (hi - lo).astype(jnp.float32).reshape(shape)

def pool_mixer(a_ctx, a_lat, w_pool, b_pool, scale, need_ctx):
    B, T, D = a_lat.shape
    rows = T // GRID_W
    grid = a_lat.reshape(B, rows, GRID_W, D)
    lat_parts, ctx_parts = [], []
    for g, win in enumerate(POOL_WINDOWS):
        sl = slice(g * POOL_GROUP, (g + 1) * POOL_GROUP)
        hg = grid[..., sl]
        pooled = box_mean(box_mean(hg, 2, win), 1, win).astype(hg.dtype) - hg
        lat_parts.append(pooled.reshape(B, T, POOL_GROUP) @ w_pool[g] + b_pool[g])
        if need_ctx:
            cg = a_ctx[..., sl]
            pooled_c = box_mean(cg, 1, win).astype(cg.dtype) - cg
            ctx_parts.append(pooled_c @ w_pool[g] + b_pool[g])
    out_lat = jnp.concatenate(lat_parts, axis=-1) * scale
    out_ctx = jnp.concatenate(ctx_parts, axis=-1) * scale if need_ctx else None
    return out_ctx, out_lat

def sqrelu_mlp(h, w1, w2):
    return jnp.square(jax.nn.relu(h @ w1)) @ w2

def second_inputs(seed: int = 0) -> dict:
    key = jax.random.key(seed)
    keys = iter(jax.random.split(key, 48))

    def normal(shape, scale):
        return jax.random.normal(next(keys), shape, jnp.float32) * scale

    def gain(shape):
        return 1.0 + normal(shape, 0.02)

    n_gla = sum(1 for i in range(DEPTH) if i % N_MIXERS == 0)
    n_mlstm = sum(1 for i in range(DEPTH) if i % N_MIXERS == 1)
    n_pool = sum(1 for i in range(DEPTH) if i % N_MIXERS == 2)
    d = D_MODEL
    gate_i = normal((n_mlstm, N_DIRS, MLSTM_HEADS), 0.1)
    gate_f = jnp.linspace(3.0, 6.0, MLSTM_HEADS, dtype=jnp.float32) + normal((n_mlstm, N_DIRS, MLSTM_HEADS), 0.1)
    return {
        'x': normal((BATCH, SEQ, d), 1.0),
        'c': normal((BATCH, d), 1.0),
        'ctx': normal((BATCH, CTX_LEN, d), 1.0),
        'c_ctx': normal((d,), 1.0),
        'ada_w': normal((DEPTH, d, 6 * d), 0.5 * d ** -0.5),
        'ada_b': normal((DEPTH, 6 * d), 0.01),
        'norm1_g': gain((DEPTH, d)),
        'norm2_g': gain((DEPTH, d)),
        'mlp_w1': normal((DEPTH, d, D_FF_2), d ** -0.5),
        'mlp_w2': normal((DEPTH, D_FF_2, d), D_FF_2 ** -0.5),
        'gla_w_in': normal((n_gla, d, GLA_IN), d ** -0.5),
        'gla_w_a1': normal((n_gla, N_DIRS, d, GLA_GATE_RANK), d ** -0.5),
        'gla_w_a2': normal((n_gla, N_DIRS, GLA_GATE_RANK, GLA_DK), GLA_GATE_RANK ** -0.5),
        'gla_b_a': normal((n_gla, N_DIRS, GLA_DK), 0.1),
        'gla_g_head': gain((n_gla, GLA_HEADS, GLA_HV)),
        'gla_w_o': normal((n_gla, GLA_DV, d), GLA_DV ** -0.5),
        'mlstm_w_up': normal((n_mlstm, d, 2 * MLSTM_INNER), d ** -0.5),
        'mlstm_conv_w': normal((n_mlstm, MLSTM_CONV, MLSTM_INNER), MLSTM_CONV ** -0.5),
        'mlstm_conv_b': normal((n_mlstm, MLSTM_INNER), 0.01),
        'mlstm_w_qkv': normal((n_mlstm, 3, MLSTM_N_BLOCKS, MLSTM_QKV_BLOCK, MLSTM_QKV_BLOCK), MLSTM_QKV_BLOCK ** -0.5),
        'mlstm_w_gate': normal((n_mlstm, N_DIRS, 3 * MLSTM_INNER, 2 * MLSTM_HEADS), (3 * MLSTM_INNER) ** -0.5),
        'mlstm_b_gate': jnp.concatenate([gate_i, gate_f], axis=-1),
        'mlstm_g_norm': gain((n_mlstm, MLSTM_HEADS, MLSTM_HD)),
        'mlstm_skip': gain((n_mlstm, MLSTM_INNER)),
        'mlstm_w_down': normal((n_mlstm, MLSTM_INNER, d), MLSTM_INNER ** -0.5),
        'pool_w': normal((n_pool, len(POOL_WINDOWS), POOL_GROUP, POOL_GROUP), POOL_GROUP ** -0.5),
        'pool_b': normal((n_pool, len(POOL_WINDOWS), POOL_GROUP), 0.01),
        'pool_scale': gain((n_pool, d)),
        'final_g': gain((d,)),
    }

def second_block(x, c, ctx, c_ctx, ada_w, ada_b, norm1_g, norm2_g, mlp_w1, mlp_w2,
              gla_w_in, gla_w_a1, gla_w_a2, gla_b_a, gla_g_head, gla_w_o,
              mlstm_w_up, mlstm_conv_w, mlstm_conv_b, mlstm_w_qkv, mlstm_w_gate, mlstm_b_gate,
              mlstm_g_norm, mlstm_skip, mlstm_w_down,
              pool_w, pool_b, pool_scale, final_g):
    silu_c = jax.nn.silu(c)
    silu_cc = jax.nn.silu(c_ctx)
    h_lat, h_ctx = x, ctx
    for i in range(DEPTH):
        kind, j = i % N_MIXERS, i // N_MIXERS
        need_ctx = i < DEPTH - 1
        mod_l = jnp.split((silu_c @ ada_w[i] + ada_b[i])[:, None, :], 6, axis=-1)
        mod_c = jnp.split((silu_cc @ ada_w[i] + ada_b[i])[None, None, :], 6, axis=-1)
        a_lat = modulate(rmsnorm(h_lat, norm1_g[i]), mod_l[0], mod_l[1])
        a_ctx = modulate(rmsnorm(h_ctx, norm1_g[i]), mod_c[0], mod_c[1])
        if kind == 0:
            o_ctx, o_lat = gla_mixer(a_ctx, a_lat, gla_w_in[j], gla_w_a1[j], gla_w_a2[j], gla_b_a[j],
                                     gla_g_head[j], gla_w_o[j], need_ctx)
        elif kind == 1:
            o_ctx, o_lat = mlstm_mixer(a_ctx, a_lat, mlstm_w_up[j], mlstm_conv_w[j], mlstm_conv_b[j],
                                       mlstm_w_qkv[j], mlstm_w_gate[j], mlstm_b_gate[j],
                                       mlstm_g_norm[j], mlstm_skip[j], mlstm_w_down[j], need_ctx)
        else:
            o_ctx, o_lat = pool_mixer(a_ctx, a_lat, pool_w[j], pool_b[j], pool_scale[j], need_ctx)
        h_lat = h_lat + mod_l[2] * o_lat
        h_lat = h_lat + mod_l[5] * sqrelu_mlp(modulate(rmsnorm(h_lat, norm2_g[i]), mod_l[3], mod_l[4]),
                                              mlp_w1[i], mlp_w2[i])
        if need_ctx:
            h_ctx = h_ctx + mod_c[2] * o_ctx
            h_ctx = h_ctx + mod_c[5] * sqrelu_mlp(modulate(rmsnorm(h_ctx, norm2_g[i]), mod_c[3], mod_c[4]),
                                                  mlp_w1[i], mlp_w2[i])
    return rmsnorm(h_lat, final_g)


def setup_inputs(seed=0):
    out = dict(first_inputs(seed))
    for name, value in second_inputs(seed + 1).items():
        if name != "x":
            out[name + "_2"] = value
    return out


def reference(
    x, c, w_ada, b_ada, ln1, ln2, w_in, conv_w, ssm_conv_w, ssm_conv_b, dt_bias, a_log, d_skip,
    ssm_norm_w, w_conv_out, w_ssm_out, w_o, w_up, w_down, final_norm, c_2, ctx_2, c_ctx_2,
    ada_w_2, ada_b_2, norm1_g_2, norm2_g_2, mlp_w1_2, mlp_w2_2, gla_w_in_2, gla_w_a1_2,
    gla_w_a2_2, gla_b_a_2, gla_g_head_2, gla_w_o_2, mlstm_w_up_2, mlstm_conv_w_2,
    mlstm_conv_b_2, mlstm_w_qkv_2, mlstm_w_gate_2, mlstm_b_gate_2, mlstm_g_norm_2, mlstm_skip_2,
    mlstm_w_down_2, pool_w_2, pool_b_2, pool_scale_2, final_g_2,
):
    x = first_block(
        x, c, w_ada, b_ada, ln1, ln2, w_in, conv_w, ssm_conv_w, ssm_conv_b, dt_bias, a_log,
        d_skip, ssm_norm_w, w_conv_out, w_ssm_out, w_o, w_up, w_down, final_norm,
    )
    return second_block(
        x, c_2, ctx_2, c_ctx_2, ada_w_2, ada_b_2, norm1_g_2, norm2_g_2, mlp_w1_2, mlp_w2_2,
        gla_w_in_2, gla_w_a1_2, gla_w_a2_2, gla_b_a_2, gla_g_head_2, gla_w_o_2, mlstm_w_up_2,
        mlstm_conv_w_2, mlstm_conv_b_2, mlstm_w_qkv_2, mlstm_w_gate_2, mlstm_b_gate_2,
        mlstm_g_norm_2, mlstm_skip_2, mlstm_w_down_2, pool_w_2, pool_b_2, pool_scale_2,
        final_g_2,
    )


_drawn_inputs = setup_inputs


def setup_inputs(seed=0):
    import zlib

    import numpy as np

    out = dict(_drawn_inputs(seed))
    spreads = {}
    factors = {'ssm_conv_b': 8.0,
     'd_skip': 6.867,
     'ssm_norm_w': 3.193,
     'c_ctx_2': 3.812,
     'ada_b_2': 3.274,
     'norm1_g_2': 6.783,
     'norm2_g_2': 19.283,
     'gla_b_a_2': 5.661,
     'gla_g_head_2': 8.0,
     'final_g_2': 7.805}
    for name, (base, spread) in spreads.items():
        noise = np.random.default_rng([zlib.crc32(name.encode()), seed]).standard_normal(out[name].shape)
        drawn = base * np.exp(spread * noise) if base else spread * noise
        out[name] = jnp.asarray(drawn.astype(out[name].dtype))
    for name, factor in factors.items():
        out[name] = (out[name] * factor).astype(out[name].dtype)
    return out
```

```python
import concourse.bass as bass
from concourse import mybir
from contextlib import ExitStack

P = 128
D = 1024
T = 512
TC = 256
TA = T + TC
KT = D // P
SSM_GROUPS = 8
HEADS = 32
CH = 128
NCH = T // CH
NGLA = 4
GV = 256
GC = 64
TAU = 16.0
EPS = 1e-6
SLOTS = 4
RAW = 2
AHEAD = SLOTS - 1

PHASES = [
    ("ssm0", 6, [0, 1, 2, 3, 0, 1], 1),
    ("ssm", 12, [2, 3, 0, 1, 2, 3, 0, 1, 2, 3, 0, 1], 3),
    ("ssm7", 6, [2, 3, 0, 1, 2, 3], 1),
    ("gate_ssm", 8, [0, 1, 2, 3, 0, 1, 2, 3], 1),
    ("ssm_out", 4, [0, 1], 4),
    ("conv", 4, [0, 1, 2, 3], 8),
    ("conv_out", 4, [0, 1, 2, 3], 2),
    ("w_o", 4, [0, 1, 2, 3], 2),
    ("up1a", 4, [0, 1, 2, 3], 4), ("down1a", 4, [0, 1], 4),
    ("up1b", 4, [0, 1, 2, 3], 4), ("down1b", 4, [0, 1], 4),
    ("gla_q", 4, [0, 1, 2, 3], 1), ("gla_r", 4, [0, 1, 2, 3], 2),
    ("gla_k", 4, [0, 1, 2, 3], 1), ("gla_v", 8, [0, 1, 2, 3, 0, 1, 2, 3], 1),
    ("gla_o", 4, [0, 1, 2, 3], 2),
    ("up2a", 4, [0, 1, 2, 3], 4), ("down2a", 4, [0, 1], 4),
    ("up2b", 4, [0, 1, 2, 3], 4), ("down2b", 4, [0, 1], 4),
]


def phase_table():
    table, unit, used = {}, 0, [0, 0, 0, 0]
    for name, n, banks, steps in PHASES:
        table[name] = dict(u0=unit, n=n, steps=steps, banks=banks, used=list(used),
                           per=[banks.count(b) for b in range(4)])
        unit += n * steps
        for b in range(4):
            used[b] += banks.count(b) * steps
    table["end"] = dict(u0=unit)
    return table


PH = phase_table()
UNITS = PH["end"]["u0"]

PARAMS = [("b_ada", 48), ("ln1", 8), ("ln2", 8), ("conv_w", 24), ("ssm_w", 128), ("ssm_b", 32),
          ("ssm_norm", 16), ("d_skip", 16), ("dt_bias", 1), ("a_log", 1), ("final_norm", 8), ("c", 8),
          ("c_2", 8), ("c_ctx", 8), ("b_ada_2", 48), ("norm1", 8), ("norm2", 8), ("b_a", 8),
          ("g_head", 8), ("final_2", 8)]
PCOL, _at = {}, 0
for _n, _w in PARAMS:
    PCOL[_n] = _at
    _at += _w
NPAR = _at
CONSTS = [("ident", 128), ("ones", 128), ("last_row", 128), ("causal_add", 128), ("resets", 512)]
CCOL, _at = {}, 0
for _n, _w in CONSTS:
    CCOL[_n] = _at
    _at += _w
NCON = _at
GCON = [("reset_f", TA), ("reset_b", TA), ("mask_f", 128), ("mask_b", 128)]
GCOL, _at = {}, 0
for _n, _w in GCON:
    GCOL[_n] = _at
    _at += _w
NGCON = _at


def build(nc, xT, ctxT, units, w_dt, w_a1, w_a2, ada1, ada2, params, consts, gconsts, outT):
    f32, f32r, i32 = mybir.dt.float32, mybir.dt.float32r, mybir.dt.int32
    ALU, ACT = mybir.AluOpType, mybir.ActivationFunctionType

    scratch = nc.dram_tensor("decay_rows", (2, HEADS, T), f32, kind="Internal").ap()

    ctx = ExitStack()
    with ctx:
        base = (nc.sbuf_base + 31) // 32 * 32
        end = nc.sbuf_usable_end // 32 * 32

        class Region:
            def __init__(self, start, size):
                self.at, self.end = start, start + size

            def take(self, name, shape, dt=f32):
                n = 4
                for s in shape[1:]:
                    n *= s
                t = nc.alloc_sbuf_tensor_at(name, shape, dt, offset=self.at)
                self.at += (n + 31) // 32 * 32
                assert self.at <= self.end, (name, self.at, self.end)
                return t

        def sem(name):
            return ctx.enter_context(nc.semaphore(name))

        keep = Region(base, 6784)
        par = keep.take("par", [P, NPAR])
        con = keep.take("con", [P, NCON])
        mod = keep.take("mod", [P, 112 + 16])
        g1s = keep.take("g1s", [P, 40])
        c_act = keep.take("c_act", [P, 24])
        glb = keep.take("glb", [P, 2, 12])
        gld = keep.take("gld", [P, 2, 12])
        tick = keep.take("tick", [P, 1])
        RW = keep.end
        rings = Region(RW, 40960)
        wraw = rings.take("wraw", [P, RAW, KT * P])
        whi = rings.take("whi", [P, SLOTS, KT * P], f32r)
        wlo = rings.take("wlo", [P, SLOTS, KT * P], f32r)
        RU = rings.end
        ureg = Region(RU, 32768)
        uhi = ureg.take("uhi", [P, KT, T], f32r)
        ulo = ureg.take("ulo", [P, KT, T], f32r)
        RV = ureg.end
        vreg = Region(RV, 65536)
        vhi = vreg.take("vhi", [P, 16, T], f32r)
        vlo = vreg.take("vlo", [P, 16, T], f32r)
        RM = vreg.end
        mreg = Region(RM, 16384)
        mg = mreg.take("mg", [P, KT, T])
        RT = mreg.end
        WORK = end - RT

        x0 = Region(RM, 16384).take("x0", [P, KT, T])
        slab = Region(RV, 65536).take("slab", [P, 8, KT, 256])
        NT = Region(end - 10240, 10240)
        nsq = NT.take("nsq", [P, 2, T])
        nrs = NT.take("nrs", [P, T])
        nt = NT.take("nt", [P, 2, T])
        dtr = Region(RV, 40960)
        dw = dtr.take("dw", [P, KT * P])
        dwh = dtr.take("dwh", [P, KT * P], f32r)
        dwl = dtr.take("dwl", [P, KT * P], f32r)
        dx, de, dd, dl, dr, dac, dea = [dtr.take(n, [P, T]) for n in ("dx", "de", "dd", "dl", "dr", "dac", "dea")]
        nega = dtr.take("nega", [P, 1])
        sr = Region(RT, WORK)
        pads = sr.take("pads", [P, 2, T + 3])
        bc = sr.take("bc", [P, 2, 2, T])
        xs = sr.take("xs", [P, 2, T])
        ys = sr.take("ys", [P, 2, 2, T])
        zs = sr.take("zs", [P, 2, T])
        es = sr.take("es", [P, NCH, 4, CH])
        eac = sr.take("eac", [P, 2, T])
        srs = sr.take("srs", [P, T])
        dtT = sr.take("dtT", [P, NCH, HEADS])
        acT = sr.take("acT", [P, NCH, HEADS])
        endT = sr.take("endT", [P, NCH, HEADS])
        decT = sr.take("decT", [P, NCH, HEADS])
        v14 = Region(RV + 14 * 2048, 4096)
        xdt = v14.take("xdt", [P, 2, 256])
        xend = v14.take("xend", [P, 2, 256])
        v14l = Region(RV + 32768 + 14 * 2048, 4096)
        bT = v14l.take("bT", [P, 2, CH])
        st = v14l.take("st", [P, 256])
        ty = v14l.take("ty", [P, 2, CH])
        cr = Region(RT, WORK)
        xr = cr.take("xr", [P, KT, T])
        aacc = cr.take("aacc", [P, 4096])
        aring = cr.take("aring", [P, 2, 512])
        CT = cr.at
        ccx = cr.take("ccx", [P, T + 2])
        ccs = cr.take("ccs", [P, T])
        ct = cr.take("ct", [P, T])
        cy = cr.take("cy", [P, T])
        sg = cr.take("sg", [P, T])
        mr = Region(CT, end - CT)
        r1 = mr.take("r1", [P, 2, T])
        hq = mr.take("hq", [P, T])

        gv = Region(RV, 65536)
        kf = gv.take("kf", [P, NGLA, TA])
        qf = gv.take("qf", [P, NGLA, T])
        rf = gv.take("rf", [P, KT, T])
        VT = gv.at
        vt = gv.take("vt", [P, TA // P, D])
        az = gv.take("az", [P, TA])
        wa = Region(VT, 12288)
        wa1 = wa.take("wa1", [P, KT * P])
        wa1h = wa.take("wa1h", [P, KT * P], f32r)
        wa1l = wa.take("wa1l", [P, KT * P], f32r)
        gu = Region(RM, 16384)
        uch = gu.take("uch", [P, KT, TC], f32r)
        ucl = gu.take("ucl", [P, KT, TC], f32r)
        gm = Region(RM, 16384)
        vh = gm.take("vh", [P, TA // P, GV])
        kdT = gm.take("kdT", [P, 2, TA // P, P])
        gst = gm.take("gst", [P, 2, GV])
        atts = gm.take("atts", [P, 2, P])
        gt = Region(RT + 16384, end - 10240 - RT - 16384)
        gcon = gt.take("gcon", [P, NGCON])
        wa2c = gt.take("wa2c", [P, P])
        GT = gt.at
        zz = gt.take("zz", [P, TA])
        ez = gt.take("ez", [P, TA])
        qd = gt.take("qd", [P, 2, T])
        ki = gt.take("ki", [P, 2, T])
        am = gt.take("am", [P, 2, P])
        gx = Region(GT, 8192)
        xc = gx.take("xc", [P, KT, TC])
        vf = Region(GT, 6144).take("vf", [P, 2, TA])

        psum = [ctx.enter_context(nc.psum_tensor(f"bank{i}", [P, T], f32)) for i in range(8)]
        ident = con[:, CCOL["ident"]:CCOL["ident"] + 128]
        ones = con[:, CCOL["ones"]:CCOL["ones"] + 128]
        last_row = con[:, CCOL["last_row"]:CCOL["last_row"] + 128]
        causal_add = con[:, CCOL["causal_add"]:CCOL["causal_add"] + 128]
        resets = con[:, CCOL["resets"]:CCOL["resets"] + 512]

        def pc(name, j=0):
            return par[:, PCOL[name] + j:PCOL[name] + j + 1]

        def pcd(name, j):
            return par[:, bass.ds(PCOL[name] + j, 1)]

        sgs = Region(RV + 8 * 2048, 16384).take("sgs", [P, KT, T])

        w_loaded = [sem(f"w_loaded{i}") for i in range(RAW)]
        w_hi = sem("w_hi")
        w_split = sem("w_split")
        unit_done = sem("unit_done")
        bank_free = [sem(f"bank_free{i}") for i in range(4)]
        in_ld = sem("in_ld"); slab_ld = [sem(f"slab_ld{i}") for i in range(8)]
        x_ld = sem("x_ld")

        def wait(eng, s, v):
            if isinstance(v, int) and v <= 0:
                return
            eng.wait_ge(s, v)

        def run(eng, steps, body, peel_last=False, peel_first=False):
            n = steps - (1 if peel_last else 0)
            if peel_first or n == 1:
                body(0)
            if n > 1:
                with eng.Fori(1 if peel_first else 0, n) as it:
                    body(it)
            if peel_last:
                body(steps - 1)

        def split_hi(act, ph, it, k):
            p = PH[ph]
            at = p["u0"] + k + AHEAD
            if isinstance(it, int) and at + it * p["n"] >= UNITS:
                return
            hi_part(act, at, it * (p["n"] // 4) if p["n"] % 4 == 0 else 0)

        def hi_part(act, at, quads):
            act.wait_ge(w_loaded[at % RAW], (quads * 2 + at // RAW + 1) * 16)
            wait(act, unit_done, quads * 4 + at - AHEAD)
            act.activation(whi[:, at % SLOTS, :], wraw[:, at % RAW, :], ACT.Copy).then_inc(w_hi, 1)

        def split_lo(dve, ph, it, k):
            p = PH[ph]
            at = p["u0"] + k + AHEAD
            if isinstance(it, int) and at + it * p["n"] >= UNITS:
                return
            lo_part(dve, at, it * (p["n"] // 4) if p["n"] % 4 == 0 else 0)

        def lo_part(dve, at, quads):
            dve.wait_ge(w_hi, quads * 4 + at + 1)
            dve.tensor_tensor(wlo[:, at % SLOTS, :], wraw[:, at % RAW, :],
                              whi[:, at % SLOTS, :].bitcast(f32), ALU.subtract).then_inc(w_split, 1)

        def wait_unit(eng, ph, it, k):
            p = PH[ph]
            eng.wait_ge(unit_done, it * p["n"] + p["u0"] + k + 1)

        def split_products(pe, out, hi, lo, rhs_hi, rhs_lo, first, last, tiles_ready=None):
            for k in range(KT):
                if tiles_ready is not None:
                    tiles_ready(k)
                wh, wl = hi[:, k * P:(k + 1) * P], lo[:, k * P:(k + 1) * P]
                pe.matmul(out, wh, rhs_hi(k), start=first and k == 0, stop=False)
                pe.matmul(out, wh, rhs_lo(k), start=False, stop=False)
                mm = pe.matmul(out, wl, rhs_hi(k), start=False, stop=last and k == KT - 1)
            return mm

        def pe_unit(pe, ph, it, k, rhs_hi, rhs_lo, out_i=None, first=True, last=True, tiles_ready=None):
            p = PH[ph]
            out_i = k if out_i is None else out_i
            b = p["banks"][out_i]
            pe.wait_ge(w_split, it * p["n"] + p["u0"] + k + 1)
            if first:
                wait(pe, bank_free[b], it * p["per"][b] + p["used"][b] + p["banks"][:out_i].count(b))
            s = (p["u0"] + k) % SLOTS
            mm = split_products(pe, psum[b][:], whi[:, s, :], wlo[:, s, :], rhs_hi, rhs_lo, first, last, tiles_ready)
            mm.then_inc(unit_done, 1)

        def bank(ph, i):
            return psum[PH[ph]["banks"][i]]

        def freed(ph, i):
            return bank_free[PH[ph]["banks"][i]]

        norm_sem = {s: sem(f"norm_{s}") for s in ("sq", "summed", "mean", "rs", "t", "hi", "u")}

        class Norm:
            def __init__(self, order, modulated, x, tok, gain, shift, hi, lo, bank):
                self.x, self.n, self.gain, self.shift, self.hi, self.lo, self.bank = x, tok, gain, shift, hi, lo, bank
                self.one, self.all, self.mods = order, order * KT, modulated * KT

            def ready(self, eng, tiles):
                eng.wait_ge(norm_sem["u"], self.all + tiles)

            def act(self, act, x_ready):
                n = self.n
                for j in range(KT):
                    x_ready(act, j)
                    wait(act, norm_sem["summed"], self.all + j - 1)
                    act.activation(nsq[:, j % 2, :n], self.x(j), ACT.Square).then_inc(norm_sem["sq"], 1)
                act.wait_ge(norm_sem["mean"], self.one + 1)
                act.activation(nrs[:, :n], nrs[:, :n], ACT.Ln)
                act.drain()
                act.activation(nrs[:, :n], nrs[:, :n], ACT.Exp, scale=-0.5).then_inc(norm_sem["rs"], 1)
                if self.hi is not None:
                    for j in range(KT):
                        act.wait_ge(norm_sem["t"], self.mods + j + 1)
                        act.activation(self.hi(j), nt[:, j % 2, :n], ACT.Identity,
                                       scale=self.gain(j), bias=self.shift(j)).then_inc(norm_sem["hi"], 1)

            def pe(self, pe):
                for j in range(KT):
                    pe.wait_ge(norm_sem["sq"], self.all + j + 1)
                    pe.matmul(self.bank[:, :self.n], ones, nsq[:, j % 2, :self.n], start=j == 0,
                              stop=j == KT - 1).then_inc(norm_sem["summed"], 1)

            def dve(self, dve):
                n = self.n
                dve.wait_ge(norm_sem["summed"], self.all + KT)
                dve.tensor_scalar(nrs[:, :n], self.bank[:, :n], 1.0 / D, EPS, ALU.mult, ALU.add
                                  ).then_inc(norm_sem["mean"], 1)
                dve.wait_ge(norm_sem["rs"], self.one + 1)
                if self.hi is None:
                    for j in range(KT):
                        dve.scalar_tensor_tensor(self.x(j), self.x(j), self.gain(j), nrs[:, :n],
                                                 ALU.mult, ALU.mult).then_inc(norm_sem["u"], 1)
                    dve.drain()
                    return

                def scaled(j):
                    dve.tensor_tensor(nt[:, j % 2, :n], self.x(j), nrs[:, :n], ALU.mult).then_inc(norm_sem["t"], 1)
                    dve.drain()
                    dve.tensor_scalar(nsq[:, j % 2, :n], nt[:, j % 2, :n], self.gain(j), self.shift(j),
                                      ALU.mult, ALU.add)
                    dve.drain()

                scaled(0)
                for j in range(KT):
                    if j >= 1:
                        dve.wait_ge(norm_sem["hi"], self.mods + j)
                    if j + 1 < KT:
                        scaled(j + 1)
                    dve.wait_ge(norm_sem["hi"], self.mods + j + 1)
                    dve.tensor_tensor(self.lo(j), nsq[:, j % 2, :n], self.hi(j).bitcast(f32),
                                      ALU.subtract).then_inc(norm_sem["u"], 1)
                    dve.drain()

        def u_h(k):
            return uhi[:, k, :]

        def u_l(k):
            return ulo[:, k, :]

        norm_a = Norm(0, 0, lambda j: x0[:, j, :], T, lambda j: g1s[:, j:j + 1], lambda j: mod[:, j:j + 1],
                      u_h, u_l, psum[6])

        S = {n: sem(n) for n in ("cact", "mod_ps", "mod_rdy", "dw_ld", "dw_hi", "dw_lo", "dt_ps", "dt_e", "dt_w", "dt_ln", "dt_ac", "dt_ea", "scr_st", "dt_tp", "dt_tok", "dt_last", "dt_lastd", "dt_done", "dt_nega", "pad0", "cv_a", "cv_d", "cv_s", "y_skip", "z_s", "e_ld0", "e_ld1", "e_ld2", "e_ld3", "e_seg", "e_exp", "eac_ld", "pe_a", "dt_dec", "m_rdy", "pe_b", "b_dve", "f_y", "f_sq", "f_pe", "f_ms", "f_rs", "f_n", "f_hi", "f_fin")}

        def pe_a(pe, g, par_, c):
            pe.wait_ge(S["cv_s"], 4 * g + 4)
            if c == 0:
                wait(pe, S["b_dve"], 4 * g)
            b = psum[4 + c % 2]
            wait(pe, S["m_rdy"], 4 * g + c - 1)
            s = slice(c * CH, (c + 1) * CH)
            pe.matmul(b[:, 384:512], bc[:, par_, 0, s], bc[:, par_, 1, s], start=True, stop=True)
            for q in range(2):
                pe.transpose(b[:, q * 128:(q + 1) * 128], xs[:, q, s], ident)
            pe.transpose(b[:, 256:384], bc[:, par_, 0, s], ident).then_inc(S["pe_a"], 1)

        def pe_b(pe, g, par_, c):
            pe.wait_ge(S["m_rdy"], 4 * g + c + 1)
            wait(pe, S["b_dve"], 4 * g + c)
            if c == 0:
                wait(pe, S["f_ms"], g)
            s = slice(c * CH, (c + 1) * CH)
            for h in range(4):
                mm = pe.matmul(psum[6][(h % 2) * 64:(h % 2) * 64 + 64, (h // 2) * CH:(h // 2 + 1) * CH],
                               xdt[:, c % 2, h * 64:(h + 1) * 64], es[:, c, h, :], start=True, stop=True)
            if c > 0:
                for q in range(2):
                    mm = pe.matmul(psum[6][:, 256 + q * CH:256 + (q + 1) * CH], st[:, q * 128:(q + 1) * 128],
                                   bc[:, par_, 1, s], start=True, stop=True)
            if c < NCH - 1:
                mm = pe.matmul(psum[7][:, 0:256], bT[:, c % 2, :], xend[:, c % 2, :], start=True, stop=True)
            mm.then_inc(S["pe_b"], 1)

        def pe_n(pe, g):
            pe.wait_ge(S["f_sq"], g + 1)
            wait(pe, S["b_dve"], 4 * g + 4)
            for q in range(2):
                mm = pe.matmul(psum[6][:], ones, zs[:, q, :], start=q == 0, stop=q == 1)
            mm.then_inc(S["f_pe"], 1)

        def pe_slot(pe, k, g, par_, prev):
            if prev and k == 0:
                pe_a(pe, g - 1, 1 - par_, 2)
                pe_b(pe, g - 1, 1 - par_, 1)
            if prev and k == 1:
                pe_a(pe, g - 1, 1 - par_, 3)
                pe_b(pe, g - 1, 1 - par_, 2)
            if prev and k == 2:
                pe_b(pe, g - 1, 1 - par_, 3)
            if prev and k == 4:
                pe_n(pe, g - 1)
            if g is not None and not isinstance(g, str):
                if k == 4 and not tail(g):
                    pe_a(pe, g, par_, 0)
                if k == 5 and not tail(g):
                    pe_a(pe, g, par_, 1)
                    pe_b(pe, g, par_, 0)

        def tail(g):
            return isinstance(g, int) and g == SSM_GROUPS

        def act_conv(act, g, par_, k, it, ph, ku):
            wait_unit(act, ph, it, ku)
            dst = conv_dst(par_, k)
            if k >= 2:
                wait(act, S["pe_a"], 4 * g)
                wait(act, S["y_skip"], g)
            wait(act, S["cv_d"], 4 * g + k - 1)
            ps = bank(ph, ku)
            act.activation(dst, ps[:], ACT.Identity, scale=pcd("ssm_w", 96 + 4 * g + k),
                           bias=pcd("ssm_b", 4 * g + k))
            act.activation(pads[:, k % 2, 3:], ps[:], ACT.Copy).then_inc(S["cv_a"], 1)
            act.drain().then_inc(freed(ph, ku), 1)

        def conv_dst(par_, k):
            return bc[:, par_, k, :] if k < 2 else xs[:, k - 2, :]

        def act_silu(act, g, par_, k):
            act.wait_ge(S["cv_d"], 4 * g + k + 1)
            act.activation(conv_dst(par_, k), conv_dst(par_, k), ACT.Silu).then_inc(S["cv_s"], 1)

        def act_slot(act, k, g, par_, prev, it, ph, ku, here):
            if 1 <= k <= 3 and here:
                act_silu(act, g, par_, k - 1)
            if k == 4:
                if here:
                    act_silu(act, g, par_, 3)
                if prev:
                    act.wait_ge(S["f_y"], g)
                    act.activation(zs[:], ys[:, 1 - par_, :, :], ACT.Square).then_inc(S["f_sq"], 1)
            if k == 5:
                if prev:
                    act.wait_ge(S["f_ms"], g)
                    act.activation(srs[:], srs[:], ACT.Ln)
                    act.drain()
                    act.activation(srs[:], srs[:], ACT.Exp, scale=-0.5).then_inc(S["f_rs"], 1)
                    act.wait_ge(S["f_n"], g)
                    act.activation(vhi[:, bass.ds(2 * g - 2, 2), :], ys[:, 1 - par_, :, :],
                                   ACT.Copy).then_inc(S["f_hi"], 1)
            if here:
                if k < 4:
                    act_conv(act, g, par_, k, it, ph, ku)
                else:
                    wait_unit(act, ph, it, ku)
                    wait(act, S["f_pe"], g)
                    act.activation(zs[:, k - 4, :], bank(ph, ku)[:], ACT.Silu).then_inc(S["z_s"], 1)
                    act.drain().then_inc(freed(ph, ku), 1)
                    if k == 4:
                        act.wait_ge(S["e_seg"], 4 * g + 4)
                        act.activation(es[:], es[:], ACT.Exp).then_inc(S["e_exp"], 1)

        def dve_taps(dve, g, par_, k):
            dve.wait_ge(S["cv_a"], 4 * g + k + 1)
            dst = conv_dst(par_, k)
            for tap in range(3):
                last = dve.scalar_tensor_tensor(dst, pads[:, k % 2, tap:tap + T], pcd("ssm_w", 32 * tap + 4 * g + k),
                                                dst, ALU.mult, ALU.add)
                if tap < 2:
                    dve.drain()
            last.then_inc(S["cv_d"], 1)

        def per_head(t, c, g):
            return t[:, c, bass.ds(4 * g, 4)].unsqueeze(2).to_broadcast([P, 4, 64])

        def dve_a(dve, g, c):
            dve.wait_ge(S["pe_a"], 4 * g + c + 1)
            wait(dve, S["pe_b"], 4 * g + c - 1)
            b = psum[4 + c % 2]
            x4 = b[:, 0:256].rearrange("p (h f) -> p h f", h=4)
            dve.tensor_tensor(xdt[:, c % 2, :].rearrange("p (h f) -> p h f", h=4), x4, per_head(dtT, c, g), ALU.mult)
            if c < NCH - 1:
                dve.tensor_tensor(xend[:, c % 2, :].rearrange("p (h f) -> p h f", h=4), x4, per_head(endT, c, g),
                                  ALU.mult)
                dve.tensor_copy(bT[:, c % 2, :], b[:, 256:384])
            dve.wait_ge(S["e_exp"], g + 1)
            dve.tensor_tensor(es[:, c, :, :], es[:, c, :, :],
                              b[:, 384:512].unsqueeze(1).to_broadcast([P, 4, CH]), ALU.mult)
            dve.drain().then_inc(S["m_rdy"], 1)

        def dve_b(dve, g, par_, c):
            dve.wait_ge(S["pe_b"], 4 * g + c + 1)
            s = slice(c * CH, (c + 1) * CH)
            y = ys[:, par_, :, s]
            if c > 0:
                dve.wait_ge(S["eac_ld"], 64 * g + 64)
                dve.tensor_tensor(ty[:], psum[6][:, 256:512].rearrange("p (q t) -> p q t", q=2), eac[:, :, s], ALU.mult)
                dve.drain()
                dve.tensor_tensor(y, y, ty[:], ALU.add)
                dve.drain()
            dve.tensor_tensor(y, y, psum[6][:, 0:256].rearrange("p (q t) -> p q t", q=2), ALU.add)
            if c == 0:
                dve.tensor_copy(st[:], psum[7][:, 0:256])
            elif c < NCH - 1:
                s4 = st[:].rearrange("p (h f) -> p h f", h=4)
                dve.tensor_tensor(s4, s4, per_head(decT, c, g), ALU.mult)
                dve.drain()
                dve.tensor_tensor(st[:], st[:], psum[7][:, 0:256], ALU.add)
            dve.drain().then_inc(S["b_dve"], 1)

        def dve_slot(dve, k, g, par_, prev, here):
            if prev:
                q = 1 - par_
                if k == 0:
                    dve_a(dve, g - 1, 1)
                    dve_b(dve, g - 1, q, 0)
                if k == 1:
                    dve_a(dve, g - 1, 2)
                    dve_b(dve, g - 1, q, 1)
                if k == 2:
                    dve_a(dve, g - 1, 3)
                    dve_b(dve, g - 1, q, 2)
                if k == 3:
                    dve_b(dve, g - 1, q, 3)
                    dve.wait_ge(S["z_s"], 2 * g)
                    dve.tensor_tensor(ys[:, q, :, :], ys[:, q, :, :], zs[:], ALU.mult).then_inc(S["f_y"], 1)
            if here and k < 4:
                dve_taps(dve, g, par_, k)
            if k == 5:
                if prev:
                    q_ = 1 - par_
                    dve.wait_ge(S["f_pe"], g)
                    dve.tensor_scalar(srs[:], psum[6][:], 1.0 / 256, EPS, ALU.mult, ALU.add).then_inc(S["f_ms"], 1)
                    dve.wait_ge(S["f_rs"], g)
                    for q in range(2):
                        dve.scalar_tensor_tensor(ys[:, q_, q, :], ys[:, q_, q, :], pcd("ssm_norm", 2 * g - 2 + q),
                                                 srs[:], ALU.mult, ALU.mult)
                    dve.drain().then_inc(S["f_n"], 1)
                if here:
                    dve.wait_ge(S["cv_s"], 4 * g + 4)
                    wait(dve, S["f_hi"], g - 1)
                    for q in range(2):
                        last = dve.tensor_scalar(ys[:, par_, q, :], xs[:, q, :], pcd("d_skip", 2 * g + q), None, ALU.mult)
                    last.then_inc(S["y_skip"], 1)
                    dve.drain()
                    dve_a(dve, g, 0)
                if prev:
                    at = bass.ds(2 * g - 2, 2)
                    dve.wait_ge(S["f_hi"], g)
                    dve.tensor_tensor(vlo[:, at, :], ys[:, q_, :, :], vhi[:, at, :].bitcast(f32),
                                      ALU.subtract).then_inc(S["f_fin"], 1)
                    dve.drain()

        def pool_group(pool, g):
            first = isinstance(g, int) and g == 0
            for c in range(NCH):
                wait(pool, S["pe_b"], 4 * g - 4 + c + 1)
                pool.dma_start(es[:, c, :, :],
                               scratch[0, bass.ds(4 * g, 4), c * CH:(c + 1) * CH].partition_broadcast(P)
                               ).then_inc(S[f"e_ld{c}"], 16)
            wait(pool, S["b_dve"], 4 * g)
            for hh in range(2):
                for q in range(2):
                    pool.dma_start(eac[64 * hh:64 * hh + 64, q, :],
                                   scratch[1, bass.ds(4 * g + 2 * q + hh, 1), :].rearrange("a t -> (a t)").partition_broadcast(64)
                                   ).then_inc(S["eac_ld"], 16)
            for c in range(NCH):
                pool.wait_ge(S[f"e_ld{c}"], 16 * g + 16)
                pool.tensor_tensor(es[:, c, :, :], es[:, c, :, :],
                                   causal_add.unsqueeze(1).to_broadcast([P, 4, CH]), ALU.add)
                pool.drain()
                pool.tensor_tensor(es[:, c, :, :], es[:, c, :, :],
                                   acT[:, c, bass.ds(4 * g, 4)].unsqueeze(2).to_broadcast([P, 4, CH]),
                                   ALU.subtract).then_inc(S["e_seg"], 1)

        norm_b = Norm(1, 1, lambda j: xr[:, j, :], T, lambda j: g1s[:, 8 + j:9 + j], lambda j: mod[:, 24 + j:25 + j],
                      u_h, u_l, psum[6])
        norm_f1 = Norm(2, 2, lambda j: xr[:, j, :], T, lambda j: pc("final_norm", j), None, None, None, psum[6])

        N2 = {n: sem(n) for n in ("x2_ld", "cc_a", "cc_x", "cc_y", "cc_h", "cc_l", "cg_a", "co_d", "mh", "ml", "wo_d", "ada_ld0", "ada_ld1", "ada_done", "ada_read", "ada_mod", "r_a", "r_q", "r_h", "r_l", "dn_d", "out_st")}

        norm_g = Norm(3, 2, lambda j: xr[:, j, :], T, lambda j: g1s[:, 24 + j:25 + j], lambda j: mod[:, 48 + j:49 + j],
                      u_h, u_l, psum[6])
        norm_c = Norm(4, 3, lambda j: xc[:, j, :], TC, lambda j: g1s[:, 16 + j:17 + j], lambda j: mod[:, 96 + j:97 + j],
                      lambda j: uch[:, j, :], lambda j: ucl[:, j, :], psum[7])
        norm_m = Norm(5, 4, lambda j: xr[:, j, :], T, lambda j: g1s[:, 32 + j:33 + j], lambda j: mod[:, 72 + j:73 + j],
                      u_h, u_l, psum[6])
        norm_f2 = Norm(6, 5, lambda j: xr[:, j, :], T, lambda j: pc("final_2", j), None, None, None, psum[6])
        G = {n: sem(n) for n in ("xc_ld", "gcon_ld", "wa1_ld", "wa1_h", "wa1_l", "az_d", "az_a", "g_k", "v_a", "v_t", "v_d", "wa2_ld", "z_d", "vh_r", "za", "zl", "zb", "ex", "kd", "ktp", "ktc", "att_p", "att_d", "o_p", "st_p", "st_d", "o_sq", "o_sum", "o_ms", "o_rs", "o_n", "o_hi", "o_lo", "am0", "go_d")}
        mask = [gcon[:, GCOL[f"mask_{x}"]:GCOL[f"mask_{x}"] + P].bitcast(i32) for x in "fb"]
        reset = [gcon[:, GCOL[f"reset_{x}"]:GCOL[f"reset_{x}"] + TA] for x in "fb"]
        ZB = [(4, 5), (2, 3)]

        def v_h(k):
            return vhi[:, k, :]

        def v_l(k):
            return vlo[:, k, :]

        def ada_round(pool, n, src, col0, ccol, steps, acc0):
            def step(it):
                def load(k):
                    pool.dma_start(aring[:, k % 2, :], src[k * P:(k + 1) * P, bass.ds(it * 512 + col0, 512)]
                                   ).then_inc(N2[f"ada_ld{k % 2}"], 16)
                load(0)
                load(1)
                acc = aacc[:, bass.ds(it * 512 + acc0, 512)]
                for k in range(KT):
                    pool.wait_ge(N2[f"ada_ld{k % 2}"], it * 64 + (n * 4 + k // 2 + 1) * 16)
                    w = aring[:, k % 2, :]
                    pool.tensor_tensor(w, w, c_act[:, ccol + k:ccol + k + 1].to_broadcast([P, 512]), ALU.mult)
                    pool.drain()
                    if k == 0:
                        pool.tensor_copy(acc, w)
                    else:
                        pool.tensor_tensor(acc, acc, w, ALU.add)
                    pool.drain()
                    if k + 2 < KT:
                        load(k + 2)
            with pool.Fori(0, steps) as it:
                step(it)

        def ada_pe(pe, n):
            pe.wait_ge(N2["ada_done"], n)
            wait(pe, N2["ada_mod"], n - 1)
            for j in range(32):
                mm = pe.matmul(psum[7][:, 256 + j:257 + j], aacc[:, j * P:(j + 1) * P], ones[:, 0:1], start=True, stop=True)
            mm.then_inc(N2["ada_read"], 1)

        def ada_dve(dve, n, parts):
            dve.wait_ge(N2["ada_read"], n)
            for dst, src, count, bias in parts:
                dve.tensor_tensor(mod[:, dst:dst + count], psum[7][:, 256 + src:256 + src + count],
                                  par[:, bias:bias + count], ALU.add)
            dve.drain().then_inc(N2["ada_mod"], 1)

        def mlp_up_act(act, ph, done):
            def step(it):
                for k in range(4):
                    split_hi(act, ph, it, k)
                    wait_unit(act, ph, it, k)
                    wait(act, N2["r_q"], it * 4 + done + k - 1)
                    act.activation(r1[:, k % 2, :], bank(ph, k)[:], ACT.Relu).then_inc(N2["r_a"], 1)
                    act.drain().then_inc(freed(ph, k), 1)
                    act.activation(vhi[:, bass.ds(it * 4 + k, 1), :].rearrange("p a t -> p (a t)"), r1[:, k % 2, :],
                                   ACT.Square).then_inc(N2["r_h"], 1)
            run(act, 4, step, peel_first=done == 0)

        def mlp_up_dve(dve, ph, done):
            def step(it):
                for k in range(4):
                    split_lo(dve, ph, it, k)
                    dve.wait_ge(N2["r_a"], it * 4 + done + k + 1)
                    dve.tensor_tensor(hq[:], r1[:, k % 2, :], r1[:, k % 2, :], ALU.mult).then_inc(N2["r_q"], 1)
                    dve.drain()
                    dve.wait_ge(N2["r_h"], it * 4 + done + k + 1)
                    at = bass.ds(it * 4 + k, 1)
                    dve.tensor_tensor(vlo[:, at, :].rearrange("p a t -> p (a t)"), hq[:],
                                      vhi[:, at, :].rearrange("p a t -> p (a t)").bitcast(f32),
                                      ALU.subtract).then_inc(N2["r_l"], 1)
                    dve.drain()
            run(dve, 4, step)

        def mlp_down_pe(pe, ph, done, peel_last=False):
            def step(it):
                for k in range(4):
                    half = k % 2
                    pe.wait_ge(N2["r_l"], done + 8 + 8 * half)
                    pe_unit(pe, ph, it, k, lambda t: v_h(t + 8 * half), lambda t: v_l(t + 8 * half), out_i=k // 2,
                            first=half == 0, last=half == 1)
            run(pe, 4, step, peel_last)

        def mlp_down_dve(dve, ph, half_b, gate, peel_last=False):
            def step(it):
                for k in range(4):
                    split_lo(dve, ph, it, k)
                    if k % 2 == 0:
                        continue
                    o = k // 2
                    at = bass.ds(it * 2 + o, 1)
                    m = mg[:, at, :].rearrange("p a t -> p (a t)")
                    wait_unit(dve, ph, it, k)
                    if not half_b:
                        dve.tensor_copy(m, bank(ph, o)[:])
                        dve.drain().then_inc(freed(ph, o), 1)
                    else:
                        x = xr[:, at, :].rearrange("p a t -> p (a t)")
                        dve.tensor_tensor(m, m, bank(ph, o)[:], ALU.add)
                        dve.drain().then_inc(freed(ph, o), 1)
                        dve.scalar_tensor_tensor(x, m, mod[:, bass.ds(it * 2 + gate + o, 1)], x, ALU.mult, ALU.add)
                        dve.drain().then_inc(N2["dn_d"], 1)
            run(dve, 4, step, peel_last)

        def only_hi(act, ph, peel_last=False):
            p = PH[ph]

            def step(it):
                for k in range(p["n"]):
                    split_hi(act, ph, it, k)
            run(act, p["steps"], step, peel_last)

        def chunk_of(d, i):
            if d == 0:
                return i
            return 3 - i if i < 4 else 15 - i

        def gla_pe(pe, h):
            for d in range(2):
                b4, b5 = psum[ZB[d][0]], psum[ZB[d][1]]
                pe.wait_ge(G["wa2_ld"], h * 32 + 32)
                if d == 0:
                    wait(pe, G["st_d"], h * 22)
                else:
                    wait(pe, G["ktc"], h * 2)
                w, a = wa2c[32 * d:32 * d + 16, :], az[32 * d:32 * d + 16, :]
                pe.matmul(b4[:], w, a[:, TC:], start=True, stop=True)
                pe.matmul(b5[:, :TC], w, a[:, :TC], start=True, stop=True).then_inc(G["z_d"], 1)
            for d in range(2):
                b4, b5 = psum[ZB[d][0]], psum[ZB[d][1]]
                pe.wait_ge(G["kd"], h * 2 + d + 1)
                for i in range(TA // P):
                    b = b4 if i < 4 else b5
                    mm = pe.transpose(b[:, (i % 4) * P:(i % 4 + 1) * P], ez[:, i * P:(i + 1) * P], ident)
                mm.then_inc(G["ktp"], 1)
            def att(p):
                s = slice(p * P, (p + 1) * P)
                wait(pe, G["att_d"], h * 4 + p - 1)
                for d in range(2):
                    mm = pe.matmul(psum[p % 2][:, d * P:(d + 1) * P], ki[:, d, s], qd[:, d, s], start=True, stop=True)
                mm.then_inc(G["att_p"], 1)
            if not (isinstance(h, int) and h == 0):
                pe.wait_ge(G["o_n"], h)
            pe.wait_ge(G["zl"], h * 2 + 2)
            att(0)
            for p in range(4):
                if p < 3:
                    att(p + 1)
                pe.wait_ge(G["att_d"], h * 4 + p + 1)
                pe.wait_ge(G["vh_r"], h + 1)
                s = slice(p * P, (p + 1) * P)
                for v in range(2):
                    mm = pe.matmul(psum[6 + v][:, s], vh[:, 2 + p, v * P:(v + 1) * P], atts[:, p % 2, :], start=p == 0,
                                   stop=False, skip_group_check=True)
                mm.then_inc(G["o_p"], 1)
            for i in range(12):
                for d in range(2):
                    c = chunk_of(d, i)
                    wait(pe, G["st_d"], h * 22 + 2 * i + d - 1 if i else (h * 22 if d == 0 else h * 22))
                    if i == 0:
                        pe.wait_ge(G["ktc"], h * 2 + 2)
                    if i >= 4:
                        t = slice((c - 4) * GC, (c - 3) * GC)
                        for v in range(2):
                            mm = pe.matmul(psum[6 + v][:, t], gst[:, d, v * P:(v + 1) * P], qd[:, d, t], start=False,
                                           stop=i == 11 and d == 1, skip_group_check=True)
                    if i < 11:
                        r = slice((c % 2) * GC, (c % 2 + 1) * GC)
                        mm = pe.matmul(psum[4 + d][:, 0:GV], kdT[r, d, c // 2, :], vh[r, c // 2, :], start=True, stop=True)
                    mm.then_inc(G["st_p"], 1)
            pe.wait_ge(G["o_sq"], h + 1)
            for v in range(2):
                mm = pe.matmul(psum[0][:], ones, nsq[:, v, :], start=v == 0, stop=v == 1)
            mm.then_inc(G["o_sum"], 1)

        def gla_act(act, h):
            wait(act, G["st_p"], h * 24)
            act.activation(vh[:], vt[:, :, bass.ds(h * GV, GV)], ACT.Copy).then_inc(G["vh_r"], 1)
            for d in range(2):
                b4, b5 = psum[ZB[d][0]], psum[ZB[d][1]]
                act.wait_ge(G["z_d"], h * 2 + d + 1)
                bias = par[:, bass.ds(h + PCOL["b_a"] + 4 * d, 1)]
                wait(act, G["ktp"], h * 2 + d)
                act.activation(zz[:, TC:], b4[:], ACT.Identity, bias=bias)
                act.activation(zz[:, :TC], b5[:, :TC], ACT.Identity, bias=bias)
                act.drain()
                act.activation(ez[:], zz[:], ACT.Abs)
                act.drain()
                act.activation(ez[:], ez[:], ACT.Exp, scale=-1.0)
                act.drain()
                act.activation(ez[:], ez[:], ACT.Ln, bias=1.0).then_inc(G["za"], 1)
                act.wait_ge(G["zb"], h * 2 + d + 1)
                act.activation(gld[:, d, :], glb[:, d, :], ACT.Exp, scale=1.0 / TAU)
                act.activation(qd[:, d, :], zz[:, TC:], ACT.Exp, scale=1.0 / TAU)
                act.activation(ki[:, d, :], zz[:, TC:], ACT.Exp, scale=-1.0 / TAU)
                act.activation(ez[:], ez[:], ACT.Exp, scale=-1.0 / TAU)
                act.drain().then_inc(G["ex"], 1)
                act.wait_ge(G["ktp"], h * 2 + d + 1)
                act.activation(kdT[:, d, 0:4, :], b4[:].rearrange("p (i k) -> p i k", i=4), ACT.Copy)
                act.activation(kdT[:, d, 4:6, :], b5[:, :TC].rearrange("p (i k) -> p i k", i=2), ACT.Copy)
                act.drain().then_inc(G["ktc"], 1)
            act.wait_ge(G["st_p"], h * 24 + 24)
            for v in range(2):
                act.activation(nsq[:, v, :], psum[6 + v][:], ACT.Square)
            act.drain().then_inc(G["o_sq"], 1)
            act.wait_ge(G["o_ms"], h + 1)
            act.activation(nrs[:], nrs[:], ACT.Ln)
            act.drain()
            act.activation(nrs[:], nrs[:], ACT.Exp, scale=-0.5).then_inc(G["o_rs"], 1)
            act.wait_ge(G["o_n"], h + 1)
            act.activation(uhi[:, bass.ds(h * 2, 2), :], nt[:], ACT.Copy).then_inc(G["o_hi"], 1)

        def gla_dve(dve, h):
            for d in range(2):
                dve.wait_ge(G["za"], h * 2 + d + 1)
                wait(dve, G["st_p"], h * 24)
                dve.scalar_tensor_tensor(ez[:], zz[:], 0.0, ez[:], ALU.min, ALU.subtract)
                dve.drain()
                way = 1 if d == 0 else -1
                dve.tensor_tensor_scan(zz[:, ::way], reset[d][:, ::way], ez[:, ::way], 0.0, ALU.mult, ALU.add)
                dve.drain()
                z3 = zz[:].rearrange("p (c t) -> p c t", t=GC)
                edge = GC - 1 if d == 0 else 0
                dve.tensor_copy(glb[:, d, :], z3[:, :, edge])
                dve.tensor_tensor(ez[:].rearrange("p (c t) -> p c t", t=GC), z3,
                                  z3[:, :, edge:edge + 1].to_broadcast([P, 12, GC]), ALU.subtract)
                dve.drain().then_inc(G["zb"], 1)
                dve.wait_ge(G["ex"], h * 2 + d + 1)
                k1 = kf[:, bass.ds(h, 1), :].rearrange("p a t -> p (a t)")
                dve.tensor_tensor(ez[:], ez[:], k1, ALU.mult)
                dve.drain().then_inc(G["kd"], 1)
                dve.tensor_tensor(qd[:, d, :], qd[:, d, :], qf[:, bass.ds(h, 1), :].rearrange("p a t -> p (a t)"), ALU.mult)
                dve.tensor_tensor(ki[:, d, :], ki[:, d, :], k1[:, TC:], ALU.mult)
                dve.drain().then_inc(G["zl"], 1)
            for p in range(4):
                dve.wait_ge(G["att_p"], h * 4 + p + 1)
                wait(dve, G["o_p"], h * 4 + p - 1)
                dve.tensor_copy(tick[:], con[:, 0:1])
                for d in range(2):
                    dve.copy_predicated(am[:, d, :], mask[d], psum[p % 2][:, d * P:(d + 1) * P])
                dve.drain()
                dve.tensor_tensor(atts[:, p % 2, :], am[:, 0, :], am[:, 1, :], ALU.add)
                dve.drain().then_inc(G["att_d"], 1)
            for i in range(11):
                for d in range(2):
                    c = chunk_of(d, i)
                    dve.wait_ge(G["st_p"], h * 24 + 2 * i + d + 1)
                    if i == 0:
                        dve.tensor_copy(gst[:, d, :], psum[4 + d][:, 0:GV])
                    else:
                        dve.scalar_tensor_tensor(gst[:, d, :], gst[:, d, :], gld[:, d, c:c + 1], psum[4 + d][:, 0:GV],
                                                 ALU.mult, ALU.add)
                    dve.drain().then_inc(G["st_d"], 1)
            dve.wait_ge(G["o_sum"], h + 1)
            dve.tensor_scalar(nrs[:], psum[0][:], 1.0 / GV, EPS, ALU.mult, ALU.add).then_inc(G["o_ms"], 1)
            dve.wait_ge(G["o_rs"], h + 1)
            for v in range(2):
                dve.scalar_tensor_tensor(nt[:, v, :], psum[6 + v][:], pcd("g_head", h * 2 + v), nrs[:], ALU.mult, ALU.mult)
            dve.drain()
            at = bass.ds(h * 2, 2)
            dve.tensor_tensor(nt[:], nt[:], rf[:, at, :], ALU.mult)
            dve.drain().then_inc(G["o_n"], 1)
            dve.wait_ge(G["o_hi"], h + 1)
            dve.tensor_tensor(ulo[:, at, :], nt[:], uhi[:, at, :].bitcast(f32), ALU.subtract)
            dve.drain().then_inc(G["o_lo"], 1)

        def both(pe, ph, k):
            p = PH[ph]
            b, s = p["banks"][k], (p["u0"] + k) % SLOTS
            pe.wait_ge(w_split, p["u0"] + k + 1)
            pe.wait_ge(bank_free[b], p["used"][b] + p["banks"][:k].count(b))
            split_products(pe, psum[b][:], whi[:, s, :], wlo[:, s, :], u_h, u_l, True, True)
            split_products(pe, psum[4 + k % 2][:, :TC], whi[:, s, :], wlo[:, s, :], lambda t: uch[:, t, :],
                           lambda t: ucl[:, t, :], True, True).then_inc(unit_done, 1)

        block = ctx.enter_context(nc.Block())

        @block.sync
        def _(sp):
            sp.dma_start(par[:], params).then_inc(in_ld, 16)
            sp.dma_start(con[:], consts).then_inc(in_ld, 16)
            for j in range(2):
                sp.dma_start(x0[:, 4 * j:4 * j + 4, :],
                             xT[512 * j:512 * j + 512, :].rearrange("(k p) t -> p k t", p=P)).then_inc(x_ld, 16)
            for j in range(8):
                sp.dma_start(slab[:, j, :, :],
                             ada1[:, 256 * j:256 * j + 256].rearrange("(k p) n -> p k n", p=P)).then_inc(slab_ld[j], 16)
            for s in range(RAW):
                sp.dma_start(wraw[:, s, :], units[s]).then_inc(w_loaded[s], 16)
            sp.wait_ge(S["mod_ps"], 1)
            sp.dma_start(dw[:], w_dt).then_inc(S["dw_ld"], 16)
            with sp.Fori(1, UNITS // RAW) as i:
                for s in range(RAW):
                    sp.wait_ge(w_split, i * RAW + s - RAW + 1)
                    sp.dma_start(wraw[:, s, :], units[bass.ds(i * RAW + s, 1)].rearrange("a p n -> (a p) n")
                                 ).then_inc(w_loaded[s], 16)
            for j in range(2):
                norm_f2.ready(sp, 4 * j + 4)
                sp.dma_start(outT[512 * j:512 * j + 512, :].rearrange("(k p) t -> p k t", p=P),
                             xr[:, 4 * j:4 * j + 4, :]).then_inc(N2["out_st"], 16)
            sp.wait_ge(N2["out_st"], 32)

        @block.gpsimd
        def _(pool):
            pool.memset(pads[:, :, 0:3], 0.0).then_inc(S["pad0"], 1)
            pool.wait_ge(S["scr_st"], 32)
            pool.wait_ge(S["dt_done"], 1)
            pool_group(pool, 0)
            with pool.Fori(1, SSM_GROUPS) as g:
                pool_group(pool, g)
            pool.wait_ge(S["f_fin"], SSM_GROUPS)
            ada_round(pool, 0, ada1, 2048, 0, 8, 0)
            pool.drain().then_inc(N2["ada_done"], 1)
            pool.wait_ge(N2["ada_read"], 1)
            ada_round(pool, 8, ada2, 0, 8, 4, 0)
            ada_round(pool, 12, ada2, 0, 16, 4, 2048)
            pool.drain().then_inc(N2["ada_done"], 1)
            pool.wait_ge(N2["ada_read"], 2)
            ada_round(pool, 16, ada2, 2048, 8, 8, 0)
            pool.drain().then_inc(N2["ada_done"], 1)
            pool.wait_ge(N2["ada_read"], 3)
            pool.wait_ge(G["az_a"], 1)
            pool.memset(am[:], 0.0).then_inc(G["am0"], 1)

            def gates(h):
                wait(pool, G["z_d"], h * 2)
                for d in range(2):
                    pool.dma_start(wa2c[32 * d:32 * d + 16, :], w_a2[d, :, bass.ds(h * P, P)]).then_inc(G["wa2_ld"], 16)
            run(pool, NGLA, gates, peel_first=True)

        @block.scalar
        def _(act):
            act.wait_ge(in_ld, 32)
            act.activation(c_act[:], par[:, PCOL["c"]:PCOL["c"] + 24], ACT.Silu).then_inc(S["cact"], 1)
            for u in range(AHEAD - 1):
                hi_part(act, u, 0)
            norm_a.act(act, lambda e, j: e.wait_ge(x_ld, 32) if j == 0 else None)
            act.wait_ge(S["dw_ld"], 16)
            act.activation(dwh[:], dw[:], ACT.Copy).then_inc(S["dw_hi"], 1)
            act.activation(nega[:], pc("a_log"), ACT.Exp).then_inc(S["dt_nega"], 1)
            hi_part(act, AHEAD - 1, 0)
            act.wait_ge(S["dt_ps"], 1)
            act.activation(dx[:], psum[4][:], ACT.Identity, bias=pc("dt_bias"))
            act.drain()
            act.activation(de[:], dx[:], ACT.Abs)
            act.drain()
            act.activation(de[:], de[:], ACT.Exp, scale=-1.0).then_inc(S["dt_e"], 1)
            act.wait_ge(S["dt_w"], 1)
            act.activation(dl[:], dd[:], ACT.Ln).then_inc(S["dt_ln"], 1)
            act.wait_ge(S["dt_ac"], 1)
            act.dma_start(scratch[0], dac[0:HEADS, :]).then_inc(S["scr_st"], 16)
            act.activation(dea[:], dac[:], ACT.Exp).then_inc(S["dt_ea"], 1)
            act.wait_ge(S["dt_ea"], 1)
            act.dma_start(scratch[1], dea[0:HEADS, :]).then_inc(S["scr_st"], 16)
            act.wait_ge(S["dt_tp"], 1)
            tp = psum[5][:].rearrange("p (a c h) -> p a c h", a=4, c=NCH)
            act.activation(dtT[:], tp[:, 0, :, :], ACT.Copy)
            act.activation(acT[:], tp[:, 1, :, :], ACT.Copy)
            act.drain().then_inc(S["dt_tok"], 1)
            act.wait_ge(S["dt_last"], 1)
            act.activation(decT[:], psum[4][:, 0:128].rearrange("p (c h) -> p c h", c=NCH), ACT.Exp
                           ).then_inc(S["dt_dec"], 1)
            act.wait_ge(S["dt_lastd"], 1)
            act.activation(endT[:], endT[:], ACT.Exp)
            act.drain().then_inc(S["dt_lastd"], 1)
            act.wait_ge(S["pad0"], 1)

            def ssm(it, ph, k0, g, par_, prev):
                for k in range(6):
                    split_hi(act, ph, it, k0 + k)
                    act_slot(act, k, g, par_, prev, it, ph, k0 + k, True)

            def ssm2(it):
                ssm(it, "ssm", 0, it * 2 + 1, 1, True)
                ssm(it, "ssm", 6, it * 2 + 2, 0, True)

            ssm(0, "ssm0", 0, 0, 0, False)
            run(act, 3, ssm2)
            ssm(0, "ssm7", 0, 7, 1, True)
            for k in range(8):
                split_hi(act, "gate_ssm", 0, k)
                if k < 6:
                    act_slot(act, k, 8, 0, True, 0, "gate_ssm", k, False)
                wait_unit(act, "gate_ssm", 0, k)
                act.activation(mg[:, k, :], bank("gate_ssm", k)[:], ACT.Sigmoid)
                act.drain().then_inc(freed("gate_ssm", k), 1)
            act.wait_ge(S["f_fin"], SSM_GROUPS)
            act.dma_start(xr[:], xT.rearrange("(k p) t -> p k t", p=P)).then_inc(N2["x2_ld"], 16)
            only_hi(act, "ssm_out")

            def conv(it):
                for k in range(4):
                    split_hi(act, "conv", it, k)
                    wait_unit(act, "conv", it, k)
                    if k == 0:
                        wait(act, N2["cc_x"], it)
                        act.activation(ccs[:], bank("conv", 0)[:], ACT.Copy).then_inc(N2["cc_a"], 1)
                        act.drain().then_inc(freed("conv", 0), 1)
                    if k == 3:
                        at = bass.ds(it, 1)
                        act.activation(sgs[:, at, :].rearrange("p a t -> p (a t)"), bank("conv", 3)[:], ACT.Sigmoid)
                        act.drain().then_inc(freed("conv", 3), 1)
                        act.wait_ge(N2["cc_y"], it + 1)
                        act.activation(vhi[:, at, :].rearrange("p a t -> p (a t)"), cy[:], ACT.Copy).then_inc(N2["cc_h"], 1)
            conv(0)
            with act.Fori(1, 8) as it:
                conv(it)
            act.drain().then_inc(N2["cg_a"], 1)

            def conv_out(it):
                for k in range(4):
                    split_hi(act, "conv_out", it, k)
                    act.wait_ge(N2["co_d"], it * 4 + k + 1)
                    act.activation(uhi[:, bass.ds(it * 4 + k, 1), :], mg[:, bass.ds(it * 4 + k, 1), :],
                                   ACT.Copy).then_inc(N2["mh"], 1)
            run(act, 2, conv_out)
            only_hi(act, "w_o")
            norm_b.act(act, lambda e, j: e.wait_ge(N2["wo_d"], j + 1))
            mlp_up_act(act, "up1a", 0)
            only_hi(act, "down1a")
            mlp_up_act(act, "up1b", 16)
            only_hi(act, "down1b")
            norm_f1.act(act, lambda e, j: e.wait_ge(N2["dn_d"], j + 1))
            act.wait_ge(N2["ada_read"], 3)
            act.wait_ge(N2["dn_d"], 8)
            act.dma_start(xc[:], ctxT.rearrange("(k p) t -> p k t", p=P)).then_inc(G["xc_ld"], 16)
            act.dma_start(gcon[:], gconsts).then_inc(G["gcon_ld"], 16)
            act.dma_start(wa1[:], w_a1).then_inc(G["wa1_ld"], 16)
            norm_g.act(act, lambda e, j: norm_f1.ready(e, j + 1))
            norm_g.ready(act, 8)
            act.wait_ge(G["xc_ld"], 16)
            norm_c.act(act, lambda e, j: None)
            for k in range(4):
                split_hi(act, "gla_q", 0, k)
                wait_unit(act, "gla_q", 0, k)
                act.activation(qf[:, k, :], bank("gla_q", k)[:], ACT.Copy, scale=float(P) ** -0.5)
                act.drain().then_inc(freed("gla_q", k), 1)
            act.wait_ge(G["wa1_ld"], 16)
            act.activation(wa1h[:], wa1[:], ACT.Copy).then_inc(G["wa1_h"], 1)

            def gla_r(it):
                for k in range(4):
                    split_hi(act, "gla_r", it, k)
                    wait_unit(act, "gla_r", it, k)
                    act.activation(rf[:, bass.ds(it * 4 + k, 1), :].rearrange("p a t -> p (a t)"),
                                   bank("gla_r", k)[:], ACT.Silu)
                    act.drain().then_inc(freed("gla_r", k), 1)
            run(act, 2, gla_r)
            act.wait_ge(G["az_d"], 1)
            act.activation(az[:, TC:], psum[4][:], ACT.Copy)
            act.activation(az[:, :TC], psum[5][:, :TC], ACT.Copy)
            act.drain().then_inc(G["az_a"], 1)
            for k in range(4):
                split_hi(act, "gla_k", 0, k)
                wait_unit(act, "gla_k", 0, k)
                act.activation(kf[:, k, TC:], bank("gla_k", k)[:], ACT.Copy)
                act.activation(kf[:, k, :TC], psum[4 + k % 2][:, :TC], ACT.Copy).then_inc(G["g_k"], 1)
                act.drain().then_inc(freed("gla_k", k), 1)
            for k in range(8):
                split_hi(act, "gla_v", 0, k)
                wait_unit(act, "gla_v", 0, k)
                wait(act, G["v_t"], k - 1)
                act.activation(vf[:, k % 2, TC:], bank("gla_v", k)[:], ACT.Copy)
                act.activation(vf[:, k % 2, :TC], psum[4 + k % 2][:, :TC], ACT.Copy).then_inc(G["v_a"], 1)
                act.drain().then_inc(freed("gla_v", k), 1)
            act.wait_ge(G["v_d"], 8)
            run(act, NGLA, lambda h: gla_act(act, h), peel_first=True)
            only_hi(act, "gla_o")
            norm_m.act(act, lambda e, j: e.wait_ge(G["go_d"], j + 1))
            mlp_up_act(act, "up2a", 32)
            only_hi(act, "down2a")
            mlp_up_act(act, "up2b", 48)
            only_hi(act, "down2b", peel_last=True)
            norm_f2.act(act, lambda e, j: e.wait_ge(N2["dn_d"], 8 + j + 1))

        @block.vector
        def _(dve):
            dve.wait_ge(in_ld, 32)
            dve.wait_ge(S["mod_ps"], 1)
            dve.tensor_tensor(mod[:, 0:16], psum[7][:, 256:272], par[:, PCOL["b_ada"]:PCOL["b_ada"] + 16], ALU.add)
            dve.drain()
            dve.scalar_tensor_tensor(g1s[:, 0:8], mod[:, 8:16], 1.0, par[:, PCOL["ln1"]:PCOL["ln1"] + 8],
                                     ALU.add, ALU.mult)
            dve.drain()
            for u in range(AHEAD - 1):
                lo_part(dve, u, 0)
            norm_a.dve(dve)
            dve.wait_ge(S["dw_hi"], 1)
            dve.tensor_tensor(dwl[:], dw[:], dwh[:].bitcast(f32), ALU.subtract).then_inc(S["dw_lo"], 1)
            lo_part(dve, AHEAD - 1, 0)
            dve.wait_ge(S["dt_e"], 1)
            dve.tensor_scalar(dd[:], de[:], 1.0, None, ALU.add).then_inc(S["dt_w"], 1)
            dve.drain()
            dve.reciprocal(dr[:], dd[:])
            dve.tensor_scalar(dac[:], dd[:], -1.0, None, ALU.add)
            dve.drain()
            dve.tensor_tensor(de[:], de[:], dac[:], ALU.subtract)
            dve.drain()
            dve.tensor_tensor(de[:], de[:], dr[:], ALU.mult)
            dve.wait_ge(S["dt_ln"], 1)
            dve.drain()
            dve.tensor_tensor(de[:], de[:], dl[:], ALU.add)
            dve.drain()
            dve.scalar_tensor_tensor(dd[:], dx[:], 0.0, de[:], ALU.max, ALU.add)
            dve.wait_ge(S["dt_nega"], 1)
            dve.drain()
            dve.tensor_scalar(dr[:], dd[:], nega[:], -1.0, ALU.mult, ALU.mult)
            dve.drain()
            dve.tensor_tensor_scan(dac[:], resets, dr[:], 0.0, ALU.mult, ALU.add).then_inc(S["dt_ac"], 1)
            dve.wait_ge(S["dt_dec"], 1)
            dve.tensor_tensor(endT[:], psum[4][:, 0:128].rearrange("p (c h) -> p c h", c=NCH), acT[:],
                              ALU.subtract).then_inc(S["dt_lastd"], 1)
            dve.wait_ge(S["dt_lastd"], 2)
            dve.tensor_tensor(endT[:], endT[:], dtT[:], ALU.mult).then_inc(S["dt_done"], 1)
            dve.drain()
            dve.wait_ge(S["pad0"], 1)

            def ssm(it, ph, k0, g, par_, prev):
                for k in range(6):
                    split_lo(dve, ph, it, k0 + k)
                    dve_slot(dve, k, g, par_, prev, True)

            def ssm2(it):
                ssm(it, "ssm", 0, it * 2 + 1, 1, True)
                ssm(it, "ssm", 6, it * 2 + 2, 0, True)

            ssm(0, "ssm0", 0, 0, 0, False)
            run(dve, 3, ssm2)
            ssm(0, "ssm7", 0, 7, 1, True)
            for k in range(8):
                split_lo(dve, "gate_ssm", 0, k)
                if k < 6:
                    dve_slot(dve, k, 8, 0, True, False)
            dve.memset(ccx[:, 0:2], 0.0)
            dve.drain()

            def ssm_out(it):
                for k in range(4):
                    split_lo(dve, "ssm_out", it, k)
                    if k % 2:
                        m = mg[:, bass.ds(it * 2 + k // 2, 1), :].rearrange("p a t -> p (a t)")
                        wait_unit(dve, "ssm_out", it, k)
                        dve.tensor_tensor(m, m, bank("ssm_out", k // 2)[:], ALU.mult)
                        dve.drain().then_inc(freed("ssm_out", k // 2), 1)
            run(dve, 4, ssm_out)

            def conv(it):
                for k in range(4):
                    split_lo(dve, "conv", it, k)
                    if k == 1:
                        dve.wait_ge(N2["cc_a"], it + 1)
                        wait_unit(dve, "conv", it, 1)
                        dve.tensor_tensor(ccx[:, 2:], ccs[:], bank("conv", 1)[:], ALU.mult).then_inc(N2["cc_x"], 1)
                        dve.drain().then_inc(freed("conv", 1), 1)
                        dve.tensor_scalar(ct[:], ccx[:, 2:], pcd("conv_w", it + 16), None, ALU.mult)
                        dve.drain()
                        for tap in range(2):
                            dve.scalar_tensor_tensor(ct[:], ccx[:, tap:tap + T], pcd("conv_w", it + 8 * tap), ct[:],
                                                     ALU.mult, ALU.add)
                            dve.drain()
                    if k == 2:
                        wait_unit(dve, "conv", it, 2)
                        wait(dve, N2["cc_h"], it)
                        dve.tensor_tensor(cy[:], ct[:], bank("conv", 2)[:], ALU.mult).then_inc(N2["cc_y"], 1)
                        dve.drain().then_inc(freed("conv", 2), 1)
                    if k == 3:
                        at = bass.ds(it, 1)
                        dve.wait_ge(N2["cc_h"], it + 1)
                        dve.tensor_tensor(vlo[:, at, :].rearrange("p a t -> p (a t)"), cy[:],
                                          vhi[:, at, :].rearrange("p a t -> p (a t)").bitcast(f32),
                                          ALU.subtract).then_inc(N2["cc_l"], 1)
                        dve.drain()
            conv(0)
            with dve.Fori(1, 8) as it:
                conv(it)
            dve.wait_ge(N2["cg_a"], 1)

            def conv_out(it):
                for k in range(4):
                    at = bass.ds(it * 4 + k, 1)
                    m = mg[:, at, :].rearrange("p a t -> p (a t)")
                    split_lo(dve, "conv_out", it, k)
                    wait_unit(dve, "conv_out", it, k)
                    dve.tensor_tensor(ct[:], sgs[:, at, :].rearrange("p a t -> p (a t)"), bank("conv_out", k)[:], ALU.mult)
                    dve.drain().then_inc(freed("conv_out", k), 1)
                    dve.tensor_tensor(m, m, ct[:], ALU.add).then_inc(N2["co_d"], 1)
                    dve.drain()
                    dve.wait_ge(N2["mh"], it * 4 + k + 1)
                    dve.tensor_tensor(ulo[:, at, :].rearrange("p a t -> p (a t)"), m,
                                      uhi[:, at, :].rearrange("p a t -> p (a t)").bitcast(f32),
                                      ALU.subtract).then_inc(N2["ml"], 1)
                    dve.drain()
            run(dve, 2, conv_out)
            b1 = PCOL["b_ada"]
            ada_dve(dve, 1, [(16, 0, 32, b1 + 16)])
            dve.scalar_tensor_tensor(g1s[:, 8:16], mod[:, 32:40], 1.0, par[:, PCOL["ln2"]:PCOL["ln2"] + 8],
                                     ALU.add, ALU.mult)
            dve.wait_ge(N2["x2_ld"], 16)
            dve.drain()

            def w_o(it):
                for k in range(4):
                    at = bass.ds(it * 4 + k, 1)
                    x = xr[:, at, :].rearrange("p a t -> p (a t)")
                    split_lo(dve, "w_o", it, k)
                    wait_unit(dve, "w_o", it, k)
                    dve.scalar_tensor_tensor(x, bank("w_o", k)[:], mod[:, bass.ds(it * 4 + 16 + k, 1)], x,
                                             ALU.mult, ALU.add).then_inc(N2["wo_d"], 1)
                    dve.drain().then_inc(freed("w_o", k), 1)
            run(dve, 2, w_o)
            norm_b.dve(dve)
            mlp_up_dve(dve, "up1a", 0)
            mlp_down_dve(dve, "down1a", False, 0)
            b2 = PCOL["b_ada_2"]
            ada_dve(dve, 2, [(48, 0, 16, b2), (96, 16, 16, b2)])
            mlp_up_dve(dve, "up1b", 16)
            mlp_down_dve(dve, "down1b", True, 40)
            ada_dve(dve, 3, [(64, 0, 32, b2 + 16)])
            for at, scale, gain in ((16, 104, "norm1"), (24, 56, "norm1"), (32, 80, "norm2")):
                dve.scalar_tensor_tensor(g1s[:, at:at + 8], mod[:, scale:scale + 8], 1.0,
                                         par[:, PCOL[gain]:PCOL[gain] + 8], ALU.add, ALU.mult)
            dve.drain()
            norm_f1.dve(dve)
            norm_g.dve(dve)
            norm_c.dve(dve)
            for k in range(4):
                split_lo(dve, "gla_q", 0, k)
            dve.wait_ge(G["wa1_h"], 1)
            dve.tensor_tensor(wa1l[:], wa1[:], wa1h[:].bitcast(f32), ALU.subtract).then_inc(G["wa1_l"], 1)

            def only_lo(ph):
                p = PH[ph]

                def step(it):
                    for k in range(p["n"]):
                        split_lo(dve, ph, it, k)
                run(dve, p["steps"], step)
            only_lo("gla_r")
            only_lo("gla_k")
            for k in range(9):
                if k < 8:
                    split_lo(dve, "gla_v", 0, k)
                if k >= 1:
                    j = k - 1
                    dve.wait_ge(G["v_t"], j + 1)
                    dve.tensor_copy(vt[:, 0:4, j * P:(j + 1) * P], psum[6][:].rearrange("p (i v) -> p i v", i=4))
                    dve.tensor_copy(vt[:, 4:6, j * P:(j + 1) * P], psum[7][:, :TC].rearrange("p (i v) -> p i v", i=2))
                    dve.drain().then_inc(G["v_d"], 1)
            dve.wait_ge(G["gcon_ld"], 16)
            dve.wait_ge(G["am0"], 1)
            run(dve, NGLA, lambda h: gla_dve(dve, h), peel_first=True)

            def gla_o(it):
                for k in range(4):
                    x = xr[:, bass.ds(it * 4 + k, 1), :].rearrange("p a t -> p (a t)")
                    split_lo(dve, "gla_o", it, k)
                    wait_unit(dve, "gla_o", it, k)
                    dve.scalar_tensor_tensor(x, bank("gla_o", k)[:], mod[:, bass.ds(it * 4 + 64 + k, 1)], x,
                                             ALU.mult, ALU.add).then_inc(G["go_d"], 1)
                    dve.drain().then_inc(freed("gla_o", k), 1)
            run(dve, 2, gla_o)
            norm_m.dve(dve)
            mlp_up_dve(dve, "up2a", 32)
            mlp_down_dve(dve, "down2a", False, 0)
            mlp_up_dve(dve, "up2b", 48)
            mlp_down_dve(dve, "down2b", True, 88, peel_last=True)
            norm_f2.dve(dve)

        @block.tensor
        def _(pe):
            pe.wait_ge(in_ld, 32)
            norm_a.pe(pe)
            pe.wait_ge(S["cact"], 1)
            for j in range(16):
                if j % 2 == 0:
                    pe.wait_ge(slab_ld[j // 2], 16)
                for k in range(KT):
                    mm = pe.matmul(psum[7][:, 256 + j:257 + j], slab[:, j // 2, k, (j % 2) * P:(j % 2 + 1) * P],
                                   c_act[:, k:k + 1], start=k == 0, stop=k == KT - 1)
            mm.then_inc(S["mod_ps"], 1)
            pe.wait_ge(S["dw_lo"], 1)
            split_products(pe, psum[4][:], dwh[:], dwl[:], u_h, u_l, True, True,
                           lambda k: norm_a.ready(pe, k + 1)).then_inc(S["dt_ps"], 1)

            def ssm(it, ph, k0, g, par_, prev):
                for k in range(6):
                    pe_unit(pe, ph, it, k0 + k, u_h, u_l)
                    if not prev and k == 0:
                        pe.wait_ge(S["dt_ac"], 1)
                        for a, src in ((0, dd), (1, dac)):
                            for c in range(NCH):
                                mm = pe.transpose(psum[5][:, a * 128 + c * 32:a * 128 + c * 32 + 32],
                                                  src[0:HEADS, c * CH:(c + 1) * CH], ident[0:HEADS, 0:HEADS])
                        mm.then_inc(S["dt_tp"], 1)
                    if not prev and k == 1:
                        pe.wait_ge(S["dt_tok"], 1)
                        pe.matmul(psum[4][:, 0:128], last_row, acT[:].rearrange("p c h -> p (c h)"),
                                  start=True, stop=True).then_inc(S["dt_last"], 1)
                    if not prev and k == 4:
                        pe.wait_ge(S["dt_done"], 1)
                    pe_slot(pe, k, g, par_, prev)

            def ssm2(it):
                ssm(it, "ssm", 0, it * 2 + 1, 1, True)
                ssm(it, "ssm", 6, it * 2 + 2, 0, True)

            ssm(0, "ssm0", 0, 0, 0, False)
            run(pe, 3, ssm2)
            ssm(0, "ssm7", 0, 7, 1, True)
            for k in range(8):
                pe_unit(pe, "gate_ssm", 0, k, u_h, u_l)
                if k < 6:
                    pe_slot(pe, k, 8, 0, True)
            pe.wait_ge(S["f_fin"], SSM_GROUPS)

            def ssm_out(it):
                for k in range(4):
                    half = k % 2
                    pe_unit(pe, "ssm_out", it, k, lambda t: v_h(t + 8 * half), lambda t: v_l(t + 8 * half),
                            out_i=k // 2, first=half == 0, last=half == 1)
            run(pe, 4, ssm_out)

            def plain(ph, hi, lo):
                p = PH[ph]

                def step(it):
                    for k in range(p["n"]):
                        pe_unit(pe, ph, it, k, hi, lo)
                run(pe, p["steps"], step)
            plain("conv", u_h, u_l)
            pe.wait_ge(N2["cc_l"], 8)
            plain("conv_out", v_h, v_l)
            ada_pe(pe, 1)
            pe.wait_ge(N2["ml"], 8)
            plain("w_o", u_h, u_l)
            norm_b.pe(pe)
            norm_b.ready(pe, 8)
            plain("up1a", u_h, u_l)
            mlp_down_pe(pe, "down1a", 0)
            ada_pe(pe, 2)
            plain("up1b", u_h, u_l)
            mlp_down_pe(pe, "down1b", 16)
            ada_pe(pe, 3)
            norm_f1.pe(pe)
            norm_g.pe(pe)
            norm_c.pe(pe)
            norm_g.ready(pe, 8)
            plain("gla_q", u_h, u_l)
            plain("gla_r", u_h, u_l)
            norm_c.ready(pe, 8)
            pe.wait_ge(G["wa1_l"], 1)
            split_products(pe, psum[4][:], wa1h[:], wa1l[:], u_h, u_l, True, True)
            split_products(pe, psum[5][:, :TC], wa1h[:], wa1l[:], lambda t: uch[:, t, :], lambda t: ucl[:, t, :],
                           True, True).then_inc(G["az_d"], 1)
            for k in range(4):
                if k == 0:
                    pe.wait_ge(G["az_a"], 1)
                wait(pe, G["g_k"], k - 1)
                both(pe, "gla_k", k)
            for k in range(9):
                if k < 8:
                    if k < 2:
                        pe.wait_ge(G["g_k"], 3 + k)
                    wait(pe, G["v_a"], k - 1)
                    both(pe, "gla_v", k)
                if k >= 1:
                    j = k - 1
                    pe.wait_ge(G["v_a"], j + 1)
                    wait(pe, G["v_d"], j)
                    for i in range(TA // P):
                        b = psum[6] if i < 4 else psum[7]
                        mm = pe.transpose(b[:, (i % 4) * P:(i % 4 + 1) * P], vf[:, j % 2, i * P:(i + 1) * P], ident)
                    mm.then_inc(G["v_t"], 1)
            pe.wait_ge(G["v_d"], 8)
            pe.wait_ge(bank_free[0], PH["gla_o"]["used"][0])
            pe.wait_ge(bank_free[1], PH["gla_o"]["used"][1])
            pe.wait_ge(bank_free[2], PH["gla_o"]["used"][2])
            pe.wait_ge(bank_free[3], PH["gla_o"]["used"][3])
            run(pe, NGLA, lambda h: gla_pe(pe, h), peel_first=True)
            pe.wait_ge(G["o_lo"], NGLA)
            plain("gla_o", u_h, u_l)
            norm_m.pe(pe)
            norm_m.ready(pe, 8)
            plain("up2a", u_h, u_l)
            mlp_down_pe(pe, "down2a", 32)
            plain("up2b", u_h, u_l)
            mlp_down_pe(pe, "down2b", 48)
            norm_f2.pe(pe)


def weight_units(i):
    import numpy as np

    def unit(w, row, col):
        return w[row:row + D, col:col + P].reshape(KT, P, P).transpose(1, 0, 2).reshape(P, KT * P)

    w_in, inner = i["w_in"][0], 2048
    gates, cb, cc, cx, z, xbc = 0, 2048, 3072, 4096, 5120, 7168
    b0, c0 = xbc + inner, xbc + inner + SSM_GROUPS * P
    out = []
    for g in range(SSM_GROUPS):
        cols = [b0 + g * P, c0 + g * P, xbc + 2 * g * P, xbc + (2 * g + 1) * P, z + 2 * g * P, z + (2 * g + 1) * P]
        out += [unit(w_in, 0, c) for c in cols]
    out += [unit(w_in, 0, gates + D + j * P) for j in range(KT)]
    out += [unit(i["w_ssm_out"][0], h * D, j * P) for j in range(KT) for h in range(2)]
    out += [unit(w_in, 0, c + j * P) for j in range(KT) for c in (cc, cx, cb, gates)]
    out += [unit(i["w_conv_out"][0], 0, j * P) for j in range(KT)]
    out += [unit(i["w_o"][0], 0, j * P) for j in range(KT)]

    def mlp(up, down):
        for half in range(2):
            for j in range(16):
                yield unit(up, 0, (16 * half + j) * P)
            for j in range(KT):
                for h in range(2):
                    yield unit(down, (2 * half + h) * D, j * P)
    out += mlp(i["w_up"][0], i["w_down"][0])
    gla = i["gla_w_in_2"][0]
    for at, n in ((0, 4), (2048, 8), (512, 4), (1024, 8)):
        out += [unit(gla, 0, at + j * P) for j in range(n)]
    out += [unit(i["gla_w_o_2"][0], 0, j * P) for j in range(KT)]
    out += mlp(i["mlp_w1_2"][0], i["mlp_w2_2"][0])
    assert len(out) == UNITS
    return np.stack(out)


def packed_params(i):
    import numpy as np

    def cols(v):
        return np.asarray(v).reshape(-1, P).T

    inner = 2048
    conv = np.asarray(i["ssm_conv_w"][0])
    bias = np.asarray(i["ssm_conv_b"][0])
    tiles = []
    for g in range(SSM_GROUPS):
        tiles += [inner + g * P, inner + SSM_GROUPS * P + g * P, 2 * g * P, (2 * g + 1) * P]
    ssm_w = np.stack([conv[tap, t:t + P] for tap in range(4) for t in tiles], axis=1)
    ssm_b = np.stack([bias[t:t + P] for t in tiles], axis=1)
    skip = np.repeat(i["d_skip"][0], 64)
    parts = {
        "b_ada": cols(i["b_ada"][0]), "ln1": cols(i["ln1"][0]), "ln2": cols(i["ln2"][0]),
        "conv_w": cols(i["conv_w"][0]), "ssm_w": ssm_w, "ssm_b": ssm_b, "ssm_norm": cols(i["ssm_norm_w"][0]),
        "d_skip": cols(skip), "dt_bias": np.tile(i["dt_bias"][0], 4)[:, None], "a_log": np.tile(i["a_log"][0], 4)[:, None],
        "final_norm": cols(i["final_norm"]), "c": cols(i["c"][0]), "c_2": cols(i["c_2"][0]), "c_ctx": cols(i["c_ctx_2"]),
        "b_ada_2": cols(i["ada_b_2"][0]), "norm1": cols(i["norm1_g_2"][0]), "norm2": cols(i["norm2_g_2"][0]),
        "b_a": cols(i["gla_b_a_2"][0]), "g_head": cols(i["gla_g_head_2"][0]), "final_2": cols(i["final_g_2"]),
    }
    for name, width in PARAMS:
        assert parts[name].shape == (P, width), (name, parts[name].shape)
    return np.ascontiguousarray(np.concatenate([parts[n] for n, _ in PARAMS], axis=1))


def constants():
    import numpy as np
    f = np.float32
    s, t = np.arange(P)[:, None], np.arange(P)[None, :]
    last = np.zeros((P, P), f)
    last[P - 1] = 1.0
    con = [np.eye(P, dtype=f), np.ones((P, P), f), last, np.where(t >= s, 0.0, -1e30).astype(f),
           np.broadcast_to((np.arange(T) % CH != 0).astype(f), (P, T))]
    same = s // GC == t // GC
    at = np.arange(TA) % GC
    gcon = [np.broadcast_to((at != 0).astype(f), (P, TA)), np.broadcast_to((at != GC - 1).astype(f), (P, TA)),
            (same & (t >= s)).astype(f), (same & (t <= s)).astype(f)]
    return np.concatenate(con, axis=1), np.concatenate(gcon, axis=1)


def kernel(**inputs):
    import numpy as np
    import concourse.bacc as bacc
    from concourse.bass_utils import run_bass_kernel_spmd

    i = {k: np.asarray(v) for k, v in inputs.items()}

    def tiles(w):
        return np.ascontiguousarray(w.reshape(KT, P, P).transpose(1, 0, 2).reshape(P, KT * P))

    a1 = np.zeros((D, P), np.float32)
    for d in range(2):
        a1[:, 32 * d:32 * d + 16] = i["gla_w_a1_2"][0, d]
    con, gcon = constants()
    arrays = {
        "xT": np.ascontiguousarray(i["x"][0].T),
        "ctxT": np.ascontiguousarray(i["ctx_2"][0].T),
        "units": weight_units(i),
        "w_dt": tiles(np.concatenate([i["w_in"][0][:, 11264:11296]] * 4, axis=1)),
        "w_a1": tiles(a1),
        "w_a2": np.ascontiguousarray(i["gla_w_a2_2"][0]),
        "ada1": np.ascontiguousarray(i["w_ada"][0]),
        "ada2": np.ascontiguousarray(i["ada_w_2"][0]),
        "params": packed_params(i),
        "consts": con,
        "gconsts": gcon,
    }
    nc = bacc.Bacc("TRN2", target_bir_lowering=False, num_devices=1)
    args = [nc.dram_tensor(f"in_{n}", a.shape, mybir.dt.from_np(a.dtype), kind="ExternalInput").ap()
            for n, a in arrays.items()]
    out = nc.dram_tensor("outT", (D, T), mybir.dt.float32, kind="ExternalOutput").ap()
    build(nc, *args, out)
    r = run_bass_kernel_spmd(nc, [{f"in_{n}": a for n, a in arrays.items()}], core_ids=[0])
    return np.ascontiguousarray(r.results[0]["outT"].T)[None]
```

```python
import concourse.bass as bass
from concourse import mybir
from contextlib import ExitStack

P = 128
D = 1024
T = 512
TC = 256
TA = T + TC
KT = D // P
SSM_GROUPS = 8
HEADS = 32
CH = 128
NCH = T // CH
NGLA = 4
GV = 256
GC = 64
TAU = 16.0
EPS = 1e-6
SLOTS = 4
RAW = 2
ARING = 4
ADA_PIECES = [64, 96, 160]
AHEAD = SLOTS - 1

PHASES = [
    ("ssm0", 6, [0, 1, 2, 3, 0, 1], 1),
    ("ssm", 12, [2, 3, 0, 1, 2, 3, 0, 1, 2, 3, 0, 1], 3),
    ("ssm7", 6, [2, 3, 0, 1, 2, 3], 1),
    ("gate_ssm", 8, [0, 1, 2, 3, 0, 1, 2, 3], 1),
    ("ssm_out", 4, [0, 1], 4),
    ("conv", 4, [0, 1, 2, 3], 8),
    ("conv_out", 4, [0, 1, 2, 3], 2),
    ("w_o", 4, [0, 1, 2, 3], 2),
    ("up1a", 4, [0, 1, 2, 3], 4), ("down1a", 4, [0, 1], 4),
    ("up1b", 4, [0, 1, 2, 3], 4), ("down1b", 4, [0, 1], 4),
    ("gla_q", 4, [0, 1, 2, 3], 1), ("gla_k", 4, [0, 1, 2, 3], 1),
    ("gla_v", 8, [0, 1, 2, 3, 0, 1, 2, 3], 1), ("gla_r", 8, [0, 1, 2, 3, 0, 1, 2, 3], 1),
    ("gla_o", 4, [0, 1, 2, 3], 2),
    ("up2a", 4, [0, 1, 2, 3], 4), ("down2a", 4, [0, 1], 4),
    ("up2b", 4, [0, 1, 2, 3], 4), ("down2b", 4, [0, 1], 4),
]


def phase_table():
    table, unit, used = {}, 0, [0, 0, 0, 0]
    for name, n, banks, steps in PHASES:
        table[name] = dict(u0=unit, n=n, steps=steps, banks=banks, used=list(used),
                           per=[banks.count(b) for b in range(4)])
        unit += n * steps
        for b in range(4):
            used[b] += banks.count(b) * steps
    table["end"] = dict(u0=unit)
    return table


PH = phase_table()
UNITS = PH["end"]["u0"]

PARAMS = [("b_ada", 48), ("ln1", 8), ("ln2", 8), ("conv_w", 24), ("ssm_w", 128), ("ssm_b", 32),
          ("ssm_norm", 16), ("d_skip", 16), ("dt_bias", 1), ("a_log", 1), ("final_norm", 8), ("c", 8),
          ("c_2", 8), ("c_ctx", 8), ("b_ada_2", 48), ("norm1", 8), ("norm2", 8), ("b_a", 8),
          ("g_head", 8), ("final_2", 8)]
PCOL, _at = {}, 0
for _n, _w in PARAMS:
    PCOL[_n] = _at
    _at += _w
NPAR = _at
CONSTS = [("ident", 128), ("ones", 128), ("last_row", 128), ("causal_add", 128), ("resets", 512)]
CCOL, _at = {}, 0
for _n, _w in CONSTS:
    CCOL[_n] = _at
    _at += _w
NCON = _at
GCON = [("reset_f", TA), ("reset_b", TA), ("mask_f", 128), ("mask_b", 128)]
GCOL, _at = {}, 0
for _n, _w in GCON:
    GCOL[_n] = _at
    _at += _w
NGCON = _at


def build(nc, xT, ctxT, units, w_dt, w_a1, w_a2, ada1, ada2, params, consts, gconsts, outT):
    f32, f32r, i32 = mybir.dt.float32, mybir.dt.float32r, mybir.dt.int32
    ALU, ACT = mybir.AluOpType, mybir.ActivationFunctionType

    scratch = nc.dram_tensor("decay_rows", (2, HEADS, T), f32, kind="Internal").ap()

    ctx = ExitStack()
    with ctx:
        base = (nc.sbuf_base + 31) // 32 * 32
        end = nc.sbuf_usable_end // 32 * 32

        class Region:
            def __init__(self, start, size):
                self.at, self.end = start, start + size

            def take(self, name, shape, dt=f32):
                n = 4
                for s in shape[1:]:
                    n *= s
                t = nc.alloc_sbuf_tensor_at(name, shape, dt, offset=self.at)
                self.at += (n + 31) // 32 * 32
                assert self.at <= self.end, (name, self.at, self.end)
                return t

        def sem(name):
            return ctx.enter_context(nc.semaphore(name))

        keep = Region(base, 6912)
        par = keep.take("par", [P, NPAR])
        con = keep.take("con", [P, NCON])
        mod = keep.take("mod", [P, 112 + 16])
        g1s = keep.take("g1s", [P, 40])
        c_act = keep.take("c_act", [P, 24])
        glb = keep.take("glb", [P, 2, 12])
        gld = keep.take("gld", [P, 2, 2, 12])
        tick = keep.take("tick", [P, 1])
        RW = keep.end
        rings = Region(RW, 40960)
        wraw = rings.take("wraw", [P, RAW, KT * P])
        whi = rings.take("whi", [P, SLOTS, KT * P], f32r)
        wlo = rings.take("wlo", [P, SLOTS, KT * P], f32r)
        RU = rings.end
        ureg = Region(RU, 32768)
        uhi = ureg.take("uhi", [P, KT, T], f32r)
        ulo = ureg.take("ulo", [P, KT, T], f32r)
        RV = ureg.end
        vreg = Region(RV, 65536)
        vhi = vreg.take("vhi", [P, 16, T], f32r)
        vlo = vreg.take("vlo", [P, 16, T], f32r)
        RM = vreg.end
        mreg = Region(RM, 16384)
        mg = mreg.take("mg", [P, KT, T])
        RT = mreg.end
        WORK = end - RT

        x0 = Region(RM, 16384).take("x0", [P, KT, T])
        slab = Region(RV, 65536).take("slab", [P, 8, KT, 256])
        NT = Region(end - 10240, 10240)
        nsq = NT.take("nsq", [P, 2, T])
        nrs = NT.take("nrs", [P, T])
        nt = NT.take("nt", [P, 2, T])
        dtr = Region(RV, 40960)
        dw = dtr.take("dw", [P, KT * P])
        dwh = dtr.take("dwh", [P, KT * P], f32r)
        dwl = dtr.take("dwl", [P, KT * P], f32r)
        dx, de, dd, dl, dr, dac, dea = [dtr.take(n, [P, T]) for n in ("dx", "de", "dd", "dl", "dr", "dac", "dea")]
        nega = dtr.take("nega", [P, 1])
        sr = Region(RT, WORK)
        pads = sr.take("pads", [P, 2, T + 3])
        bc = sr.take("bc", [P, 2, 2, T])
        xs = sr.take("xs", [P, 2, T])
        ys = sr.take("ys", [P, 2, 2, T])
        zs = sr.take("zs", [P, 2, T])
        es = sr.take("es", [P, NCH, 4, CH])
        eac = sr.take("eac", [P, 2, T])
        srs = sr.take("srs", [P, T])
        dtT = sr.take("dtT", [P, NCH, HEADS])
        acT = sr.take("acT", [P, NCH, HEADS])
        endT = sr.take("endT", [P, NCH, HEADS])
        decT = sr.take("decT", [P, NCH, HEADS])
        v14 = Region(RV + 14 * 2048, 4096)
        xdt = v14.take("xdt", [P, 2, 256])
        xend = v14.take("xend", [P, 2, 256])
        v14l = Region(RV + 32768 + 14 * 2048, 4096)
        bT = v14l.take("bT", [P, 2, CH])
        st = v14l.take("st", [P, 256])
        ty = v14l.take("ty", [P, 2, CH])
        cr = Region(RT, WORK)
        xr = cr.take("xr", [P, KT, T])
        aacc = cr.take("aacc", [P, 4096])
        aring = cr.take("aring", [P, ARING, 512])
        CT = cr.at
        ccx = cr.take("ccx", [P, T + 2])
        ccs = cr.take("ccs", [P, T])
        ct = cr.take("ct", [P, T])
        cy = cr.take("cy", [P, T])
        mr = Region(CT, end - CT)
        r1 = mr.take("r1", [P, 2, T])
        hq = mr.take("hq", [P, T])

        gv = Region(RV, 65536)
        kf = gv.take("kf", [P, NGLA, TA])
        qf = gv.take("qf", [P, NGLA, T])
        rf = gv.take("rf", [P, KT, T])
        VT = gv.at
        vt = gv.take("vt", [P, TA // P, D])
        az = gv.take("az", [P, TA])
        wa = Region(VT, 12288)
        wa1 = wa.take("wa1", [P, KT * P])
        wa1h = wa.take("wa1h", [P, KT * P], f32r)
        wa1l = wa.take("wa1l", [P, KT * P], f32r)
        gu = Region(RM, 16384)
        uch = gu.take("uch", [P, KT, TC], f32r)
        ucl = gu.take("ucl", [P, KT, TC], f32r)
        gm = Region(RM, 16384)
        kdT = [gm.take(f"kdT{i}", [P, 2, TA // P, P]) for i in range(2)]
        gst = gm.take("gst", [P, 2, GV])
        atts = gm.take("atts", [P, 2, P])
        gt = Region(RT + 16384, end - 10240 - RT - 16384)
        gcon = gt.take("gcon", [P, NGCON])
        wa2c = gt.take("wa2c", [P, P])
        GT = gt.at
        zz = gt.take("zz", [P, TA])
        ez = gt.take("ez", [P, TA])
        qd = [gt.take("qd0", [P, 2, T]), nc.alloc_sbuf_tensor_at("qd1", [P, 2, T], f32, offset=RU + 6 * 2048)]
        ki = [gt.take("ki0", [P, 2, T]), nc.alloc_sbuf_tensor_at("ki1", [P, 2, T], f32, offset=RU + 14 * 2048)]
        am = gt.take("am", [P, 2, P])
        gx = Region(GT, 8192)
        xc = gx.take("xc", [P, KT, TC])
        vf = Region(GT, 6144).take("vf", [P, 2, TA])

        psum = [ctx.enter_context(nc.psum_tensor(f"bank{i}", [P, T], f32)) for i in range(8)]
        ident = con[:, CCOL["ident"]:CCOL["ident"] + 128]
        ones = con[:, CCOL["ones"]:CCOL["ones"] + 128]
        last_row = con[:, CCOL["last_row"]:CCOL["last_row"] + 128]
        causal_add = con[:, CCOL["causal_add"]:CCOL["causal_add"] + 128]
        resets = con[:, CCOL["resets"]:CCOL["resets"] + 512]

        def pc(name, j=0):
            return par[:, PCOL[name] + j:PCOL[name] + j + 1]

        def pcd(name, j):
            return par[:, bass.ds(PCOL[name] + j, 1)]

        sgs = Region(RV + 8 * 2048, 16384).take("sgs", [P, KT, T])

        w_loaded = [sem(f"w_loaded{i}") for i in range(RAW)]
        w_hi = sem("w_hi")
        w_split = sem("w_split")
        unit_done = sem("unit_done")
        bank_free = [sem(f"bank_free{i}") for i in range(4)]
        in_ld = sem("in_ld"); slab_ld = [sem(f"slab_ld{i}") for i in range(8)]
        x_ld = sem("x_ld")

        def wait(eng, s, v):
            if isinstance(v, int) and v <= 0:
                return
            eng.wait_ge(s, v)

        def run(eng, steps, body, peel_last=False, peel_first=False):
            n = steps - (1 if peel_last else 0)
            if peel_first or n == 1:
                body(0)
            if n > 1:
                with eng.Fori(1 if peel_first else 0, n) as it:
                    body(it)
            if peel_last:
                body(steps - 1)

        def split_hi(act, ph, it, k):
            p = PH[ph]
            at = p["u0"] + k + AHEAD
            if isinstance(it, int) and at + it * p["n"] >= UNITS:
                return
            hi_part(act, at, it * (p["n"] // 4) if p["n"] % 4 == 0 else 0)

        def hi_part(act, at, quads):
            act.wait_ge(w_loaded[at % RAW], (quads * 2 + at // RAW + 1) * 16)
            wait(act, unit_done, quads * 4 + at - AHEAD)
            act.activation(whi[:, at % SLOTS, :], wraw[:, at % RAW, :], ACT.Copy).then_inc(w_hi, 1)

        def split_lo(dve, ph, it, k):
            p = PH[ph]
            at = p["u0"] + k + AHEAD
            if isinstance(it, int) and at + it * p["n"] >= UNITS:
                return
            lo_part(dve, at, it * (p["n"] // 4) if p["n"] % 4 == 0 else 0)

        def lo_part(dve, at, quads):
            dve.wait_ge(w_hi, quads * 4 + at + 1)
            dve.tensor_tensor(wlo[:, at % SLOTS, :], wraw[:, at % RAW, :],
                              whi[:, at % SLOTS, :].bitcast(f32), ALU.subtract).then_inc(w_split, 1)

        def wait_unit(eng, ph, it, k):
            p = PH[ph]
            eng.wait_ge(unit_done, it * p["n"] + p["u0"] + k + 1)

        def split_products(pe, out, hi, lo, rhs_hi, rhs_lo, first, last, tiles_ready=None):
            for k in range(KT):
                if tiles_ready is not None:
                    tiles_ready(k)
                wh, wl = hi[:, k * P:(k + 1) * P], lo[:, k * P:(k + 1) * P]
                pe.matmul(out, wh, rhs_hi(k), start=first and k == 0, stop=False)
                pe.matmul(out, wh, rhs_lo(k), start=False, stop=False)
                mm = pe.matmul(out, wl, rhs_hi(k), start=False, stop=last and k == KT - 1)
            return mm

        def pe_unit(pe, ph, it, k, rhs_hi, rhs_lo, out_i=None, first=True, last=True, tiles_ready=None):
            p = PH[ph]
            out_i = k if out_i is None else out_i
            b = p["banks"][out_i]
            pe.wait_ge(w_split, it * p["n"] + p["u0"] + k + 1)
            if first:
                wait(pe, bank_free[b], it * p["per"][b] + p["used"][b] + p["banks"][:out_i].count(b))
            s = (p["u0"] + k) % SLOTS
            mm = split_products(pe, psum[b][:], whi[:, s, :], wlo[:, s, :], rhs_hi, rhs_lo, first, last, tiles_ready)
            mm.then_inc(unit_done, 1)

        def bank(ph, i):
            return psum[PH[ph]["banks"][i]]

        def freed(ph, i):
            return bank_free[PH[ph]["banks"][i]]

        norm_sem = {s: sem(f"norm_{s}") for s in ("sq", "summed", "mean", "rs", "t", "hi", "u")}

        class Norm:
            def __init__(self, order, modulated, x, tok, gain, shift, hi, lo, bank):
                self.x, self.n, self.gain, self.shift, self.hi, self.lo, self.bank = x, tok, gain, shift, hi, lo, bank
                self.one, self.all, self.mods = order, order * KT, modulated * KT

            def ready(self, eng, tiles):
                eng.wait_ge(norm_sem["u"], self.all + tiles)

            def act(self, act, x_ready):
                n = self.n
                for j in range(KT):
                    x_ready(act, j)
                    wait(act, norm_sem["summed"], self.all + j - 1)
                    act.activation(nsq[:, j % 2, :n], self.x(j), ACT.Square).then_inc(norm_sem["sq"], 1)
                act.wait_ge(norm_sem["mean"], self.one + 1)
                act.activation(nrs[:, :n], nrs[:, :n], ACT.Ln)
                act.drain()
                act.activation(nrs[:, :n], nrs[:, :n], ACT.Exp, scale=-0.5).then_inc(norm_sem["rs"], 1)
                if self.hi is not None:
                    for j in range(KT):
                        act.wait_ge(norm_sem["t"], self.mods + j + 1)
                        act.activation(self.hi(j), nt[:, j % 2, :n], ACT.Identity,
                                       scale=self.gain(j), bias=self.shift(j)).then_inc(norm_sem["hi"], 1)

            def pe(self, pe):
                for j in range(KT):
                    pe.wait_ge(norm_sem["sq"], self.all + j + 1)
                    pe.matmul(self.bank[:, :self.n], ones, nsq[:, j % 2, :self.n], start=j == 0,
                              stop=j == KT - 1).then_inc(norm_sem["summed"], 1)

            def dve(self, dve):
                n = self.n
                dve.wait_ge(norm_sem["summed"], self.all + KT)
                dve.tensor_scalar(nrs[:, :n], self.bank[:, :n], 1.0 / D, EPS, ALU.mult, ALU.add
                                  ).then_inc(norm_sem["mean"], 1)
                dve.wait_ge(norm_sem["rs"], self.one + 1)
                if self.hi is None:
                    for j in range(KT):
                        dve.scalar_tensor_tensor(self.x(j), self.x(j), self.gain(j), nrs[:, :n],
                                                 ALU.mult, ALU.mult).then_inc(norm_sem["u"], 1)
                    dve.drain()
                    return

                def scaled(j):
                    dve.tensor_tensor(nt[:, j % 2, :n], self.x(j), nrs[:, :n], ALU.mult).then_inc(norm_sem["t"], 1)
                    dve.drain()
                    dve.tensor_scalar(nsq[:, j % 2, :n], nt[:, j % 2, :n], self.gain(j), self.shift(j),
                                      ALU.mult, ALU.add)
                    dve.drain()

                scaled(0)
                for j in range(KT):
                    if j >= 1:
                        dve.wait_ge(norm_sem["hi"], self.mods + j)
                    if j + 1 < KT:
                        scaled(j + 1)
                    dve.wait_ge(norm_sem["hi"], self.mods + j + 1)
                    dve.tensor_tensor(self.lo(j), nsq[:, j % 2, :n], self.hi(j).bitcast(f32),
                                      ALU.subtract).then_inc(norm_sem["u"], 1)
                    dve.drain()

        def u_h(k):
            return uhi[:, k, :]

        def u_l(k):
            return ulo[:, k, :]

        norm_a = Norm(0, 0, lambda j: x0[:, j, :], T, lambda j: g1s[:, j:j + 1], lambda j: mod[:, j:j + 1],
                      u_h, u_l, psum[6])

        S = {n: sem(n) for n in ("cact", "mod_ps", "mod_rdy", "dw_ld", "dw_hi", "dw_lo", "dt_ps", "dt_e", "dt_w", "dt_ln", "dt_ac", "dt_ea", "scr_st", "dt_tp", "dt_tok", "dt_last", "dt_lastd", "dt_done", "dt_nega", "pad0", "cv_a", "cv_d", "cv_s", "y_skip", "z_s", "e_ld0", "e_ld1", "e_ld2", "e_ld3", "e_seg", "e_exp", "eac_ld", "pe_a", "dt_dec", "m_rdy", "pe_b", "b_dve", "f_y", "f_sq", "f_pe", "f_ms", "f_rs", "f_n", "f_hi", "f_fin")}

        def pe_a(pe, g, par_, c):
            pe.wait_ge(S["cv_s"], 4 * g + 4)
            if c == 0:
                wait(pe, S["b_dve"], 4 * g)
            b = psum[4 + c % 2]
            wait(pe, S["m_rdy"], 4 * g + c - 1)
            s = slice(c * CH, (c + 1) * CH)
            pe.matmul(b[:, 384:512], bc[:, par_, 0, s], bc[:, par_, 1, s], start=True, stop=True)
            for q in range(2):
                pe.transpose(b[:, q * 128:(q + 1) * 128], xs[:, q, s], ident)
            pe.transpose(b[:, 256:384], bc[:, par_, 0, s], ident).then_inc(S["pe_a"], 1)

        def pe_b(pe, g, par_, c):
            pe.wait_ge(S["m_rdy"], 4 * g + c + 1)
            wait(pe, S["b_dve"], 4 * g + c)
            if c == 0:
                wait(pe, S["f_ms"], g)
            s = slice(c * CH, (c + 1) * CH)
            for h in range(4):
                mm = pe.matmul(psum[6][(h % 2) * 64:(h % 2) * 64 + 64, (h // 2) * CH:(h // 2 + 1) * CH],
                               xdt[:, c % 2, h * 64:(h + 1) * 64], es[:, c, h, :], start=True, stop=True)
            if c > 0:
                for q in range(2):
                    mm = pe.matmul(psum[6][:, 256 + q * CH:256 + (q + 1) * CH], st[:, q * 128:(q + 1) * 128],
                                   bc[:, par_, 1, s], start=True, stop=True)
            if c < NCH - 1:
                mm = pe.matmul(psum[7][:, 0:256], bT[:, c % 2, :], xend[:, c % 2, :], start=True, stop=True)
            mm.then_inc(S["pe_b"], 1)

        def pe_n(pe, g):
            pe.wait_ge(S["f_sq"], g + 1)
            wait(pe, S["b_dve"], 4 * g + 4)
            for q in range(2):
                mm = pe.matmul(psum[6][:], ones, zs[:, q, :], start=q == 0, stop=q == 1)
            mm.then_inc(S["f_pe"], 1)

        def pe_slot(pe, k, g, par_, prev):
            if prev and k == 0:
                pe_a(pe, g - 1, 1 - par_, 2)
                pe_b(pe, g - 1, 1 - par_, 1)
            if prev and k == 1:
                pe_a(pe, g - 1, 1 - par_, 3)
                pe_b(pe, g - 1, 1 - par_, 2)
            if prev and k == 2:
                pe_b(pe, g - 1, 1 - par_, 3)
            if prev and k == 4:
                pe_n(pe, g - 1)
            if g is not None and not isinstance(g, str):
                if k == 4 and not tail(g):
                    pe_a(pe, g, par_, 0)
                if k == 5 and not tail(g):
                    pe_a(pe, g, par_, 1)
                    pe_b(pe, g, par_, 0)

        def tail(g):
            return isinstance(g, int) and g == SSM_GROUPS

        def act_conv(act, g, par_, k, it, ph, ku):
            wait_unit(act, ph, it, ku)
            dst = conv_dst(par_, k)
            if k >= 2:
                wait(act, S["pe_a"], 4 * g)
                wait(act, S["y_skip"], g)
            wait(act, S["cv_d"], 4 * g + k - 1)
            ps = bank(ph, ku)
            act.activation(dst, ps[:], ACT.Identity, scale=pcd("ssm_w", 96 + 4 * g + k),
                           bias=pcd("ssm_b", 4 * g + k))
            act.activation(pads[:, k % 2, 3:], ps[:], ACT.Copy).then_inc(S["cv_a"], 1)
            act.drain().then_inc(freed(ph, ku), 1)

        def conv_dst(par_, k):
            return bc[:, par_, k, :] if k < 2 else xs[:, k - 2, :]

        def act_silu(act, g, par_, k):
            act.wait_ge(S["cv_d"], 4 * g + k + 1)
            act.activation(conv_dst(par_, k), conv_dst(par_, k), ACT.Silu).then_inc(S["cv_s"], 1)

        def act_slot(act, k, g, par_, prev, it, ph, ku, here):
            if 1 <= k <= 3 and here:
                act_silu(act, g, par_, k - 1)
            if k == 4:
                if here:
                    act_silu(act, g, par_, 3)
                if prev:
                    act.wait_ge(S["f_y"], g)
                    act.activation(zs[:], ys[:, 1 - par_, :, :], ACT.Square).then_inc(S["f_sq"], 1)
            if k == 5:
                if prev:
                    act.wait_ge(S["f_ms"], g)
                    act.activation(srs[:], srs[:], ACT.Ln)
                    act.drain()
                    act.activation(srs[:], srs[:], ACT.Exp, scale=-0.5).then_inc(S["f_rs"], 1)
                    act.wait_ge(S["f_n"], g)
                    act.activation(vhi[:, bass.ds(2 * g - 2, 2), :], ys[:, 1 - par_, :, :],
                                   ACT.Copy).then_inc(S["f_hi"], 1)
            if here:
                if k < 4:
                    act_conv(act, g, par_, k, it, ph, ku)
                else:
                    wait_unit(act, ph, it, ku)
                    wait(act, S["f_pe"], g)
                    act.activation(zs[:, k - 4, :], bank(ph, ku)[:], ACT.Silu).then_inc(S["z_s"], 1)
                    act.drain().then_inc(freed(ph, ku), 1)
                    if k == 4:
                        act.wait_ge(S["e_seg"], 4 * g + 4)
                        act.activation(es[:], es[:], ACT.Exp).then_inc(S["e_exp"], 1)

        def dve_taps(dve, g, par_, k):
            dve.wait_ge(S["cv_a"], 4 * g + k + 1)
            dst = conv_dst(par_, k)
            for tap in range(3):
                last = dve.scalar_tensor_tensor(dst, pads[:, k % 2, tap:tap + T], pcd("ssm_w", 32 * tap + 4 * g + k),
                                                dst, ALU.mult, ALU.add)
                if tap < 2:
                    dve.drain()
            last.then_inc(S["cv_d"], 1)

        def per_head(t, c, g):
            return t[:, c, bass.ds(4 * g, 4)].unsqueeze(2).to_broadcast([P, 4, 64])

        def dve_a(dve, g, c):
            dve.wait_ge(S["pe_a"], 4 * g + c + 1)
            wait(dve, S["pe_b"], 4 * g + c - 1)
            b = psum[4 + c % 2]
            x4 = b[:, 0:256].rearrange("p (h f) -> p h f", h=4)
            dve.tensor_tensor(xdt[:, c % 2, :].rearrange("p (h f) -> p h f", h=4), x4, per_head(dtT, c, g), ALU.mult)
            if c < NCH - 1:
                dve.tensor_tensor(xend[:, c % 2, :].rearrange("p (h f) -> p h f", h=4), x4, per_head(endT, c, g),
                                  ALU.mult)
                dve.tensor_copy(bT[:, c % 2, :], b[:, 256:384])
            dve.wait_ge(S["e_exp"], g + 1)
            dve.tensor_tensor(es[:, c, :, :], es[:, c, :, :],
                              b[:, 384:512].unsqueeze(1).to_broadcast([P, 4, CH]), ALU.mult)
            dve.drain().then_inc(S["m_rdy"], 1)

        def dve_b(dve, g, par_, c):
            dve.wait_ge(S["pe_b"], 4 * g + c + 1)
            s = slice(c * CH, (c + 1) * CH)
            y = ys[:, par_, :, s]
            if c > 0:
                dve.wait_ge(S["eac_ld"], 64 * g + 64)
                dve.tensor_tensor(ty[:], psum[6][:, 256:512].rearrange("p (q t) -> p q t", q=2), eac[:, :, s], ALU.mult)
                dve.drain()
                dve.tensor_tensor(y, y, ty[:], ALU.add)
                dve.drain()
            dve.tensor_tensor(y, y, psum[6][:, 0:256].rearrange("p (q t) -> p q t", q=2), ALU.add)
            if c == 0:
                dve.tensor_copy(st[:], psum[7][:, 0:256])
            elif c < NCH - 1:
                s4 = st[:].rearrange("p (h f) -> p h f", h=4)
                dve.tensor_tensor(s4, s4, per_head(decT, c, g), ALU.mult)
                dve.drain()
                dve.tensor_tensor(st[:], st[:], psum[7][:, 0:256], ALU.add)
            dve.drain().then_inc(S["b_dve"], 1)

        def dve_slot(dve, k, g, par_, prev, here):
            if prev:
                q = 1 - par_
                if k == 0:
                    dve_a(dve, g - 1, 1)
                    dve_b(dve, g - 1, q, 0)
                if k == 1:
                    dve_a(dve, g - 1, 2)
                    dve_b(dve, g - 1, q, 1)
                if k == 2:
                    dve_a(dve, g - 1, 3)
                    dve_b(dve, g - 1, q, 2)
                if k == 3:
                    dve_b(dve, g - 1, q, 3)
                    dve.wait_ge(S["z_s"], 2 * g)
                    dve.tensor_tensor(ys[:, q, :, :], ys[:, q, :, :], zs[:], ALU.mult).then_inc(S["f_y"], 1)
            if here and k < 4:
                dve_taps(dve, g, par_, k)
            if k == 5:
                if prev:
                    q_ = 1 - par_
                    dve.wait_ge(S["f_pe"], g)
                    dve.tensor_scalar(srs[:], psum[6][:], 1.0 / 256, EPS, ALU.mult, ALU.add).then_inc(S["f_ms"], 1)
                    dve.wait_ge(S["f_rs"], g)
                    for q in range(2):
                        dve.scalar_tensor_tensor(ys[:, q_, q, :], ys[:, q_, q, :], pcd("ssm_norm", 2 * g - 2 + q),
                                                 srs[:], ALU.mult, ALU.mult)
                    dve.drain().then_inc(S["f_n"], 1)
                if here:
                    dve.wait_ge(S["cv_s"], 4 * g + 4)
                    for q in range(2):
                        last = dve.tensor_scalar(ys[:, par_, q, :], xs[:, q, :], pcd("d_skip", 2 * g + q), None, ALU.mult)
                    last.then_inc(S["y_skip"], 1)
                    dve.drain()
                    dve_a(dve, g, 0)
                if prev:
                    at = bass.ds(2 * g - 2, 2)
                    dve.wait_ge(S["f_hi"], g)
                    dve.tensor_tensor(vlo[:, at, :], ys[:, q_, :, :], vhi[:, at, :].bitcast(f32),
                                      ALU.subtract).then_inc(S["f_fin"], 1)
                    dve.drain()

        def pool_group(pool, g):
            first = isinstance(g, int) and g == 0
            for c in range(NCH):
                wait(pool, S["pe_b"], 4 * g - 4 + c + 1)
                pool.dma_start(es[:, c, :, :],
                               scratch[0, bass.ds(4 * g, 4), c * CH:(c + 1) * CH].partition_broadcast(P)
                               ).then_inc(S[f"e_ld{c}"], 16)
            wait(pool, S["b_dve"], 4 * g)
            for hh in range(2):
                for q in range(2):
                    pool.dma_start(eac[64 * hh:64 * hh + 64, q, :],
                                   scratch[1, bass.ds(4 * g + 2 * q + hh, 1), :].rearrange("a t -> (a t)").partition_broadcast(64)
                                   ).then_inc(S["eac_ld"], 16)
            for c in range(NCH):
                pool.wait_ge(S[f"e_ld{c}"], 16 * g + 16)
                pool.tensor_tensor(es[:, c, :, :], es[:, c, :, :],
                                   causal_add.unsqueeze(1).to_broadcast([P, 4, CH]), ALU.add)
                pool.drain()
                pool.tensor_tensor(es[:, c, :, :], es[:, c, :, :],
                                   acT[:, c, bass.ds(4 * g, 4)].unsqueeze(2).to_broadcast([P, 4, CH]),
                                   ALU.subtract).then_inc(S["e_seg"], 1)

        norm_b = Norm(1, 1, lambda j: xr[:, j, :], T, lambda j: g1s[:, 8 + j:9 + j], lambda j: mod[:, 24 + j:25 + j],
                      u_h, u_l, psum[6])
        norm_f1 = Norm(2, 2, lambda j: xr[:, j, :], T, lambda j: pc("final_norm", j), None, None, None, psum[6])

        N2 = {n: sem(n) for n in ("x2_ld", "cc_a", "cc_x", "cc_y", "cc_h", "cc_l", "cg_a", "co_d", "mh", "ml", "wo_d", "ada_ld0", "ada_ld1", "ada_ld2", "ada_ld3", "ada_used", "ada_read", "ada_mod", "r_a", "r_q", "r_h", "r_l", "dn_d", "out_st")}

        norm_g = Norm(3, 2, lambda j: xr[:, j, :], T, lambda j: g1s[:, 24 + j:25 + j], lambda j: mod[:, 48 + j:49 + j],
                      u_h, u_l, psum[6])
        norm_c = Norm(4, 3, lambda j: xc[:, j, :], TC, lambda j: g1s[:, 16 + j:17 + j], lambda j: mod[:, 96 + j:97 + j],
                      lambda j: uch[:, j, :], lambda j: ucl[:, j, :], psum[7])
        norm_m = Norm(5, 4, lambda j: xr[:, j, :], T, lambda j: g1s[:, 32 + j:33 + j], lambda j: mod[:, 72 + j:73 + j],
                      u_h, u_l, psum[6])
        norm_f2 = Norm(6, 5, lambda j: xr[:, j, :], T, lambda j: pc("final_2", j), None, None, None, psum[6])
        G = {n: sem(n) for n in ("xc_ld", "gcon_ld", "wa1_ld", "wa1_h", "wa1_l", "az_d", "az_a", "g_k", "v_a", "v_t", "v_d", "wa2_ld", "z_d", "exq", "za", "zl", "zb", "ex", "kd", "ktp", "ktc", "att_p", "att_d", "o_p", "st_p", "st_d", "o_sq", "o_sum", "o_ms", "o_rs", "o_n", "o_hi", "o_lo", "am0", "go_d")}
        mask = [gcon[:, GCOL[f"mask_{x}"]:GCOL[f"mask_{x}"] + P].bitcast(i32) for x in "fb"]
        reset = [gcon[:, GCOL[f"reset_{x}"]:GCOL[f"reset_{x}"] + TA] for x in "fb"]

        def prep_banks(h, d):
            return [psum[b] for b in (((4, 5), (6, 7))[d] if h == 0 else (2, 3))]

        def v_h(k):
            return vhi[:, k, :]

        def v_l(k):
            return vlo[:, k, :]

        def ada_load(pool, laps, src, col0, ks, steps):
            def step(it):
                for n, k in enumerate(ks):
                    wait(pool, N2["ada_used"], it * len(ks) + (laps - 1) * ARING + n + 1)
                    pool.dma_start(aring[:, n % ARING, :], src[k * P:(k + 1) * P, bass.ds(it * 512 + col0, 512)]
                                   ).then_inc(N2[f"ada_ld{n % ARING}"], 16)
            run(pool, steps, step, peel_first=laps == 0)

        def ada_piece(dve, laps, it, ks, n, accs):
            k, per = ks[n], len(ks) // ARING
            dve.wait_ge(N2[f"ada_ld{n % ARING}"], it * (16 * per) + (laps + n // ARING + 1) * 16)
            for ccol, acc0 in accs:
                acc = aacc[:, bass.ds(it * 512 + acc0, 512)]
                w, c = aring[:, n % ARING, :], c_act[:, ccol + k:ccol + k + 1]
                if k == 0:
                    last = dve.tensor_scalar(acc, w, c, None, ALU.mult)
                else:
                    last = dve.scalar_tensor_tensor(acc, w, c, acc, ALU.mult, ALU.add)
            last.then_inc(N2["ada_used"], 1)
            dve.drain()

        def ada_pe(pe, n):
            pe.wait_ge(N2["ada_used"], ADA_PIECES[n - 1])
            wait(pe, N2["ada_mod"], n - 1)
            for j in range(32):
                mm = pe.matmul(psum[7][:, 256 + j:257 + j], aacc[:, j * P:(j + 1) * P], ones[:, 0:1], start=True, stop=True)
            mm.then_inc(N2["ada_read"], 1)

        def ada_dve(dve, n, parts):
            dve.wait_ge(N2["ada_read"], n)
            for dst, src, count, bias in parts:
                dve.tensor_tensor(mod[:, dst:dst + count], psum[7][:, 256 + src:256 + src + count],
                                  par[:, bias:bias + count], ALU.add)
            dve.drain().then_inc(N2["ada_mod"], 1)

        def mlp_up_act(act, ph, done):
            def step(it):
                for k in range(4):
                    split_hi(act, ph, it, k)
                    wait_unit(act, ph, it, k)
                    wait(act, N2["r_q"], it * 4 + done + k - 1)
                    act.activation(r1[:, k % 2, :], bank(ph, k)[:], ACT.Relu).then_inc(N2["r_a"], 1)
                    act.drain().then_inc(freed(ph, k), 1)
                    act.activation(vhi[:, bass.ds(it * 4 + k, 1), :].rearrange("p a t -> p (a t)"), r1[:, k % 2, :],
                                   ACT.Square).then_inc(N2["r_h"], 1)
            run(act, 4, step, peel_first=done == 0)

        def mlp_up_dve(dve, ph, done, beside=lambda it, k: None):
            def step(it):
                for k in range(4):
                    split_lo(dve, ph, it, k)
                    dve.wait_ge(N2["r_a"], it * 4 + done + k + 1)
                    dve.tensor_tensor(hq[:], r1[:, k % 2, :], r1[:, k % 2, :], ALU.mult).then_inc(N2["r_q"], 1)
                    dve.drain()
                    dve.wait_ge(N2["r_h"], it * 4 + done + k + 1)
                    at = bass.ds(it * 4 + k, 1)
                    dve.tensor_tensor(vlo[:, at, :].rearrange("p a t -> p (a t)"), hq[:],
                                      vhi[:, at, :].rearrange("p a t -> p (a t)").bitcast(f32),
                                      ALU.subtract).then_inc(N2["r_l"], 1)
                    dve.drain()
                    beside(it, k)
            run(dve, 4, step)

        def mlp_down_pe(pe, ph, done, peel_last=False):
            def step(it):
                for k in range(4):
                    half = k % 2
                    pe.wait_ge(N2["r_l"], done + 8 + 8 * half)
                    pe_unit(pe, ph, it, k, lambda t: v_h(t + 8 * half), lambda t: v_l(t + 8 * half), out_i=k // 2,
                            first=half == 0, last=half == 1)
            run(pe, 4, step, peel_last)

        def mlp_down_dve(dve, ph, half_b, gate, peel_last=False, beside=lambda it, k: None):
            def step(it):
                for k in range(4):
                    split_lo(dve, ph, it, k)
                    beside(it, k)
                    if k % 2 == 0:
                        continue
                    o = k // 2
                    at = bass.ds(it * 2 + o, 1)
                    m = mg[:, at, :].rearrange("p a t -> p (a t)")
                    wait_unit(dve, ph, it, k)
                    if not half_b:
                        dve.tensor_copy(m, bank(ph, o)[:])
                        dve.drain().then_inc(freed(ph, o), 1)
                    else:
                        x = xr[:, at, :].rearrange("p a t -> p (a t)")
                        dve.tensor_tensor(m, m, bank(ph, o)[:], ALU.add)
                        dve.drain().then_inc(freed(ph, o), 1)
                        dve.scalar_tensor_tensor(x, m, mod[:, bass.ds(it * 2 + gate + o, 1)], x, ALU.mult, ALU.add)
                        dve.drain().then_inc(N2["dn_d"], 1)
            run(dve, 4, step, peel_last)

        def only_hi(act, ph, peel_last=False):
            p = PH[ph]

            def step(it):
                for k in range(p["n"]):
                    split_hi(act, ph, it, k)
            run(act, p["steps"], step, peel_last)

        def chunk_of(d, i):
            if d == 0:
                return i
            return 3 - i if i < 4 else 15 - i

        def gate_pe(pe, h, d):
            n = 2 * h + d
            pe.wait_ge(G["wa2_ld"], h * 32 + 32)
            if h > 0:
                pe.wait_ge(G["ktc"], n)
            b4, b5 = prep_banks(h, d)
            w, a = wa2c[32 * d:32 * d + 16, :], az[32 * d:32 * d + 16, :]
            pe.matmul(b4[:], w, a[:, TC:], start=True, stop=True)
            pe.matmul(b5[:, :TC], w, a[:, :TC], start=True, stop=True).then_inc(G["z_d"], 1)

        def gate_act(act, h, d):
            n = 2 * h + d
            b4, b5 = prep_banks(h, d)
            bias = pc("b_a", h + 4 * d)
            act.wait_ge(G["z_d"], n + 1)
            wait(act, G["ktp"], n)
            for func, dst in ((ACT.Abs, ez), (ACT.Identity, zz)):
                act.activation(dst[:, TC:], b4[:], func, bias=bias)
                act.activation(dst[:, :TC], b5[:, :TC], func, bias=bias)
            act.drain()
            act.activation(ez[:], ez[:], ACT.Exp, scale=-1.0)
            act.drain()
            act.activation(ez[:], ez[:], ACT.Ln, bias=1.0).then_inc(G["za"], 1)

        def logs_dve(dve, h, d):
            dve.wait_ge(G["za"], 2 * h + d + 1)
            dve.scalar_tensor_tensor(ez[:], zz[:], 0.0, ez[:], ALU.min, ALU.subtract)
            dve.drain()
            way = 1 if d == 0 else -1
            dve.tensor_tensor_scan(zz[:, ::way], reset[d][:, ::way], ez[:, ::way], 0.0, ALU.mult, ALU.add)
            dve.drain()
            z3 = zz[:].rearrange("p (c t) -> p c t", t=GC)
            edge = GC - 1 if d == 0 else 0
            dve.tensor_copy(glb[:, d, :], z3[:, :, edge])
            dve.tensor_tensor(ez[:].rearrange("p (c t) -> p c t", t=GC), z3,
                              z3[:, :, edge:edge + 1].to_broadcast([P, 12, GC]), ALU.subtract)
            dve.drain().then_inc(G["zb"], 1)

        def decay_act(act, h, d):
            act.wait_ge(G["zb"], 2 * h + d + 1)
            act.activation(ez[:], ez[:], ACT.Exp, scale=-1.0 / TAU).then_inc(G["ex"], 1)
            act.activation(gld[:, h % 2, d, :], glb[:, d, :], ACT.Exp, scale=1.0 / TAU)
            act.activation(qd[h % 2][:, d, :], zz[:, TC:], ACT.Exp, scale=1.0 / TAU)
            act.activation(ki[h % 2][:, d, :], zz[:, TC:], ACT.Exp, scale=-1.0 / TAU)
            act.drain().then_inc(G["exq"], 1)

        def keys_dve(dve, h, d):
            dve.wait_ge(G["ex"], 2 * h + d + 1)
            dve.tensor_tensor(ez[:], ez[:], kf[:, h, :], ALU.mult).then_inc(G["kd"], 1)
            dve.wait_ge(G["exq"], 2 * h + d + 1)
            q, k = qd[h % 2][:, d, :], ki[h % 2][:, d, :]
            dve.tensor_tensor(q, q, qf[:, h, :], ALU.mult)
            dve.tensor_tensor(k, k, kf[:, h, TC:], ALU.mult)
            dve.drain().then_inc(G["zl"], 1)

        def keys_pe(pe, h, d):
            pe.wait_ge(G["kd"], 2 * h + d + 1)
            for i in range(TA // P):
                b = prep_banks(h, d)[i // 4]
                mm = pe.transpose(b[:, (i % 4) * P:(i % 4 + 1) * P], ez[:, i * P:(i + 1) * P], ident)
            mm.then_inc(G["ktp"], 1)

        def keys_act(act, h, d):
            b4, b5 = prep_banks(h, d)
            act.wait_ge(G["ktp"], 2 * h + d + 1)
            act.activation(kdT[h % 2][:, d, 0:4, :], b4[:].rearrange("p (i k) -> p i k", i=4), ACT.Copy)
            act.activation(kdT[h % 2][:, d, 4:6, :], b5[:, :TC].rearrange("p (i k) -> p i k", i=2), ACT.Copy)
            act.drain().then_inc(G["ktc"], 1)

        def head_values(h, i, v0=0, v1=GV):
            return vt[:, i, h * GV + v0:h * GV + v1]

        def att_pe(pe, h):
            def scores(p):
                s = slice(p * P, (p + 1) * P)
                wait(pe, G["att_d"], h * 4 + p - 1)
                for d in range(2):
                    mm = pe.matmul(psum[p % 2][:, d * P:(d + 1) * P], ki[h % 2][:, d, s], qd[h % 2][:, d, s],
                                   start=True, stop=True)
                mm.then_inc(G["att_p"], 1)
            wait(pe, G["o_ms"], h)
            pe.wait_ge(G["zl"], h * 2 + 2)
            scores(0)
            wait(pe, G["o_n"], h)
            for p in range(4):
                if p < 3:
                    scores(p + 1)
                pe.wait_ge(G["att_d"], h * 4 + p + 1)
                s = slice(p * P, (p + 1) * P)
                for v in range(2):
                    mm = pe.matmul(psum[6 + v][:, s], head_values(h, 2 + p, v * P, v * P + P), atts[:, p % 2, :],
                                   start=p == 0, stop=False, skip_group_check=True)
                mm.then_inc(G["o_p"], 1)

        def att_dve(dve, h, p):
            dve.wait_ge(G["att_p"], h * 4 + p + 1)
            wait(dve, G["o_p"], h * 4 + p - 1)
            dve.tensor_copy(tick[:], con[:, 0:1])
            for d in range(2):
                dve.copy_predicated(am[:, d, :], mask[d], psum[p % 2][:, d * P:(d + 1) * P])
            dve.drain()
            dve.tensor_tensor(atts[:, p % 2, :], am[:, 0, :], am[:, 1, :], ALU.add).then_inc(G["att_d"], 1)
            dve.drain()

        def states_pe(pe, h, first, last):
            for s in range(first, last):
                i, d = s // 2, s % 2
                c = chunk_of(d, i)
                wait(pe, G["st_d"], h * 22 + s - 1)
                if i == 0:
                    pe.wait_ge(G["ktc"], h * 2 + 2)
                if i >= 4:
                    t = slice((c - 4) * GC, (c - 3) * GC)
                    for v in range(2):
                        mm = pe.matmul(psum[6 + v][:, t], gst[:, d, v * P:(v + 1) * P], qd[h % 2][:, d, t], start=False,
                                       stop=s == 23, skip_group_check=True)
                if i < 11:
                    r = slice((c % 2) * GC, (c % 2 + 1) * GC)
                    mm = pe.matmul(psum[4 + d][:, 0:GV], kdT[h % 2][r, d, c // 2, :], head_values(h, c // 2)[r, :],
                                   start=True, stop=True)
                mm.then_inc(G["st_p"], 1)

        def states_dve(dve, h, first, last):
            for s in range(first, last):
                i, d = s // 2, s % 2
                c = chunk_of(d, i)
                dve.wait_ge(G["st_p"], h * 24 + s + 1)
                if i == 0:
                    dve.tensor_copy(gst[:, d, :], psum[4 + d][:, 0:GV]).then_inc(G["st_d"], 1)
                else:
                    dve.scalar_tensor_tensor(gst[:, d, :], gst[:, d, :], gld[:, h % 2, d, c:c + 1], psum[4 + d][:, 0:GV],
                                             ALU.mult, ALU.add).then_inc(G["st_d"], 1)
                dve.drain()

        def out_act(act, h):
            act.wait_ge(G["st_p"], h * 24 + 24)
            for v in range(2):
                act.activation(nsq[:, v, :], psum[6 + v][:], ACT.Square)
            act.drain().then_inc(G["o_sq"], 1)
            act.wait_ge(G["o_ms"], h + 1)
            act.activation(nrs[:], nrs[:], ACT.Ln)
            act.drain()
            act.activation(nrs[:], nrs[:], ACT.Exp, scale=-0.5).then_inc(G["o_rs"], 1)

        def out_hi_act(act, h):
            act.wait_ge(G["o_n"], h + 1)
            act.activation(uhi[:, 2 * h:2 * h + 2, :], nt[:], ACT.Copy).then_inc(G["o_hi"], 1)

        def out_pe(pe, h):
            pe.wait_ge(G["o_sq"], h + 1)
            pe.wait_ge(G["att_d"], h * 4 + 4)
            for v in range(2):
                mm = pe.matmul(psum[0][:], ones, nsq[:, v, :], start=v == 0, stop=v == 1)
            mm.then_inc(G["o_sum"], 1)

        def out_mean_dve(dve, h):
            dve.wait_ge(G["o_sum"], h + 1)
            dve.tensor_scalar(nrs[:], psum[0][:], 1.0 / GV, EPS, ALU.mult, ALU.add).then_inc(G["o_ms"], 1)

        def out_gated_dve(dve, h):
            dve.wait_ge(G["o_rs"], h + 1)
            for v in range(2):
                dve.scalar_tensor_tensor(nt[:, v, :], psum[6 + v][:], pc("g_head", h * 2 + v), nrs[:], ALU.mult, ALU.mult)
            dve.drain()
            dve.tensor_tensor(nt[:], nt[:], rf[:, 2 * h:2 * h + 2, :], ALU.mult)
            dve.drain().then_inc(G["o_n"], 1)

        def out_lo_dve(dve, h):
            at = slice(2 * h, 2 * h + 2)
            dve.wait_ge(G["o_hi"], h + 1)
            dve.tensor_tensor(ulo[:, at, :], nt[:], uhi[:, at, :].bitcast(f32), ALU.subtract)
            dve.drain().then_inc(G["o_lo"], 1)

        def head_pe(pe, h):
            more = h + 1 < NGLA
            states_pe(pe, h, 0, 4)
            if h > 0:
                out_pe(pe, h - 1)
            if more:
                gate_pe(pe, h + 1, 0)
            states_pe(pe, h, 4, 8)
            att_pe(pe, h)
            states_pe(pe, h, 8, 14)
            if more:
                keys_pe(pe, h + 1, 0)
                gate_pe(pe, h + 1, 1)
            states_pe(pe, h, 14, 24)
            if more:
                keys_pe(pe, h + 1, 1)

        def head_act(act, h):
            more = h + 1 < NGLA
            if h > 0:
                out_act(act, h - 1)
            if more:
                gate_act(act, h + 1, 0)
            if h > 0:
                out_hi_act(act, h - 1)
            if more:
                decay_act(act, h + 1, 0)
                keys_act(act, h + 1, 0)
                gate_act(act, h + 1, 1)
                decay_act(act, h + 1, 1)
                keys_act(act, h + 1, 1)

        def head_dve(dve, h):
            more = h + 1 < NGLA
            states_dve(dve, h, 0, 4)
            if h > 0:
                out_mean_dve(dve, h - 1)
            states_dve(dve, h, 4, 8)
            if h > 0:
                out_gated_dve(dve, h - 1)
            if more:
                logs_dve(dve, h + 1, 0)
            for p in range(4):
                att_dve(dve, h, p)
            if h > 0:
                out_lo_dve(dve, h - 1)
            if more:
                keys_dve(dve, h + 1, 0)
            states_dve(dve, h, 8, 16)
            if more:
                logs_dve(dve, h + 1, 1)
            states_dve(dve, h, 16, 22)
            if more:
                keys_dve(dve, h + 1, 1)

        def both(pe, ph, k):
            p = PH[ph]
            b, s = p["banks"][k], (p["u0"] + k) % SLOTS
            pe.wait_ge(w_split, p["u0"] + k + 1)
            pe.wait_ge(bank_free[b], p["used"][b] + p["banks"][:k].count(b))
            split_products(pe, psum[b][:], whi[:, s, :], wlo[:, s, :], u_h, u_l, True, True)
            split_products(pe, psum[4 + k % 2][:, :TC], whi[:, s, :], wlo[:, s, :], lambda t: uch[:, t, :],
                           lambda t: ucl[:, t, :], True, True).then_inc(unit_done, 1)

        block = ctx.enter_context(nc.Block())

        @block.sync
        def _(sp):
            sp.dma_start(par[:], params).then_inc(in_ld, 16)
            sp.dma_start(con[:], consts).then_inc(in_ld, 16)
            for j in range(2):
                sp.dma_start(x0[:, 4 * j:4 * j + 4, :],
                             xT[512 * j:512 * j + 512, :].rearrange("(k p) t -> p k t", p=P)).then_inc(x_ld, 16)
            for j in range(8):
                sp.dma_start(slab[:, j, :, :],
                             ada1[:, 256 * j:256 * j + 256].rearrange("(k p) n -> p k n", p=P)).then_inc(slab_ld[j], 16)
            for s in range(RAW):
                sp.dma_start(wraw[:, s, :], units[s]).then_inc(w_loaded[s], 16)
            sp.wait_ge(S["mod_ps"], 1)
            sp.dma_start(dw[:], w_dt).then_inc(S["dw_ld"], 16)
            with sp.Fori(1, UNITS // RAW) as i:
                for s in range(RAW):
                    sp.wait_ge(w_split, i * RAW + s - RAW + 1)
                    sp.dma_start(wraw[:, s, :], units[bass.ds(i * RAW + s, 1)].rearrange("a p n -> (a p) n")
                                 ).then_inc(w_loaded[s], 16)
            for j in range(2):
                norm_f2.ready(sp, 4 * j + 4)
                sp.dma_start(outT[512 * j:512 * j + 512, :].rearrange("(k p) t -> p k t", p=P),
                             xr[:, 4 * j:4 * j + 4, :]).then_inc(N2["out_st"], 16)
            sp.wait_ge(N2["out_st"], 32)

        @block.gpsimd
        def _(pool):
            pool.memset(pads[:, :, 0:3], 0.0).then_inc(S["pad0"], 1)
            pool.wait_ge(S["scr_st"], 32)
            pool.wait_ge(S["dt_done"], 1)
            pool_group(pool, 0)
            with pool.Fori(1, SSM_GROUPS) as g:
                pool_group(pool, g)
            pool.wait_ge(S["f_fin"], SSM_GROUPS)
            k8 = list(range(KT))
            ada_load(pool, 0, ada1, 2048, k8, 8)
            norm_b.ready(pool, 8)
            ada_load(pool, 16, ada2, 0, k8[:4], 4)
            ada_load(pool, 20, ada2, 0, k8[4:], 4)
            ada_load(pool, 24, ada2, 2048, k8, 8)
            pool.wait_ge(N2["ada_read"], 3)
            pool.wait_ge(G["az_a"], 1)
            pool.memset(am[:], 0.0).then_inc(G["am0"], 1)

            def gates(h):
                wait(pool, G["z_d"], h * 2)
                for d in range(2):
                    pool.dma_start(wa2c[32 * d:32 * d + 16, :], w_a2[d, :, bass.ds(h * P, P)]).then_inc(G["wa2_ld"], 16)
            run(pool, NGLA, gates, peel_first=True)

        @block.scalar
        def _(act):
            act.wait_ge(in_ld, 32)
            act.activation(c_act[:], par[:, PCOL["c"]:PCOL["c"] + 24], ACT.Silu).then_inc(S["cact"], 1)
            for u in range(AHEAD - 1):
                hi_part(act, u, 0)
            norm_a.act(act, lambda e, j: e.wait_ge(x_ld, 32) if j == 0 else None)
            act.wait_ge(S["dw_ld"], 16)
            act.activation(dwh[:], dw[:], ACT.Copy).then_inc(S["dw_hi"], 1)
            act.activation(nega[:], pc("a_log"), ACT.Exp).then_inc(S["dt_nega"], 1)
            hi_part(act, AHEAD - 1, 0)
            act.wait_ge(S["dt_ps"], 1)
            act.activation(dx[:], psum[4][:], ACT.Identity, bias=pc("dt_bias"))
            act.drain()
            act.activation(de[:], dx[:], ACT.Abs)
            act.drain()
            act.activation(de[:], de[:], ACT.Exp, scale=-1.0).then_inc(S["dt_e"], 1)
            act.wait_ge(S["dt_w"], 1)
            act.activation(dl[:], dd[:], ACT.Ln).then_inc(S["dt_ln"], 1)
            act.wait_ge(S["dt_ac"], 1)
            act.dma_start(scratch[0], dac[0:HEADS, :]).then_inc(S["scr_st"], 16)
            act.activation(dea[:], dac[:], ACT.Exp).then_inc(S["dt_ea"], 1)
            act.wait_ge(S["dt_ea"], 1)
            act.dma_start(scratch[1], dea[0:HEADS, :]).then_inc(S["scr_st"], 16)
            act.wait_ge(S["dt_tp"], 1)
            tp = psum[5][:].rearrange("p (a c h) -> p a c h", a=4, c=NCH)
            act.activation(dtT[:], tp[:, 0, :, :], ACT.Copy)
            act.activation(acT[:], tp[:, 1, :, :], ACT.Copy)
            act.drain().then_inc(S["dt_tok"], 1)
            act.wait_ge(S["dt_last"], 1)
            act.activation(decT[:], psum[4][:, 0:128].rearrange("p (c h) -> p c h", c=NCH), ACT.Exp
                           ).then_inc(S["dt_dec"], 1)
            act.wait_ge(S["dt_lastd"], 1)
            act.activation(endT[:], endT[:], ACT.Exp)
            act.drain().then_inc(S["dt_lastd"], 1)
            act.wait_ge(S["pad0"], 1)

            def ssm(it, ph, k0, g, par_, prev):
                for k in range(6):
                    split_hi(act, ph, it, k0 + k)
                    act_slot(act, k, g, par_, prev, it, ph, k0 + k, True)

            def ssm2(it):
                ssm(it, "ssm", 0, it * 2 + 1, 1, True)
                ssm(it, "ssm", 6, it * 2 + 2, 0, True)

            ssm(0, "ssm0", 0, 0, 0, False)
            run(act, 3, ssm2)
            ssm(0, "ssm7", 0, 7, 1, True)
            for k in range(8):
                split_hi(act, "gate_ssm", 0, k)
                if k < 6:
                    act_slot(act, k, 8, 0, True, 0, "gate_ssm", k, False)
                wait_unit(act, "gate_ssm", 0, k)
                act.activation(mg[:, k, :], bank("gate_ssm", k)[:], ACT.Sigmoid)
                act.drain().then_inc(freed("gate_ssm", k), 1)
            act.wait_ge(S["f_fin"], SSM_GROUPS)
            act.dma_start(xr[:], xT.rearrange("(k p) t -> p k t", p=P)).then_inc(N2["x2_ld"], 16)
            only_hi(act, "ssm_out")

            def conv(it):
                for k in range(4):
                    split_hi(act, "conv", it, k)
                    wait_unit(act, "conv", it, k)
                    if k == 0:
                        wait(act, N2["cc_x"], it)
                        act.activation(ccs[:], bank("conv", 0)[:], ACT.Copy).then_inc(N2["cc_a"], 1)
                        act.drain().then_inc(freed("conv", 0), 1)
                    if k == 3:
                        at = bass.ds(it, 1)
                        act.activation(sgs[:, at, :].rearrange("p a t -> p (a t)"), bank("conv", 3)[:], ACT.Sigmoid)
                        act.drain().then_inc(freed("conv", 3), 1)
                        act.wait_ge(N2["cc_y"], it + 1)
                        act.activation(vhi[:, at, :].rearrange("p a t -> p (a t)"), cy[:], ACT.Copy).then_inc(N2["cc_h"], 1)
            conv(0)
            with act.Fori(1, 8) as it:
                conv(it)
            act.drain().then_inc(N2["cg_a"], 1)

            def conv_out(it):
                for k in range(4):
                    split_hi(act, "conv_out", it, k)
                    act.wait_ge(N2["co_d"], it * 4 + k + 1)
                    act.activation(uhi[:, bass.ds(it * 4 + k, 1), :], mg[:, bass.ds(it * 4 + k, 1), :],
                                   ACT.Copy).then_inc(N2["mh"], 1)
            run(act, 2, conv_out)
            only_hi(act, "w_o")
            act.wait_ge(N2["ada_used"], ADA_PIECES[0])
            norm_b.act(act, lambda e, j: e.wait_ge(N2["wo_d"], j + 1))
            mlp_up_act(act, "up1a", 0)
            only_hi(act, "down1a")
            mlp_up_act(act, "up1b", 16)
            only_hi(act, "down1b")
            act.wait_ge(N2["ada_used"], ADA_PIECES[2])
            norm_f1.act(act, lambda e, j: e.wait_ge(N2["dn_d"], j + 1))
            act.wait_ge(N2["ada_read"], 3)
            act.wait_ge(N2["dn_d"], 8)
            act.dma_start(xc[:], ctxT.rearrange("(k p) t -> p k t", p=P)).then_inc(G["xc_ld"], 16)
            act.dma_start(gcon[:], gconsts).then_inc(G["gcon_ld"], 16)
            act.dma_start(wa1[:], w_a1).then_inc(G["wa1_ld"], 16)
            norm_g.act(act, lambda e, j: norm_f1.ready(e, j + 1))
            norm_g.ready(act, 8)
            act.wait_ge(G["xc_ld"], 16)
            norm_c.act(act, lambda e, j: None)
            for k in range(4):
                split_hi(act, "gla_q", 0, k)
                wait_unit(act, "gla_q", 0, k)
                act.activation(qf[:, k, :], bank("gla_q", k)[:], ACT.Copy, scale=float(P) ** -0.5)
                act.drain().then_inc(freed("gla_q", k), 1)
            act.wait_ge(G["wa1_ld"], 16)
            act.activation(wa1h[:], wa1[:], ACT.Copy).then_inc(G["wa1_h"], 1)

            act.wait_ge(G["az_d"], 1)
            act.activation(az[:, TC:], psum[4][:], ACT.Copy)
            act.activation(az[:, :TC], psum[5][:, :TC], ACT.Copy)
            act.drain().then_inc(G["az_a"], 1)
            for k in range(4):
                split_hi(act, "gla_k", 0, k)
                wait_unit(act, "gla_k", 0, k)
                act.activation(kf[:, k, TC:], bank("gla_k", k)[:], ACT.Copy)
                act.activation(kf[:, k, :TC], psum[4 + k % 2][:, :TC], ACT.Copy).then_inc(G["g_k"], 1)
                act.drain().then_inc(freed("gla_k", k), 1)
            for k in range(8):
                split_hi(act, "gla_v", 0, k)
                wait_unit(act, "gla_v", 0, k)
                wait(act, G["v_t"], k - 1)
                act.activation(vf[:, k % 2, TC:], bank("gla_v", k)[:], ACT.Copy)
                act.activation(vf[:, k % 2, :TC], psum[4 + k % 2][:, :TC], ACT.Copy).then_inc(G["v_a"], 1)
                act.drain().then_inc(freed("gla_v", k), 1)
            act.wait_ge(G["v_t"], 8)
            for k in range(8):
                split_hi(act, "gla_r", 0, k)
                if k == 1:
                    gate_act(act, 0, 0)
                if k == 3:
                    decay_act(act, 0, 0)
                if k == 4:
                    keys_act(act, 0, 0)
                    gate_act(act, 0, 1)
                if k == 6:
                    decay_act(act, 0, 1)
                wait_unit(act, "gla_r", 0, k)
                act.activation(rf[:, k, :], bank("gla_r", k)[:], ACT.Silu)
                act.drain().then_inc(freed("gla_r", k), 1)
                if k == 7:
                    keys_act(act, 0, 1)
            for h in range(NGLA):
                head_act(act, h)
            out_act(act, NGLA - 1)
            out_hi_act(act, NGLA - 1)
            only_hi(act, "gla_o")
            norm_m.act(act, lambda e, j: e.wait_ge(G["go_d"], j + 1))
            mlp_up_act(act, "up2a", 32)
            only_hi(act, "down2a")
            mlp_up_act(act, "up2b", 48)
            only_hi(act, "down2b", peel_last=True)
            norm_f2.act(act, lambda e, j: e.wait_ge(N2["dn_d"], 8 + j + 1))

        @block.vector
        def _(dve):
            dve.wait_ge(in_ld, 32)
            dve.wait_ge(S["mod_ps"], 1)
            dve.tensor_tensor(mod[:, 0:16], psum[7][:, 256:272], par[:, PCOL["b_ada"]:PCOL["b_ada"] + 16], ALU.add)
            dve.drain()
            dve.scalar_tensor_tensor(g1s[:, 0:8], mod[:, 8:16], 1.0, par[:, PCOL["ln1"]:PCOL["ln1"] + 8],
                                     ALU.add, ALU.mult)
            dve.drain()
            for u in range(AHEAD - 1):
                lo_part(dve, u, 0)
            norm_a.dve(dve)
            dve.wait_ge(S["dw_hi"], 1)
            dve.tensor_tensor(dwl[:], dw[:], dwh[:].bitcast(f32), ALU.subtract).then_inc(S["dw_lo"], 1)
            lo_part(dve, AHEAD - 1, 0)
            dve.wait_ge(S["dt_e"], 1)
            dve.tensor_scalar(dd[:], de[:], 1.0, None, ALU.add).then_inc(S["dt_w"], 1)
            dve.drain()
            dve.reciprocal(dr[:], dd[:])
            dve.tensor_scalar(dac[:], dd[:], -1.0, None, ALU.add)
            dve.drain()
            dve.tensor_tensor(de[:], de[:], dac[:], ALU.subtract)
            dve.drain()
            dve.tensor_tensor(de[:], de[:], dr[:], ALU.mult)
            dve.wait_ge(S["dt_ln"], 1)
            dve.drain()
            dve.tensor_tensor(de[:], de[:], dl[:], ALU.add)
            dve.drain()
            dve.scalar_tensor_tensor(dd[:], dx[:], 0.0, de[:], ALU.max, ALU.add)
            dve.wait_ge(S["dt_nega"], 1)
            dve.drain()
            dve.tensor_scalar(dr[:], dd[:], nega[:], -1.0, ALU.mult, ALU.mult)
            dve.drain()
            dve.tensor_tensor_scan(dac[:], resets, dr[:], 0.0, ALU.mult, ALU.add).then_inc(S["dt_ac"], 1)
            dve.wait_ge(S["dt_dec"], 1)
            dve.tensor_tensor(endT[:], psum[4][:, 0:128].rearrange("p (c h) -> p c h", c=NCH), acT[:],
                              ALU.subtract).then_inc(S["dt_lastd"], 1)
            dve.wait_ge(S["dt_lastd"], 2)
            dve.tensor_tensor(endT[:], endT[:], dtT[:], ALU.mult).then_inc(S["dt_done"], 1)
            dve.drain()
            dve.wait_ge(S["pad0"], 1)

            def ssm(it, ph, k0, g, par_, prev):
                for k in range(6):
                    split_lo(dve, ph, it, k0 + k)
                    dve_slot(dve, k, g, par_, prev, True)

            def ssm2(it):
                ssm(it, "ssm", 0, it * 2 + 1, 1, True)
                ssm(it, "ssm", 6, it * 2 + 2, 0, True)

            ssm(0, "ssm0", 0, 0, 0, False)
            run(dve, 3, ssm2)
            ssm(0, "ssm7", 0, 7, 1, True)
            for k in range(8):
                split_lo(dve, "gate_ssm", 0, k)
                if k < 6:
                    dve_slot(dve, k, 8, 0, True, False)
            dve.memset(ccx[:, 0:2], 0.0)
            dve.drain()

            def ssm_out(it):
                for k in range(4):
                    split_lo(dve, "ssm_out", it, k)
                    if k % 2:
                        m = mg[:, bass.ds(it * 2 + k // 2, 1), :].rearrange("p a t -> p (a t)")
                        wait_unit(dve, "ssm_out", it, k)
                        dve.tensor_tensor(m, m, bank("ssm_out", k // 2)[:], ALU.mult)
                        dve.drain().then_inc(freed("ssm_out", k // 2), 1)
            run(dve, 4, ssm_out)

            k8 = list(range(KT))

            def conv(it):
                for k in range(4):
                    split_lo(dve, "conv", it, k)
                    for n in (2 * k, 2 * k + 1):
                        ada_piece(dve, 0, it, k8, n, [(0, 0)])
                    if k == 1:
                        dve.wait_ge(N2["cc_a"], it + 1)
                        wait_unit(dve, "conv", it, 1)
                        dve.tensor_tensor(ccx[:, 2:], ccs[:], bank("conv", 1)[:], ALU.mult).then_inc(N2["cc_x"], 1)
                        dve.drain().then_inc(freed("conv", 1), 1)
                        dve.tensor_scalar(ct[:], ccx[:, 2:], pcd("conv_w", it + 16), None, ALU.mult)
                        dve.drain()
                        for tap in range(2):
                            dve.scalar_tensor_tensor(ct[:], ccx[:, tap:tap + T], pcd("conv_w", it + 8 * tap), ct[:],
                                                     ALU.mult, ALU.add)
                            dve.drain()
                    if k == 2:
                        wait_unit(dve, "conv", it, 2)
                        wait(dve, N2["cc_h"], it)
                        dve.tensor_tensor(cy[:], ct[:], bank("conv", 2)[:], ALU.mult).then_inc(N2["cc_y"], 1)
                        dve.drain().then_inc(freed("conv", 2), 1)
                    if k == 3:
                        at = bass.ds(it, 1)
                        dve.wait_ge(N2["cc_h"], it + 1)
                        dve.tensor_tensor(vlo[:, at, :].rearrange("p a t -> p (a t)"), cy[:],
                                          vhi[:, at, :].rearrange("p a t -> p (a t)").bitcast(f32),
                                          ALU.subtract).then_inc(N2["cc_l"], 1)
                        dve.drain()
            conv(0)
            with dve.Fori(1, 8) as it:
                conv(it)
            dve.wait_ge(N2["cg_a"], 1)

            def conv_out(it):
                for k in range(4):
                    at = bass.ds(it * 4 + k, 1)
                    m = mg[:, at, :].rearrange("p a t -> p (a t)")
                    split_lo(dve, "conv_out", it, k)
                    wait_unit(dve, "conv_out", it, k)
                    dve.tensor_tensor(ct[:], sgs[:, at, :].rearrange("p a t -> p (a t)"), bank("conv_out", k)[:], ALU.mult)
                    dve.drain().then_inc(freed("conv_out", k), 1)
                    dve.tensor_tensor(m, m, ct[:], ALU.add).then_inc(N2["co_d"], 1)
                    dve.drain()
                    dve.wait_ge(N2["mh"], it * 4 + k + 1)
                    dve.tensor_tensor(ulo[:, at, :].rearrange("p a t -> p (a t)"), m,
                                      uhi[:, at, :].rearrange("p a t -> p (a t)").bitcast(f32),
                                      ALU.subtract).then_inc(N2["ml"], 1)
                    dve.drain()
            run(dve, 2, conv_out)
            b1 = PCOL["b_ada"]
            ada_dve(dve, 1, [(16, 0, 32, b1 + 16)])
            dve.scalar_tensor_tensor(g1s[:, 8:16], mod[:, 32:40], 1.0, par[:, PCOL["ln2"]:PCOL["ln2"] + 8],
                                     ALU.add, ALU.mult)
            dve.wait_ge(N2["x2_ld"], 16)
            dve.drain()

            def w_o(it):
                for k in range(4):
                    at = bass.ds(it * 4 + k, 1)
                    x = xr[:, at, :].rearrange("p a t -> p (a t)")
                    split_lo(dve, "w_o", it, k)
                    wait_unit(dve, "w_o", it, k)
                    dve.scalar_tensor_tensor(x, bank("w_o", k)[:], mod[:, bass.ds(it * 4 + 16 + k, 1)], x,
                                             ALU.mult, ALU.add).then_inc(N2["wo_d"], 1)
                    dve.drain().then_inc(freed("w_o", k), 1)
            run(dve, 2, w_o)
            norm_b.dve(dve)
            both_c = [(8, 0), (16, 2048)]

            def two_pieces(laps):
                def beside(it, k):
                    for n in (2 * k, 2 * k + 1):
                        ada_piece(dve, laps, it, k8, n, [(8, (laps - 24) * 256)])
                return beside
            mlp_up_dve(dve, "up1a", 0, lambda it, k: ada_piece(dve, 16, it, k8[:4], k, both_c))
            mlp_down_dve(dve, "down1a", False, 0, beside=lambda it, k: ada_piece(dve, 20, it, k8[4:], k, both_c))
            b2 = PCOL["b_ada_2"]
            ada_dve(dve, 2, [(48, 0, 16, b2), (96, 16, 16, b2)])
            mlp_up_dve(dve, "up1b", 16, two_pieces(24))
            mlp_down_dve(dve, "down1b", True, 40, beside=two_pieces(32))
            ada_dve(dve, 3, [(64, 0, 32, b2 + 16)])
            for at, scale, gain in ((16, 104, "norm1"), (24, 56, "norm1"), (32, 80, "norm2")):
                dve.scalar_tensor_tensor(g1s[:, at:at + 8], mod[:, scale:scale + 8], 1.0,
                                         par[:, PCOL[gain]:PCOL[gain] + 8], ALU.add, ALU.mult)
            dve.drain()
            norm_f1.dve(dve)
            norm_g.dve(dve)
            norm_c.dve(dve)
            for k in range(4):
                split_lo(dve, "gla_q", 0, k)
            dve.wait_ge(G["wa1_h"], 1)
            dve.tensor_tensor(wa1l[:], wa1[:], wa1h[:].bitcast(f32), ALU.subtract).then_inc(G["wa1_l"], 1)

            def only_lo(ph):
                p = PH[ph]

                def step(it):
                    for k in range(p["n"]):
                        split_lo(dve, ph, it, k)
                run(dve, p["steps"], step)
            only_lo("gla_k")
            for k in range(9):
                if k < 8:
                    split_lo(dve, "gla_v", 0, k)
                if k >= 1:
                    j = k - 1
                    dve.wait_ge(G["v_t"], j + 1)
                    dve.tensor_copy(vt[:, 0:4, j * P:(j + 1) * P], psum[6][:].rearrange("p (i v) -> p i v", i=4))
                    dve.tensor_copy(vt[:, 4:6, j * P:(j + 1) * P], psum[7][:, :TC].rearrange("p (i v) -> p i v", i=2))
                    dve.drain().then_inc(G["v_d"], 1)
            dve.wait_ge(G["gcon_ld"], 16)
            dve.wait_ge(G["am0"], 1)
            for k in range(8):
                split_lo(dve, "gla_r", 0, k)
                if k == 2:
                    logs_dve(dve, 0, 0)
                if k == 3:
                    keys_dve(dve, 0, 0)
                if k == 5:
                    logs_dve(dve, 0, 1)
                if k == 6:
                    keys_dve(dve, 0, 1)
            for h in range(NGLA):
                head_dve(dve, h)
            out_mean_dve(dve, NGLA - 1)
            out_gated_dve(dve, NGLA - 1)
            out_lo_dve(dve, NGLA - 1)

            def gla_o(it):
                for k in range(4):
                    x = xr[:, bass.ds(it * 4 + k, 1), :].rearrange("p a t -> p (a t)")
                    split_lo(dve, "gla_o", it, k)
                    wait_unit(dve, "gla_o", it, k)
                    dve.scalar_tensor_tensor(x, bank("gla_o", k)[:], mod[:, bass.ds(it * 4 + 64 + k, 1)], x,
                                             ALU.mult, ALU.add).then_inc(G["go_d"], 1)
                    dve.drain().then_inc(freed("gla_o", k), 1)
            run(dve, 2, gla_o)
            norm_m.dve(dve)
            mlp_up_dve(dve, "up2a", 32)
            mlp_down_dve(dve, "down2a", False, 0)
            mlp_up_dve(dve, "up2b", 48)
            mlp_down_dve(dve, "down2b", True, 88, peel_last=True)
            norm_f2.dve(dve)

        @block.tensor
        def _(pe):
            pe.wait_ge(in_ld, 32)
            norm_a.pe(pe)
            pe.wait_ge(S["cact"], 1)
            for j in range(16):
                if j % 2 == 0:
                    pe.wait_ge(slab_ld[j // 2], 16)
                for k in range(KT):
                    mm = pe.matmul(psum[7][:, 256 + j:257 + j], slab[:, j // 2, k, (j % 2) * P:(j % 2 + 1) * P],
                                   c_act[:, k:k + 1], start=k == 0, stop=k == KT - 1)
            mm.then_inc(S["mod_ps"], 1)
            pe.wait_ge(S["dw_lo"], 1)
            split_products(pe, psum[4][:], dwh[:], dwl[:], u_h, u_l, True, True,
                           lambda k: norm_a.ready(pe, k + 1)).then_inc(S["dt_ps"], 1)

            def ssm(it, ph, k0, g, par_, prev):
                for k in range(6):
                    pe_unit(pe, ph, it, k0 + k, u_h, u_l)
                    if not prev and k == 0:
                        pe.wait_ge(S["dt_ac"], 1)
                        for a, src in ((0, dd), (1, dac)):
                            for c in range(NCH):
                                mm = pe.transpose(psum[5][:, a * 128 + c * 32:a * 128 + c * 32 + 32],
                                                  src[0:HEADS, c * CH:(c + 1) * CH], ident[0:HEADS, 0:HEADS])
                        mm.then_inc(S["dt_tp"], 1)
                    if not prev and k == 1:
                        pe.wait_ge(S["dt_tok"], 1)
                        pe.matmul(psum[4][:, 0:128], last_row, acT[:].rearrange("p c h -> p (c h)"),
                                  start=True, stop=True).then_inc(S["dt_last"], 1)
                    if not prev and k == 4:
                        pe.wait_ge(S["dt_done"], 1)
                    pe_slot(pe, k, g, par_, prev)

            def ssm2(it):
                ssm(it, "ssm", 0, it * 2 + 1, 1, True)
                ssm(it, "ssm", 6, it * 2 + 2, 0, True)

            ssm(0, "ssm0", 0, 0, 0, False)
            run(pe, 3, ssm2)
            ssm(0, "ssm7", 0, 7, 1, True)
            for k in range(8):
                pe_unit(pe, "gate_ssm", 0, k, u_h, u_l)
                if k < 6:
                    pe_slot(pe, k, 8, 0, True)
            pe.wait_ge(S["f_fin"], SSM_GROUPS)

            def ssm_out(it):
                for k in range(4):
                    half = k % 2
                    pe_unit(pe, "ssm_out", it, k, lambda t: v_h(t + 8 * half), lambda t: v_l(t + 8 * half),
                            out_i=k // 2, first=half == 0, last=half == 1)
            run(pe, 4, ssm_out)

            def plain(ph, hi, lo):
                p = PH[ph]

                def step(it):
                    for k in range(p["n"]):
                        pe_unit(pe, ph, it, k, hi, lo)
                run(pe, p["steps"], step)
            plain("conv", u_h, u_l)
            pe.wait_ge(N2["cc_l"], 8)
            plain("conv_out", v_h, v_l)
            ada_pe(pe, 1)
            pe.wait_ge(N2["ml"], 8)
            plain("w_o", u_h, u_l)
            norm_b.pe(pe)
            norm_b.ready(pe, 8)
            plain("up1a", u_h, u_l)
            mlp_down_pe(pe, "down1a", 0)
            ada_pe(pe, 2)
            plain("up1b", u_h, u_l)
            mlp_down_pe(pe, "down1b", 16)
            ada_pe(pe, 3)
            norm_f1.pe(pe)
            norm_g.pe(pe)
            norm_c.pe(pe)
            norm_g.ready(pe, 8)
            plain("gla_q", u_h, u_l)
            norm_c.ready(pe, 8)
            pe.wait_ge(G["wa1_l"], 1)
            split_products(pe, psum[4][:], wa1h[:], wa1l[:], u_h, u_l, True, True)
            split_products(pe, psum[5][:, :TC], wa1h[:], wa1l[:], lambda t: uch[:, t, :], lambda t: ucl[:, t, :],
                           True, True).then_inc(G["az_d"], 1)
            for k in range(4):
                if k == 0:
                    pe.wait_ge(G["az_a"], 1)
                wait(pe, G["g_k"], k - 1)
                both(pe, "gla_k", k)
            for k in range(9):
                if k < 8:
                    if k < 2:
                        pe.wait_ge(G["g_k"], 3 + k)
                    wait(pe, G["v_a"], k - 1)
                    both(pe, "gla_v", k)
                if k >= 1:
                    j = k - 1
                    pe.wait_ge(G["v_a"], j + 1)
                    wait(pe, G["v_d"], j)
                    for i in range(TA // P):
                        b = psum[6] if i < 4 else psum[7]
                        mm = pe.transpose(b[:, (i % 4) * P:(i % 4 + 1) * P], vf[:, j % 2, i * P:(i + 1) * P], ident)
                    mm.then_inc(G["v_t"], 1)
            pe.wait_ge(G["v_d"], 8)
            for k in range(8):
                pe_unit(pe, "gla_r", 0, k, u_h, u_l)
                if k == 0:
                    gate_pe(pe, 0, 0)
                if k == 3:
                    gate_pe(pe, 0, 1)
                    keys_pe(pe, 0, 0)
                if k == 6:
                    keys_pe(pe, 0, 1)
            for b in range(4):
                pe.wait_ge(bank_free[b], PH["gla_o"]["used"][b])
            for h in range(NGLA):
                head_pe(pe, h)
            out_pe(pe, NGLA - 1)
            pe.wait_ge(G["o_lo"], NGLA)
            plain("gla_o", u_h, u_l)
            norm_m.pe(pe)
            norm_m.ready(pe, 8)
            plain("up2a", u_h, u_l)
            mlp_down_pe(pe, "down2a", 32)
            plain("up2b", u_h, u_l)
            mlp_down_pe(pe, "down2b", 48)
            norm_f2.pe(pe)


def weight_units(i):
    import numpy as np

    def unit(w, row, col):
        return w[row:row + D, col:col + P].reshape(KT, P, P).transpose(1, 0, 2).reshape(P, KT * P)

    w_in, inner = i["w_in"][0], 2048
    gates, cb, cc, cx, z, xbc = 0, 2048, 3072, 4096, 5120, 7168
    b0, c0 = xbc + inner, xbc + inner + SSM_GROUPS * P
    out = []
    for g in range(SSM_GROUPS):
        cols = [b0 + g * P, c0 + g * P, xbc + 2 * g * P, xbc + (2 * g + 1) * P, z + 2 * g * P, z + (2 * g + 1) * P]
        out += [unit(w_in, 0, c) for c in cols]
    out += [unit(w_in, 0, gates + D + j * P) for j in range(KT)]
    out += [unit(i["w_ssm_out"][0], h * D, j * P) for j in range(KT) for h in range(2)]
    out += [unit(w_in, 0, c + j * P) for j in range(KT) for c in (cc, cx, cb, gates)]
    out += [unit(i["w_conv_out"][0], 0, j * P) for j in range(KT)]
    out += [unit(i["w_o"][0], 0, j * P) for j in range(KT)]

    def mlp(up, down):
        for half in range(2):
            for j in range(16):
                yield unit(up, 0, (16 * half + j) * P)
            for j in range(KT):
                for h in range(2):
                    yield unit(down, (2 * half + h) * D, j * P)
    out += mlp(i["w_up"][0], i["w_down"][0])
    gla = i["gla_w_in_2"][0]
    for at, n in ((0, 4), (512, 4), (1024, 8), (2048, 8)):
        out += [unit(gla, 0, at + j * P) for j in range(n)]
    out += [unit(i["gla_w_o_2"][0], 0, j * P) for j in range(KT)]
    out += mlp(i["mlp_w1_2"][0], i["mlp_w2_2"][0])
    assert len(out) == UNITS
    return np.stack(out)


def packed_params(i):
    import numpy as np

    def cols(v):
        return np.asarray(v).reshape(-1, P).T

    inner = 2048
    conv = np.asarray(i["ssm_conv_w"][0])
    bias = np.asarray(i["ssm_conv_b"][0])
    tiles = []
    for g in range(SSM_GROUPS):
        tiles += [inner + g * P, inner + SSM_GROUPS * P + g * P, 2 * g * P, (2 * g + 1) * P]
    ssm_w = np.stack([conv[tap, t:t + P] for tap in range(4) for t in tiles], axis=1)
    ssm_b = np.stack([bias[t:t + P] for t in tiles], axis=1)
    skip = np.repeat(i["d_skip"][0], 64)
    parts = {
        "b_ada": cols(i["b_ada"][0]), "ln1": cols(i["ln1"][0]), "ln2": cols(i["ln2"][0]),
        "conv_w": cols(i["conv_w"][0]), "ssm_w": ssm_w, "ssm_b": ssm_b, "ssm_norm": cols(i["ssm_norm_w"][0]),
        "d_skip": cols(skip), "dt_bias": np.tile(i["dt_bias"][0], 4)[:, None], "a_log": np.tile(i["a_log"][0], 4)[:, None],
        "final_norm": cols(i["final_norm"]), "c": cols(i["c"][0]), "c_2": cols(i["c_2"][0]), "c_ctx": cols(i["c_ctx_2"]),
        "b_ada_2": cols(i["ada_b_2"][0]), "norm1": cols(i["norm1_g_2"][0]), "norm2": cols(i["norm2_g_2"][0]),
        "b_a": cols(i["gla_b_a_2"][0]), "g_head": cols(i["gla_g_head_2"][0]), "final_2": cols(i["final_g_2"]),
    }
    for name, width in PARAMS:
        assert parts[name].shape == (P, width), (name, parts[name].shape)
    return np.ascontiguousarray(np.concatenate([parts[n] for n, _ in PARAMS], axis=1))


def constants():
    import numpy as np
    f = np.float32
    s, t = np.arange(P)[:, None], np.arange(P)[None, :]
    last = np.zeros((P, P), f)
    last[P - 1] = 1.0
    con = [np.eye(P, dtype=f), np.ones((P, P), f), last, np.where(t >= s, 0.0, -1e30).astype(f),
           np.broadcast_to((np.arange(T) % CH != 0).astype(f), (P, T))]
    same = s // GC == t // GC
    at = np.arange(TA) % GC
    gcon = [np.broadcast_to((at != 0).astype(f), (P, TA)), np.broadcast_to((at != GC - 1).astype(f), (P, TA)),
            (same & (t >= s)).astype(f), (same & (t <= s)).astype(f)]
    return np.concatenate(con, axis=1), np.concatenate(gcon, axis=1)


def kernel(**inputs):
    import numpy as np
    import concourse.bacc as bacc
    from concourse.bass_utils import run_bass_kernel_spmd

    i = {k: np.asarray(v) for k, v in inputs.items()}

    def tiles(w):
        return np.ascontiguousarray(w.reshape(KT, P, P).transpose(1, 0, 2).reshape(P, KT * P))

    a1 = np.zeros((D, P), np.float32)
    for d in range(2):
        a1[:, 32 * d:32 * d + 16] = i["gla_w_a1_2"][0, d]
    con, gcon = constants()
    arrays = {
        "xT": np.ascontiguousarray(i["x"][0].T),
        "ctxT": np.ascontiguousarray(i["ctx_2"][0].T),
        "units": weight_units(i),
        "w_dt": tiles(np.concatenate([i["w_in"][0][:, 11264:11296]] * 4, axis=1)),
        "w_a1": tiles(a1),
        "w_a2": np.ascontiguousarray(i["gla_w_a2_2"][0]),
        "ada1": np.ascontiguousarray(i["w_ada"][0]),
        "ada2": np.ascontiguousarray(i["ada_w_2"][0]),
        "params": packed_params(i),
        "consts": con,
        "gconsts": gcon,
    }
    nc = bacc.Bacc("TRN2", target_bir_lowering=False, num_devices=1)
    args = [nc.dram_tensor(f"in_{n}", a.shape, mybir.dt.from_np(a.dtype), kind="ExternalInput").ap()
            for n, a in arrays.items()]
    out = nc.dram_tensor("outT", (D, T), mybir.dt.float32, kind="ExternalOutput").ap()
    build(nc, *args, out)
    r = run_bass_kernel_spmd(nc, [{f"in_{n}": a for n, a in arrays.items()}], core_ids=[0])
    return np.ascontiguousarray(r.results[0]["outT"].T)[None]
```

```python
import concourse.bass as bass
from concourse import mybir
from contextlib import ExitStack

P = 128
D = 1024
T = 512
TC = 256
TA = T + TC
KT = D // P
SSM_GROUPS = 8
HEADS = 32
CH = 128
NCH = T // CH
NGLA = 4
GV = 256
GC = 64
TAU = 16.0
EPS = 1e-6
SLOTS = 4
RAW = 2
ARING = 4
ADA_PIECES = [64, 96, 160]
AHEAD = SLOTS - 1

PHASES = [
    ("ssm0", 6, [0, 1, 2, 3, 0, 1], 1),
    ("ssm", 12, [2, 3, 0, 1, 2, 3, 0, 1, 2, 3, 0, 1], 3),
    ("ssm7", 6, [2, 3, 0, 1, 2, 3], 1),
    ("gate_ssm", 8, [0, 1, 2, 3, 0, 1, 2, 3], 1),
    ("ssm_out", 4, [0, 1], 4),
    ("conv", 4, [0, 1, 2, 3], 8),
    ("conv_out", 4, [0, 1, 2, 3], 2),
    ("w_o", 4, [0, 1, 2, 3], 2),
    ("up1a", 4, [0, 1, 2, 3], 4), ("down1a", 4, [0, 1], 4),
    ("up1b", 4, [0, 1, 2, 3], 4), ("down1b", 4, [0, 1], 4),
    ("gla_q", 4, [0, 1, 2, 3], 1), ("gla_k", 4, [0, 1, 2, 3], 1),
    ("gla_v", 8, [0, 1, 2, 3, 0, 1, 2, 3], 1), ("gla_r", 8, [0, 1, 2, 3, 0, 1, 2, 3], 1),
    ("gla_o", 4, [0, 1, 2, 3], 2),
    ("up2a", 4, [0, 1, 2, 3], 4), ("down2a", 4, [0, 1], 4),
    ("up2b", 4, [0, 1, 2, 3], 4), ("down2b", 4, [0, 1], 4),
]


def phase_table():
    table, unit, used = {}, 0, [0, 0, 0, 0]
    for name, n, banks, steps in PHASES:
        table[name] = dict(u0=unit, n=n, steps=steps, banks=banks, used=list(used),
                           per=[banks.count(b) for b in range(4)])
        unit += n * steps
        for b in range(4):
            used[b] += banks.count(b) * steps
    table["end"] = dict(u0=unit)
    return table


PH = phase_table()
UNITS = PH["end"]["u0"]

PARAMS = [("b_ada", 48), ("ln1", 8), ("ln2", 8), ("conv_w", 24), ("ssm_w", 128), ("ssm_b", 32),
          ("ssm_norm", 16), ("d_skip", 16), ("dt_bias", 1), ("a_log", 1), ("final_norm", 8), ("c", 8),
          ("c_2", 8), ("c_ctx", 8), ("b_ada_2", 48), ("norm1", 8), ("norm2", 8), ("b_a", 8),
          ("g_head", 8), ("final_2", 8)]
PCOL, _at = {}, 0
for _n, _w in PARAMS:
    PCOL[_n] = _at
    _at += _w
NPAR = _at
CONSTS = [("ident", 128), ("ones", 128), ("last_row", 128), ("causal_add", 128), ("resets", 512), ("eps", 1), ("eps_squared", 1), ("epsilons", 128)]
CCOL, _at = {}, 0
for _n, _w in CONSTS:
    CCOL[_n] = _at
    _at += _w
NCON = _at
GCON = [("reset_f", TA), ("reset_b", TA), ("mask_f", 128), ("mask_b", 128)]
GCOL, _at = {}, 0
for _n, _w in GCON:
    GCOL[_n] = _at
    _at += _w
NGCON = _at


def build(nc, xT, ctxT, units, w_dt, w_a1, w_a2, ada1, ada2, params, consts, gconsts, outT):
    f32, f32r, i32 = mybir.dt.float32, mybir.dt.float32r, mybir.dt.int32
    ALU, ACT = mybir.AluOpType, mybir.ActivationFunctionType

    scratch = nc.dram_tensor("decay_rows", (2, HEADS, T), f32, kind="Internal").ap()

    ctx = ExitStack()
    with ctx:
        base = (nc.sbuf_base + 31) // 32 * 32
        end = nc.sbuf_usable_end // 32 * 32

        class Region:
            def __init__(self, start, size):
                self.at, self.end = start, start + size

            def take(self, name, shape, dt=f32):
                n = 4
                for s in shape[1:]:
                    n *= s
                t = nc.alloc_sbuf_tensor_at(name, shape, dt, offset=self.at)
                self.at += (n + 31) // 32 * 32
                assert self.at <= self.end, (name, self.at, self.end)
                return t

        def sem(name):
            return ctx.enter_context(nc.semaphore(name))

        keep = Region(base, 7648)
        par = keep.take("par", [P, NPAR])
        con = keep.take("con", [P, NCON])
        mod = keep.take("mod", [P, 112 + 16])
        g1s = keep.take("g1s", [P, 40])
        c_act = keep.take("c_act", [P, 24])
        glb = keep.take("glb", [P, 2, 18])
        gld = keep.take("gld", [P, 2, 2, 18])
        tick = keep.take("tick", [P, 1])
        RW = keep.end
        rings = Region(RW, 40960)
        wraw = rings.take("wraw", [P, RAW, KT * P])
        whi = rings.take("whi", [P, SLOTS, KT * P], f32r)
        wlo = rings.take("wlo", [P, SLOTS, KT * P], f32r)
        RU = rings.end
        ureg = Region(RU, 32768)
        uhi = ureg.take("uhi", [P, KT, T], f32r)
        ulo = ureg.take("ulo", [P, KT, T], f32r)
        RV = ureg.end
        vreg = Region(RV, 65536)
        vhi = vreg.take("vhi", [P, 16, T], f32r)
        vlo = vreg.take("vlo", [P, 16, T], f32r)
        RM = vreg.end
        mreg = Region(RM, 16384)
        mg = mreg.take("mg", [P, KT, T])
        RT = mreg.end
        WORK = end - RT

        x0 = Region(RM, 16384).take("x0", [P, KT, T])
        NT = Region(end - 10240, 10240)
        nsq = NT.take("nsq", [P, 2, T])
        nrs = NT.take("nrs", [P, T])
        nt = NT.take("nt", [P, 2, T])
        dtr = Region(RV, 40960)
        dw = dtr.take("dw", [P, KT * P])
        dwh = dtr.take("dwh", [P, KT * P], f32r)
        dwl = dtr.take("dwl", [P, KT * P], f32r)
        dx, de, dd, dl, dr, dac, dea = [dtr.take(n, [P, T]) for n in ("dx", "de", "dd", "dl", "dr", "dac", "dea")]
        nega = dtr.take("nega", [P, 1])
        sr = Region(RT, WORK)
        pads = sr.take("pads", [P, 2, T + 3])
        bc = sr.take("bc", [P, 2, 2, T])
        xs = sr.take("xs", [P, 2, T])
        YS, ES = sr.at, sr.at + 8192 + 4096
        ys = sr.take("ys", [P, 2, 2, T])
        zs = sr.take("zs", [P, 2, T])
        es = sr.take("es", [P, NCH, 4, CH])
        eac = sr.take("eac", [P, 2, T])
        sqs = sr.take("sqs", [P, 2, T])
        srs = sr.take("srs", [P, T])
        dtT = sr.take("dtT", [P, NCH, HEADS])
        acT = sr.take("acT", [P, NCH, HEADS])
        endT = sr.take("endT", [P, NCH, HEADS])
        decT = sr.take("decT", [P, NCH, HEADS])
        v14 = Region(RV + 14 * 2048, 4096)
        slabs = [nc.alloc_sbuf_tensor_at(f"slab{i}", [P, 2 * D], f32, offset=at) for i, at in
                 enumerate([RU + 8192 * i for i in range(4)] + [RV + 40960 + 8192 * i for i in range(3)] + [YS])]
        macc = nc.alloc_sbuf_tensor_at("macc", [P, 2 * D], f32, offset=ES)
        xdt = v14.take("xdt", [P, 2, 256])
        xend = v14.take("xend", [P, 2, 256])
        v14l = Region(RV + 32768 + 14 * 2048, 4096)
        bT = v14l.take("bT", [P, 2, CH])
        st = v14l.take("st", [P, 256])
        ty = v14l.take("ty", [P, 2, CH])
        cr = Region(RT, WORK)
        xr = cr.take("xr", [P, KT, T])
        aacc = cr.take("aacc", [P, 4096])
        aring = cr.take("aring", [P, ARING, 512])
        CT = cr.at
        ccx = cr.take("ccx", [P, T + 2])
        ccs = cr.take("ccs", [P, T])
        ct = cr.take("ct", [P, T])
        cy = cr.take("cy", [P, T])
        mr = Region(CT, end - CT)
        r1 = mr.take("r1", [P, T])
        hq = mr.take("hq", [P, 2, T])

        gv = Region(RV, 65536)
        kf = gv.take("kf", [P, NGLA, TA])
        qf = gv.take("qf", [P, NGLA, T])
        rf = gv.take("rf", [P, KT, T])
        VT = gv.at
        vt = gv.take("vt", [P, TA // P, D])
        az = gv.take("az", [P, TA])
        wa = Region(VT, 12288)
        wa1 = wa.take("wa1", [P, KT * P])
        wa1h = wa.take("wa1h", [P, KT * P], f32r)
        wa1l = wa.take("wa1l", [P, KT * P], f32r)
        gu = Region(RM, 16384)
        uch = gu.take("uch", [P, KT, TC], f32r)
        ucl = gu.take("ucl", [P, KT, TC], f32r)
        gm = Region(RM, 16384)
        kdT = [gm.take(f"kdT{i}", [P, 2, TA // P, P]) for i in range(2)]
        kdf = [nc.alloc_sbuf_tensor_at(f"kdf{h}", [P, 2, TA // P - 2, GC], f32,
                                       offset=RM + 6144 if h == 0 else RV + NGLA * TA * 4 + (h - 1) * T * 4)
               for h in range(NGLA)]
        gst = gm.take("gst", [P, 2, GV])
        atts = gm.take("atts", [P, 2, P])
        am = gm.take("am", [P, 2, P])
        gt = Region(RT + 16384, end - 10240 - RT - 16384)
        gcon = gt.take("gcon", [P, NGCON])
        wa2c = gt.take("wa2c", [P, P])
        GT = gt.at
        zz = gt.take("zz", [P, TA])
        ez = gt.take("ez", [P, TA])
        qd = [gt.take("qd0", [P, 2, T]), nc.alloc_sbuf_tensor_at("qd1", [P, 2, T], f32, offset=RU + 6 * 2048)]
        ki = [gt.take("ki0", [P, 2, T]), nc.alloc_sbuf_tensor_at("ki1", [P, 2, T], f32, offset=RU + 14 * 2048)]
        gx = Region(GT, 8192)
        xc = gx.take("xc", [P, KT, TC])
        vf = Region(GT, 6144).take("vf", [P, 2, TA])

        psum = [ctx.enter_context(nc.psum_tensor(f"bank{i}", [P, T], f32)) for i in range(8)]
        ident = con[:, CCOL["ident"]:CCOL["ident"] + 128]
        ones = con[:, CCOL["ones"]:CCOL["ones"] + 128]
        last_row = con[:, CCOL["last_row"]:CCOL["last_row"] + 128]
        causal_add = con[:, CCOL["causal_add"]:CCOL["causal_add"] + 128]
        resets = con[:, CCOL["resets"]:CCOL["resets"] + 512]

        eps = con[:, CCOL["eps"]:CCOL["eps"] + 1]
        eps_squared = con[:, CCOL["eps_squared"]:CCOL["eps_squared"] + 1]
        epsilons = con[:, CCOL["epsilons"]:CCOL["epsilons"] + 128]

        def pc(name, j=0):
            return par[:, PCOL[name] + j:PCOL[name] + j + 1]

        def pcd(name, j):
            return par[:, bass.ds(PCOL[name] + j, 1)]

        sgs = Region(RV + 8 * 2048, 16384).take("sgs", [P, KT, T])

        w_loaded = [sem(f"w_loaded{i}") for i in range(RAW)]
        w_hi = sem("w_hi")
        w_split = sem("w_split")
        unit_done = sem("unit_done")
        bank_free = [sem(f"bank_free{i}") for i in range(4)]
        in_ld = sem("in_ld"); slab_ld = [sem(f"slab_ld{i}") for i in range(8)]
        x_ld = sem("x_ld")

        def wait(eng, s, v):
            if isinstance(v, int) and v <= 0:
                return
            eng.wait_ge(s, v)

        def run(eng, steps, body, peel_last=False, peel_first=False, after_first=lambda: None, before_last=lambda: None):
            n = steps - (1 if peel_last else 0)
            if peel_first or n == 1:
                body(0)
                after_first()
            if n > 1:
                with eng.Fori(1 if peel_first else 0, n) as it:
                    body(it)
            if peel_last:
                before_last()
                body(steps - 1)

        def split_hi(act, ph, it, k):
            p = PH[ph]
            at = p["u0"] + k + AHEAD
            if isinstance(it, int) and at + it * p["n"] >= UNITS:
                return
            hi_part(act, at, it * (p["n"] // 4) if p["n"] % 4 == 0 else 0)

        def hi_part(act, at, quads):
            act.wait_ge(w_loaded[at % RAW], (quads * 2 + at // RAW + 1) * 16)
            wait(act, unit_done, quads * 4 + at - AHEAD)
            act.activation(whi[:, at % SLOTS, :], wraw[:, at % RAW, :], ACT.Copy).then_inc(w_hi, 1)

        def split_lo(dve, ph, it, k):
            p = PH[ph]
            at = p["u0"] + k + AHEAD
            if isinstance(it, int) and at + it * p["n"] >= UNITS:
                return
            lo_part(dve, at, it * (p["n"] // 4) if p["n"] % 4 == 0 else 0)

        def lo_part(dve, at, quads):
            dve.wait_ge(w_hi, quads * 4 + at + 1)
            dve.tensor_tensor(wlo[:, at % SLOTS, :], wraw[:, at % RAW, :],
                              whi[:, at % SLOTS, :].bitcast(f32), ALU.subtract).then_inc(w_split, 1)

        def wait_unit(eng, ph, it, k):
            p = PH[ph]
            eng.wait_ge(unit_done, it * p["n"] + p["u0"] + k + 1)

        def split_products(pe, out, hi, lo, rhs_hi, rhs_lo, first, last, tiles_ready=None):
            for k in range(KT):
                if tiles_ready is not None:
                    tiles_ready(k)
                wh, wl = hi[:, k * P:(k + 1) * P], lo[:, k * P:(k + 1) * P]
                pe.matmul(out, wh, rhs_hi(k), start=first and k == 0, stop=False)
                pe.matmul(out, wh, rhs_lo(k), start=False, stop=False)
                mm = pe.matmul(out, wl, rhs_hi(k), start=False, stop=last and k == KT - 1)
            return mm

        def pe_unit(pe, ph, it, k, rhs_hi, rhs_lo, out_i=None, first=True, last=True, tiles_ready=None):
            p = PH[ph]
            out_i = k if out_i is None else out_i
            b = p["banks"][out_i]
            pe.wait_ge(w_split, it * p["n"] + p["u0"] + k + 1)
            if first:
                wait(pe, bank_free[b], it * p["per"][b] + p["used"][b] + p["banks"][:out_i].count(b))
            s = (p["u0"] + k) % SLOTS
            mm = split_products(pe, psum[b][:], whi[:, s, :], wlo[:, s, :], rhs_hi, rhs_lo, first, last, tiles_ready)
            mm.then_inc(unit_done, 1)

        def pe_first_units(pe, ph, ready, units=2, extra=None, rhs_hi=None, rhs_lo=None):
            rhs_hi, rhs_lo = rhs_hi or u_h, rhs_lo or u_l
            p = PH[ph]
            outs = [extra] if extra is not None else []
            for u in range(units):
                b, s = p["banks"][u], (p["u0"] + u) % SLOTS
                pe.wait_ge(w_split, p["u0"] + u + 1)
                wait(pe, bank_free[b], p["used"][b])
                outs.append((psum[b], whi[:, s, :], wlo[:, s, :], unit_done))
            for k in range(KT):
                ready(pe, k + 1)
                for out, hi, lo, done in outs:
                    wh, wl = hi[:, k * P:(k + 1) * P], lo[:, k * P:(k + 1) * P]
                    pe.matmul(out[:], wh, rhs_hi(k), start=k == 0, stop=False)
                    pe.matmul(out[:], wh, rhs_lo(k), start=False, stop=False)
                    mm = pe.matmul(out[:], wl, rhs_hi(k), start=False, stop=k == KT - 1)
                    if k == KT - 1:
                        mm.then_inc(done, 1)

        def bank(ph, i):
            return psum[PH[ph]["banks"][i]]

        def freed(ph, i):
            return bank_free[PH[ph]["banks"][i]]

        norm_sem = {s: sem(f"norm_{s}") for s in ("sq", "added", "summed", "rs", "t", "hi", "u")}

        class Norm:
            def __init__(self, order, modulated, x, tok, gain, shift, hi, lo, bank, rs=None):
                self.x, self.n, self.gain, self.shift, self.hi, self.lo, self.bank = x, tok, gain, shift, hi, lo, bank
                self.one, self.all, self.adds, self.mods = order, order * KT, order * (KT - 1), modulated * KT
                self.rs = nrs if rs is None else rs

            def ready(self, eng, tiles):
                eng.wait_ge(norm_sem["u"], self.all + tiles)

            def square(self, act, j, half):
                if not isinstance(j, int) or j >= 2:
                    act.wait_ge(norm_sem["added"], self.adds + j - 1)
                act.activation(nsq[:, half, :self.n], self.x(j), ACT.Square).then_inc(norm_sem["sq"], 1)

            def act(self, act, between=lambda: None, first=0, x_ready=lambda act, j: None):
                for j in range(first, KT):
                    x_ready(act, j)
                    self.square(act, j, j % 2)
                act.wait_ge(norm_sem["summed"], self.one + 1)
                wait(act, norm_sem["u"], self.all)
                self.root(act, self.bank)
                between()
                self.modulate(act)

            def root(self, act, mean):
                n = self.n
                act.activation(self.rs[:, :n], mean[:, :n], ACT.Ln, scale=1.0 / D, bias=eps)
                act.drain()
                act.activation(self.rs[:, :n], self.rs[:, :n], ACT.Exp, scale=-0.5).then_inc(norm_sem["rs"], 1)

            def modulate(self, act):
                for j in range(KT if self.hi is not None else 0):
                    act.wait_ge(norm_sem["t"], self.mods + j + 1)
                    if j >= 2:
                        self.ready(act, j - 1)
                    for dst in (self.hi(j), nsq[:, j % 2, :self.n]):
                        last = act.activation(dst, nt[:, j % 2, :self.n], ACT.Identity, scale=self.gain(j),
                                              bias=self.shift(j))
                    last.then_inc(norm_sem["hi"], 1)

            def pool(self, pool):
                n = self.n
                for j in range(KT - 1):
                    pool.wait_ge(norm_sem["sq"], self.all + j + 1)
                    if j == 0:
                        pool.tensor_copy(nt[:, 0, :n], nsq[:, 0, :n]).then_inc(norm_sem["added"], 1)
                    else:
                        pool.tensor_tensor(nt[:, 0, :n], nt[:, 0, :n], nsq[:, j % 2, :n], ALU.add
                                           ).then_inc(norm_sem["added"], 1)
                    pool.drain()

            def pe(self, pe):
                pe.wait_ge(norm_sem["added"], self.adds + KT - 1)
                pe.matmul(self.bank[:, :self.n], ones, nt[:, 0, :self.n], start=True, stop=False)
                pe.wait_ge(norm_sem["sq"], self.all + KT)
                pe.matmul(self.bank[:, :self.n], ones, nsq[:, 1, :self.n], start=False, stop=True
                          ).then_inc(norm_sem["summed"], 1)

            def dve(self, dve, rs_ready=None, gain=None):
                n = self.n
                dve.wait_ge(norm_sem["rs"], self.one + 1 if rs_ready is None else rs_ready)
                if self.hi is None:
                    for j in range(KT):
                        dve.scalar_tensor_tensor(self.x(j), self.x(j), self.gain(j), self.rs[:, :n],
                                                 ALU.mult, ALU.mult).then_inc(norm_sem["u"], 1)
                    dve.drain()
                    return

                def scaled(j):
                    if gain is None:
                        t = dve.tensor_tensor(nt[:, j % 2, :n], self.x(j), self.rs[:, :n], ALU.mult)
                    else:
                        t = dve.scalar_tensor_tensor(nt[:, j % 2, :n], self.x(j), gain(j), self.rs[:, :n], ALU.mult, ALU.mult)
                    t.then_inc(norm_sem["t"], 1)

                scaled(0)
                scaled(1)
                for j in range(KT):
                    dve.wait_ge(norm_sem["hi"], self.mods + j + 1)
                    dve.tensor_tensor(self.lo(j), nsq[:, j % 2, :n], self.hi(j).bitcast(f32),
                                      ALU.subtract).then_inc(norm_sem["u"], 1)
                    if j + 2 < KT:
                        scaled(j + 2)
                dve.drain()

        def double_square(act, f, j):
            act.wait_ge(norm_sem["added"], f.adds + j * 2)
            act.activation(nsq[:, 0, :], f.x(j), ACT.Square).then_inc(norm_sem["sq"], 1)
            act.activation(nsq[:, 1, :], f.x(j), ACT.Square, scale=f.gain(j)).then_inc(norm_sem["sq"], 1)

        def double_act(act, f, g):
            act.wait_ge(norm_sem["summed"], f.one + 2)
            act.activation(g.rs[:], g.bank[:], ACT.Ln, scale=1.0 / D, bias=eps_squared)
            act.activation(f.rs[:], f.bank[:], ACT.Ln, scale=1.0 / D, bias=eps)
            act.drain()
            act.activation(g.rs[:], g.rs[:], ACT.Exp, scale=-0.5).then_inc(norm_sem["rs"], 1)
            act.activation(f.rs[:], f.rs[:], ACT.Exp, scale=-0.5).then_inc(norm_sem["rs"], 1)
            g.modulate(act)

        def double_pool(pool, f):
            for j in range(KT - 1):
                for i in range(2):
                    pool.wait_ge(norm_sem["sq"], f.all + 2 * j + i + 1)
                    if j == 0:
                        pool.tensor_copy(nt[:, i, :], nsq[:, i, :]).then_inc(norm_sem["added"], 1)
                    else:
                        pool.tensor_tensor(nt[:, i, :], nt[:, i, :], nsq[:, i, :], ALU.add).then_inc(norm_sem["added"], 1)
                pool.drain()

        def double_pe(pe, f, g):
            def sums(i, half, start):
                pe.matmul(f.bank[:], ones, half(0), start=start, stop=not start)
                pe.matmul(g.bank[:], ones, half(1), start=start, stop=False)
                return pe.matmul(g.bank[:], epsilons, half(0), start=False, stop=not start)
            pe.wait_ge(norm_sem["added"], f.adds + 2 * (KT - 1))
            sums(0, lambda i: nt[:, i, :], True)
            pe.wait_ge(norm_sem["sq"], f.all + 2 * KT)
            sums(1, lambda i: nsq[:, i, :], False).then_inc(norm_sem["summed"], 2)

        def u_h(k):
            return uhi[:, k, :]

        def u_l(k):
            return ulo[:, k, :]

        norm_a = Norm(0, 0, lambda j: x0[:, j, :], T, lambda j: g1s[:, j:j + 1], lambda j: mod[:, j:j + 1],
                      u_h, u_l, psum[6])

        S = {n: sem(n) for n in ("cact", "mod_ps", "mod_acc", "dw_ld", "dw_hi", "dw_lo", "dt_ps", "dt_e", "dt_w", "dt_ln", "dt_ac", "dt_ea", "scr_st", "dt_tp", "dt_tok", "dt_last", "dt_lastd", "dt_done", "dt_nega", "pad0", "cv_a", "cv_d", "cv_s", "y_skip", "z_s", "e_ld0", "e_ld1", "e_ld2", "e_ld3", "e_seg", "e_exp", "eac_ld", "pe_a", "dt_dec", "m_rdy", "pe_b", "b_dve", "f_y", "f_sq", "f_add", "f_pe", "f_ln", "f_rs", "f_n", "f_hi", "f_fin")}

        def pe_a(pe, g, par_, c):
            pe.wait_ge(S["cv_s"], 4 * g + 4)
            if c == 0:
                wait(pe, S["b_dve"], 4 * g)
            b = psum[4 + c % 2]
            wait(pe, S["m_rdy"], 4 * g + c - 1)
            s = slice(c * CH, (c + 1) * CH)
            pe.matmul(b[:, 384:512], bc[:, par_, 0, s], bc[:, par_, 1, s], start=True, stop=True)
            for q in range(2):
                pe.transpose(b[:, q * 128:(q + 1) * 128], xs[:, q, s], ident)
            pe.transpose(b[:, 256:384], bc[:, par_, 0, s], ident).then_inc(S["pe_a"], 1)

        def pe_b(pe, g, par_, c):
            pe.wait_ge(S["m_rdy"], 4 * g + c + 1)
            wait(pe, S["b_dve"], 4 * g + c)
            if c == 0:
                wait(pe, S["f_ln"], g)
            s = slice(c * CH, (c + 1) * CH)
            for h in range(4):
                mm = pe.matmul(psum[6][(h % 2) * 64:(h % 2) * 64 + 64, (h // 2) * CH:(h // 2 + 1) * CH],
                               xdt[:, c % 2, h * 64:(h + 1) * 64], es[:, c, h, :], start=True, stop=True)
            if c > 0:
                for q in range(2):
                    mm = pe.matmul(psum[6][:, 256 + q * CH:256 + (q + 1) * CH], st[:, q * 128:(q + 1) * 128],
                                   bc[:, par_, 1, s], start=True, stop=True)
            if c < NCH - 1:
                mm = pe.matmul(psum[7][:, 0:256], bT[:, c % 2, :], xend[:, c % 2, :], start=True, stop=True)
            mm.then_inc(S["pe_b"], 1)

        def pe_n(pe, g):
            pe.wait_ge(S["f_add"], g + 1)
            pe.wait_ge(S["b_dve"], 4 * g + 4)
            pe.matmul(psum[6][:], ones, sqs[:, 0, :], start=True, stop=True).then_inc(S["f_pe"], 1)

        def pe_slot(pe, k, g, par_, prev):
            q = 1 - par_
            if prev and k == 0:
                pe_b(pe, g - 1, q, 0)
                pe_a(pe, g - 1, q, 2)
            if prev and k == 1:
                pe_b(pe, g - 1, q, 1)
                pe_a(pe, g - 1, q, 3)
            if prev and k in (2, 3):
                pe_b(pe, g - 1, q, k)
            if prev and k == 5:
                pe_n(pe, g - 1)
            if k in (4, 5) and not tail(g):
                pe_a(pe, g, par_, k - 4)

        def tail(g):
            return isinstance(g, int) and g == SSM_GROUPS

        def act_conv(act, g, par_, k, it, ph, ku):
            wait_unit(act, ph, it, ku)
            dst = conv_dst(par_, k)
            if k >= 2:
                wait(act, S["pe_a"], 4 * g)
                wait(act, S["y_skip"], g)
            wait(act, S["cv_d"], 4 * g + k - 1)
            ps = bank(ph, ku)
            act.activation(dst, ps[:], ACT.Identity, scale=pcd("ssm_w", 96 + 4 * g + k),
                           bias=pcd("ssm_b", 4 * g + k))
            act.activation(pads[:, k % 2, 3:], ps[:], ACT.Copy).then_inc(S["cv_a"], 1)
            act.drain().then_inc(freed(ph, ku), 1)

        def conv_dst(par_, k):
            return bc[:, par_, k, :] if k < 2 else xs[:, k - 2, :]

        def act_silu(act, g, par_, k):
            act.wait_ge(S["cv_d"], 4 * g + k + 1)
            act.activation(conv_dst(par_, k), conv_dst(par_, k), ACT.Silu).then_inc(S["cv_s"], 1)

        def act_slot(act, k, g, par_, prev, it, ph, ku, here):
            if 1 <= k <= 3 and here:
                act_silu(act, g, par_, k - 1)
            if k == 4 and here:
                act_silu(act, g, par_, 3)
                act.wait_ge(S["e_seg"], 4 * g + NCH - 1)
                act.activation(es[:, :NCH - 1], es[:, :NCH - 1], ACT.Exp).then_inc(S["e_exp"], 1)
            if here and k < 4:
                act_conv(act, g, par_, k, it, ph, ku)
            if here and k >= 4:
                wait_unit(act, ph, it, ku)
                wait(act, S["f_y"], g)
                act.activation(zs[:, k - 4, :], bank(ph, ku)[:], ACT.Silu).then_inc(S["z_s"], 1)
                act.drain().then_inc(freed(ph, ku), 1)
            if k == 4 and prev:
                act.wait_ge(S["f_y"], g)
                act.activation(sqs[:], ys[:, 1 - par_, :, :], ACT.Square).then_inc(S["f_sq"], 1)
            if k == 5 and here:
                act.wait_ge(S["e_seg"], 4 * g + NCH)
                act.activation(es[:, NCH - 1], es[:, NCH - 1], ACT.Exp).then_inc(S["e_exp"], 1)
            if k == 5 and prev:
                act.wait_ge(S["f_pe"], g)
                act.activation(srs[:], psum[6][:], ACT.Ln, scale=1.0 / 256, bias=eps)
                act.drain().then_inc(S["f_ln"], 1)
                act.activation(srs[:], srs[:], ACT.Exp, scale=-0.5).then_inc(S["f_rs"], 1)
                act.wait_ge(S["f_n"], g)
                act.activation(vhi[:, bass.ds(2 * g - 2, 2), :], ys[:, 1 - par_, :, :], ACT.Copy).then_inc(S["f_hi"], 1)

        def dve_taps(dve, g, par_, k):
            dve.wait_ge(S["cv_a"], 4 * g + k + 1)
            dst = conv_dst(par_, k)
            for tap in range(3):
                last = dve.scalar_tensor_tensor(dst, pads[:, k % 2, tap:tap + T], pcd("ssm_w", 32 * tap + 4 * g + k),
                                                dst, ALU.mult, ALU.add)
                if tap < 2:
                    dve.drain()
            last.then_inc(S["cv_d"], 1)

        def per_head(t, c, g):
            return t[:, c, bass.ds(4 * g, 4)].unsqueeze(2).to_broadcast([P, 4, 64])

        def dve_a(dve, g, c):
            dve.wait_ge(S["pe_a"], 4 * g + c + 1)
            wait(dve, S["pe_b"], 4 * g + c - 1)
            b = psum[4 + c % 2]
            x4 = b[:, 0:256].rearrange("p (h f) -> p h f", h=4)
            dve.tensor_tensor(xdt[:, c % 2, :].rearrange("p (h f) -> p h f", h=4), x4, per_head(dtT, c, g), ALU.mult)
            if c < NCH - 1:
                dve.tensor_tensor(xend[:, c % 2, :].rearrange("p (h f) -> p h f", h=4), x4, per_head(endT, c, g),
                                  ALU.mult)
                dve.tensor_copy(bT[:, c % 2, :], b[:, 256:384])
            dve.wait_ge(S["e_exp"], 2 * g + (2 if c == NCH - 1 else 1))
            dve.tensor_tensor(es[:, c, :, :], es[:, c, :, :],
                              b[:, 384:512].unsqueeze(1).to_broadcast([P, 4, CH]), ALU.mult)
            dve.drain().then_inc(S["m_rdy"], 1)

        def dve_b(dve, g, par_, c):
            dve.wait_ge(S["pe_b"], 4 * g + c + 1)
            s = slice(c * CH, (c + 1) * CH)
            y = ys[:, par_, :, s]
            if c > 0:
                dve.wait_ge(S["eac_ld"], 64 * g + 64)
                dve.tensor_tensor(ty[:], psum[6][:, 256:512].rearrange("p (q t) -> p q t", q=2), eac[:, :, s], ALU.mult)
                dve.drain()
                dve.tensor_tensor(y, y, ty[:], ALU.add)
                dve.drain()
            dve.tensor_tensor(y, y, psum[6][:, 0:256].rearrange("p (q t) -> p q t", q=2), ALU.add)
            if c == 0:
                dve.tensor_copy(st[:], psum[7][:, 0:256])
            elif c < NCH - 1:
                s4 = st[:].rearrange("p (h f) -> p h f", h=4)
                dve.tensor_tensor(s4, s4, per_head(decT, c, g), ALU.mult)
                dve.drain()
                dve.tensor_tensor(st[:], st[:], psum[7][:, 0:256], ALU.add)
            dve.drain().then_inc(S["b_dve"], 1)

        def dve_slot(dve, k, g, par_, prev, here):
            if prev:
                q = 1 - par_
                if k == 0:
                    dve_a(dve, g - 1, 1)
                if k in (1, 2):
                    dve_b(dve, g - 1, q, k - 1)
                    dve_a(dve, g - 1, k + 1)
                if k == 3:
                    dve_b(dve, g - 1, q, 2)
                if k == 4:
                    dve_b(dve, g - 1, q, 3)
                    dve.wait_ge(S["z_s"], 2 * g)
                    dve.tensor_tensor(ys[:, q, :, :], ys[:, q, :, :], zs[:], ALU.mult).then_inc(S["f_y"], 1)
            if here and k < 4:
                dve_taps(dve, g, par_, k)
            if k == 5:
                if here:
                    dve.wait_ge(S["cv_s"], 4 * g + 4)
                    for q in range(2):
                        last = dve.tensor_scalar(ys[:, par_, q, :], xs[:, q, :], pcd("d_skip", 2 * g + q), None, ALU.mult)
                    last.then_inc(S["y_skip"], 1)
                    dve.drain()
                    dve_a(dve, g, 0)
                if prev:
                    q_ = 1 - par_
                    dve.wait_ge(S["f_rs"], g)
                    for q in range(2):
                        dve.scalar_tensor_tensor(ys[:, q_, q, :], ys[:, q_, q, :], pcd("ssm_norm", 2 * g - 2 + q),
                                                 srs[:], ALU.mult, ALU.mult)
                    dve.drain().then_inc(S["f_n"], 1)
                if prev:
                    at = bass.ds(2 * g - 2, 2)
                    dve.wait_ge(S["f_hi"], g)
                    dve.tensor_tensor(vlo[:, at, :], ys[:, q_, :, :], vhi[:, at, :].bitcast(f32),
                                      ALU.subtract).then_inc(S["f_fin"], 1)
                    dve.drain()

        def pool_squares(pool, g):
            pool.wait_ge(S["f_sq"], g)
            pool.tensor_tensor(sqs[:, 0, :], sqs[:, 0, :], sqs[:, 1, :], ALU.add).then_inc(S["f_add"], 1)

        def pool_group(pool, g):
            def load(c):
                wait(pool, S["pe_b"], 4 * g - 4 + c + 1)
                pool.dma_start(es[:, c, :, :],
                               scratch[0, bass.ds(4 * g, 4), c * CH:(c + 1) * CH].partition_broadcast(P)
                               ).then_inc(S[f"e_ld{c}"], 16)

            def exponents(c):
                pool.wait_ge(S[f"e_ld{c}"], 16 * g + 16)
                pool.tensor_tensor(es[:, c, :, :], es[:, c, :, :],
                                   causal_add.unsqueeze(1).to_broadcast([P, 4, CH]), ALU.add)
                pool.drain()
                pool.tensor_tensor(es[:, c, :, :], es[:, c, :, :],
                                   acT[:, c, bass.ds(4 * g, 4)].unsqueeze(2).to_broadcast([P, 4, CH]),
                                   ALU.subtract).then_inc(S["e_seg"], 1)
            load(0)
            load(1)
            exponents(0)
            load(2)
            exponents(1)
            load(3)
            exponents(2)
            exponents(3)
            wait(pool, S["b_dve"], 4 * g)
            for hh in range(2):
                for q in range(2):
                    pool.dma_start(eac[64 * hh:64 * hh + 64, q, :],
                                   scratch[1, bass.ds(4 * g + 2 * q + hh, 1), :].rearrange("a t -> (a t)").partition_broadcast(64)
                                   ).then_inc(S["eac_ld"], 16)
            if not (isinstance(g, int) and g == 0):
                pool_squares(pool, g)

        def x_tile(j):
            return xr[:, bass.ds(j, 1), :].rearrange("p a t -> p (a t)")

        norm_b = Norm(1, 1, x_tile, T, lambda j: g1s[:, 8 + j:9 + j], lambda j: mod[:, 24 + j:25 + j],
                      u_h, u_l, psum[6])
        norm_f1 = Norm(2, 2, x_tile, T, lambda j: pcd("final_norm", j), None, None, None, psum[6])

        N2 = {n: sem(n) for n in ("x2_ld", "cc_a", "cc_x", "cc_y", "cc_h", "cc_l", "cg_a", "co_d", "mh", "ml", "wo_d", "ada_ld0", "ada_ld1", "ada_ld2", "ada_ld3", "ada_used", "ada_read", "ada_mod", "r_h", "r_l", "dn_d", "out_st")}

        norm_g = Norm(2, 2, x_tile, T, lambda j: g1s[:, 24 + j:25 + j], lambda j: mod[:, 48 + j:49 + j],
                      u_h, u_l, psum[5], rs=mg[:, 0, :])
        norm_c = Norm(4, 3, lambda j: xc[:, j, :], TC, lambda j: g1s[:, 16 + j:17 + j], lambda j: mod[:, 96 + j:97 + j],
                      lambda j: uch[:, j, :], lambda j: ucl[:, j, :], psum[7])
        norm_m = Norm(5, 4, x_tile, T, lambda j: g1s[:, 32 + j:33 + j], lambda j: mod[:, 72 + j:73 + j],
                      u_h, u_l, psum[6])
        norm_f2 = Norm(6, 5, x_tile, T, lambda j: pc("final_2", j), None, None, None, psum[6])
        G = {n: sem(n) for n in ("xc_ld", "gcon_ld", "wa1_ld", "wa1_h", "wa1_l", "az_d", "az_a", "g_k", "v_a", "v_t", "v_d", "wa2_ld", "z_d", "exq", "qs", "za", "zl", "zb", "ex", "kd", "ktp", "ktc", "att_p", "att_d", "o_p", "st_p", "st_d", "o_sq", "o_sum", "o_ln", "o_rs", "o_n", "o_hi", "o_lo", "am0", "go_d")}
        mask = [gcon[:, GCOL[f"mask_{x}"]:GCOL[f"mask_{x}"] + P].bitcast(i32) for x in "fb"]
        reset = [gcon[:, GCOL[f"reset_{x}"]:GCOL[f"reset_{x}"] + TA] for x in "fb"]

        def prep_banks(h, d):
            return [psum[b] for b in (((4, 5), (6, 7))[d] if h == 0 else (2, 3))]

        def v_h(k):
            return vhi[:, k, :]

        def v_l(k):
            return vlo[:, k, :]

        def ada_load(pool, laps, src, col0, ks, steps):
            def step(it):
                for n, k in enumerate(ks):
                    wait(pool, N2["ada_used"], it * len(ks) + (laps - 1) * ARING + n + 1)
                    pool.dma_start(aring[:, n % ARING, :], src[k * P:(k + 1) * P, bass.ds(it * 512 + col0, 512)]
                                   ).then_inc(N2[f"ada_ld{n % ARING}"], 16)
            run(pool, steps, step, peel_first=laps == 0)

        def ada_piece(dve, laps, it, ks, n, accs):
            k, per = ks[n], len(ks) // ARING
            dve.wait_ge(N2[f"ada_ld{n % ARING}"], it * (16 * per) + (laps + n // ARING + 1) * 16)
            for ccol, acc0 in accs:
                acc = aacc[:, bass.ds(it * 512 + acc0, 512)]
                w, c = aring[:, n % ARING, :], c_act[:, ccol + k:ccol + k + 1]
                if k == 0:
                    last = dve.tensor_scalar(acc, w, c, None, ALU.mult)
                else:
                    last = dve.scalar_tensor_tensor(acc, w, c, acc, ALU.mult, ALU.add)
            last.then_inc(N2["ada_used"], 1)
            dve.drain()

        def ada_pe(pe, n):
            pe.wait_ge(N2["ada_used"], ADA_PIECES[n - 1])
            wait(pe, N2["ada_mod"], n - 1)
            for j in range(32):
                mm = pe.matmul(psum[7][:, 256 + j:257 + j], aacc[:, j * P:(j + 1) * P], ones[:, 0:1], start=True, stop=True)
            mm.then_inc(N2["ada_read"], 1)

        def ada_dve(dve, n, parts):
            dve.wait_ge(N2["ada_read"], n)
            for dst, src, count, bias in parts:
                dve.tensor_tensor(mod[:, dst:dst + count], psum[7][:, 256 + src:256 + src + count],
                                  par[:, bias:bias + count], ALU.add)
            dve.drain().then_inc(N2["ada_mod"], 1)

        def mlp_up_act(act, ph, done):
            def step(it):
                for k in range(4):
                    split_hi(act, ph, it, k)
                    wait_unit(act, ph, it, k)
                    act.activation(r1[:], bank(ph, k)[:], ACT.Relu)
                    act.drain().then_inc(freed(ph, k), 1)
                    wait(act, N2["r_l"], it * 4 + done + k - 1)
                    act.activation(hq[:, k % 2, :], r1[:], ACT.Square)
                    act.activation(vhi[:, bass.ds(it * 4 + k, 1), :].rearrange("p a t -> p (a t)"), r1[:],
                                   ACT.Square).then_inc(N2["r_h"], 1)
                    act.drain()
            run(act, 4, step, peel_first=done == 0)

        def mlp_up_dve(dve, ph, done, beside=lambda it, k: None):
            def step(it):
                for k in range(4):
                    split_lo(dve, ph, it, k)
                    dve.wait_ge(N2["r_h"], it * 4 + done + k + 1)
                    at = bass.ds(it * 4 + k, 1)
                    dve.tensor_tensor(vlo[:, at, :].rearrange("p a t -> p (a t)"), hq[:, k % 2, :],
                                      vhi[:, at, :].rearrange("p a t -> p (a t)").bitcast(f32),
                                      ALU.subtract).then_inc(N2["r_l"], 1)
                    dve.drain()
                    beside(it, k)
            run(dve, 4, step)

        def mlp_down_pe(pe, ph, done, **peel):
            def step(it):
                for k in range(4):
                    half = k % 2
                    pe.wait_ge(N2["r_l"], done + 8 + 8 * half)
                    pe_unit(pe, ph, it, k, lambda t: v_h(t + 8 * half), lambda t: v_l(t + 8 * half), out_i=k // 2,
                            first=half == 0, last=half == 1)
            run(pe, 4, step, **peel)

        def mlp_down_dve(dve, ph, half_b, gate, peel_last=False, beside=lambda it, k: None, **peel):
            def step(it):
                for k in range(4):
                    split_lo(dve, ph, it, k)
                    beside(it, k)
                    if k % 2 == 0:
                        continue
                    o = k // 2
                    at = bass.ds(it * 2 + o, 1)
                    m = mg[:, at, :].rearrange("p a t -> p (a t)")
                    wait_unit(dve, ph, it, k)
                    if not half_b:
                        dve.tensor_copy(m, bank(ph, o)[:])
                        dve.drain().then_inc(freed(ph, o), 1)
                    else:
                        x = xr[:, at, :].rearrange("p a t -> p (a t)")
                        dve.tensor_tensor(m, m, bank(ph, o)[:], ALU.add)
                        dve.drain().then_inc(freed(ph, o), 1)
                        dve.scalar_tensor_tensor(x, m, mod[:, bass.ds(it * 2 + gate + o, 1)], x, ALU.mult, ALU.add)
                        dve.drain().then_inc(N2["dn_d"], 1)
            run(dve, 4, step, peel_last, **peel)

        def out_hi(act, ph, square, before=lambda: None):
            def step(it):
                for k in range(4):
                    split_hi(act, ph, it, k)
                    if k % 2 == 0 and not (isinstance(it, int) and it == 0):
                        square(it * 2 - 2 + k // 2, k // 2)
            run(act, 4, step, peel_first=True, peel_last=True, after_first=before)
            for j in (6, 7):
                square(j, j % 2)

        def w_o_hi(act, ph, square):
            for u in range(PH[ph]["n"] * PH[ph]["steps"]):
                split_hi(act, ph, u // 4, u % 4)
                if u >= 2:
                    square(u - 2, u % 2)
            for j in (6, 7):
                square(j, j % 2)

        def only_hi(act, ph, peel_last=False):
            p = PH[ph]

            def step(it):
                for k in range(p["n"]):
                    split_hi(act, ph, it, k)
            run(act, p["steps"], step, peel_last)

        def pair_of(d, i):
            if d == 0:
                return i
            return 1 - i if i < 2 else 7 - i

        def gate_pe(pe, h, d):
            n = 2 * h + d
            pe.wait_ge(G["wa2_ld"], h * 32 + 32)
            if h > 0:
                pe.wait_ge(G["ktc"], n)
            b4, b5 = prep_banks(h, d)
            w, a = wa2c[32 * d:32 * d + 16, :], az[32 * d:32 * d + 16, :]
            pe.matmul(b4[:], w, a[:, TC:], start=True, stop=True)
            pe.matmul(b5[:, :TC], w, a[:, :TC], start=True, stop=True).then_inc(G["z_d"], 1)

        def gate_act(act, h, d):
            n = 2 * h + d
            b4, b5 = prep_banks(h, d)
            bias = pc("b_a", h + 4 * d)
            act.wait_ge(G["z_d"], n + 1)
            wait(act, G["ktp"], n)
            for func, dst in ((ACT.Abs, ez), (ACT.Identity, zz)):
                act.activation(dst[:, TC:], b4[:], func, bias=bias)
                act.activation(dst[:, :TC], b5[:, :TC], func, bias=bias)
            act.drain()
            act.activation(ez[:], ez[:], ACT.Exp, scale=-1.0)
            act.drain()
            act.activation(ez[:], ez[:], ACT.Ln, bias=1.0).then_inc(G["za"], 1)

        def logs_dve(dve, h, d):
            dve.wait_ge(G["za"], 2 * h + d + 1)
            dve.scalar_tensor_tensor(ez[:], zz[:], 0.0, ez[:], ALU.min, ALU.subtract)
            dve.drain()
            way = 1 if d == 0 else -1
            dve.tensor_tensor_scan(zz[:, ::way], reset[d][:, ::way], ez[:, ::way], 0.0, ALU.mult, ALU.add)
            dve.drain()
            z3 = zz[:].rearrange("p (c t) -> p c t", t=GC)
            edge = GC - 1 if d == 0 else 0
            dve.tensor_copy(glb[:, d, 0:12], z3[:, :, edge])
            dve.tensor_tensor(ez[:].rearrange("p (c t) -> p c t", t=GC), z3,
                              z3[:, :, edge:edge + 1].to_broadcast([P, 12, GC]), ALU.subtract)
            dve.drain()
            pairs = glb[:, d, 0:12].rearrange("p (r a) -> p r a", a=2)
            dve.tensor_tensor(glb[:, d, 12:18], pairs[:, :, 0], pairs[:, :, 1], ALU.add)
            dve.drain().then_inc(G["zb"], 1)

        def decay_act(act, h, d):
            act.wait_ge(G["zb"], 2 * h + d + 1)
            act.activation(gld[:, h % 2, d, :], glb[:, d, :], ACT.Exp, scale=1.0 / TAU)
            act.activation(ez[:], ez[:], ACT.Exp, scale=-1.0 / TAU)
            act.drain().then_inc(G["ex"], 1)
            act.activation(qd[h % 2][:, d, :], zz[:, TC:], ACT.Exp, scale=1.0 / TAU)
            act.activation(ki[h % 2][:, d, :], zz[:, TC:], ACT.Exp, scale=-1.0 / TAU)
            act.drain().then_inc(G["exq"], 1)

        def chunk_decays(h, d, a):
            g = gld[:, h % 2, d, 0:12].rearrange("p (r a) -> p r a", a=2)
            return g[:, :, a:a + 1].to_broadcast([P, TA // P, GC])

        def keys_dve(dve, h, d):
            dve.wait_ge(G["ex"], 2 * h + d + 1)
            dve.tensor_tensor(ez[:], ez[:], kf[:, h, :], ALU.mult)
            dve.drain()
            first = ez[:].rearrange("p (r a t) -> p r a t", a=2, t=GC)[:, :, d, :]
            dve.tensor_copy(kdf[h][:, d, :, :], first[:, 2:, :])
            dve.drain()
            dve.tensor_tensor(first, first, chunk_decays(h, d, 1 - d), ALU.mult).then_inc(G["kd"], 1)

        def decayed_pool(pool, h, d):
            pool.wait_ge(G["exq"], 2 * h + d + 1)
            q, k = qd[h % 2][:, d, :], ki[h % 2][:, d, :]
            pool.tensor_tensor(q, q, qf[:, h, :], ALU.mult)
            pool.tensor_tensor(k, k, kf[:, h, TC:], ALU.mult)
            pool.drain().then_inc(G["zl"], 1)

        def keys_pe(pe, h, d):
            pe.wait_ge(G["kd"], 2 * h + d + 1)
            for i in range(TA // P):
                b = prep_banks(h, d)[i // 4]
                mm = pe.transpose(b[:, (i % 4) * P:(i % 4 + 1) * P], ez[:, i * P:(i + 1) * P], ident)
            mm.then_inc(G["ktp"], 1)

        def keys_act(act, h, d):
            b4, b5 = prep_banks(h, d)
            act.wait_ge(G["ktp"], 2 * h + d + 1)
            act.activation(kdT[h % 2][:, d, 0:4, :], b4[:].rearrange("p (i k) -> p i k", i=4), ACT.Copy)
            act.activation(kdT[h % 2][:, d, 4:6, :], b5[:, :TC].rearrange("p (i k) -> p i k", i=2), ACT.Copy)
            act.drain().then_inc(G["ktc"], 1)

        def head_values(h, i, v0=0, v1=GV):
            return vt[:, i, h * GV + v0:h * GV + v1]

        def att_pe(pe, h):
            def scores(p):
                s = slice(p * P, (p + 1) * P)
                b = psum[1 - p % 2]
                wait(pe, G["att_d"], h * 4 + p - 1)
                for d in range(2):
                    pe.matmul(b[:, d * P:(d + 1) * P], ki[h % 2][:, d, s], qd[h % 2][:, d, s], start=True, stop=True)
                for d in range(2):
                    at = p * P + (1 - d) * GC
                    mm = pe.matmul(b[d * GC:(d + 1) * GC, 2 * P + d * GC:2 * P + (d + 1) * GC], kdf[h][:, d, p, :],
                                   qd[h % 2][:, d, at:at + GC], start=True, stop=True)
                mm.then_inc(G["att_p"], 1)
            pe.wait_ge(G["zl"], h * 2 + 2)
            scores(0)
            wait(pe, G["o_ln"], h)
            scores(1)
            wait(pe, G["o_n"], h)
            for p in range(4):
                if 1 <= p < 3:
                    scores(p + 1)
                pe.wait_ge(G["att_d"], h * 4 + p + 1)
                s = slice(p * P, (p + 1) * P)
                for v in range(2):
                    mm = pe.matmul(psum[6 + v][:, s], head_values(h, 2 + p, v * P, v * P + P), atts[:, p % 2, :],
                                   start=p == 0, stop=False, skip_group_check=True)
                mm.then_inc(G["o_p"], 1)

        def att_dve(dve, h, p):
            dve.wait_ge(G["att_p"], h * 4 + p + 1)
            wait(dve, G["o_p"], h * 4 + p - 1)
            dve.tensor_copy(tick[:], con[:, 0:1])
            for d in range(2):
                dve.copy_predicated(am[:, d, :], mask[d], psum[1 - p % 2][:, d * P:(d + 1) * P])
            dve.drain()
            for d in range(2):
                dve.tensor_copy(am[d * GC:(d + 1) * GC, d, (1 - d) * GC:(2 - d) * GC],
                                psum[1 - p % 2][d * GC:(d + 1) * GC, 2 * P + d * GC:2 * P + (d + 1) * GC])
            dve.drain()
            dve.tensor_tensor(atts[:, p % 2, :], am[:, 0, :], am[:, 1, :], ALU.add).then_inc(G["att_d"], 1)
            dve.drain()

        def queries_dve(dve, h):
            dve.wait_ge(G["att_p"], h * 4 + 4)
            for d in range(2):
                q = qd[h % 2][:, d, :].rearrange("p (r a t) -> p r a t", a=2, t=GC)[:, :, 1 - d, :]
                dve.tensor_tensor(q, q, chunk_decays(h, d, d)[:, 2:, :], ALU.mult)
            dve.drain().then_inc(G["qs"], 1)

        def states_pe(pe, h, first, last):
            for s in range(first, last):
                i, d = s // 2, s % 2
                r = pair_of(d, i)
                wait(pe, G["st_d"], h * 10 + s - 1)
                if i == 0:
                    pe.wait_ge(G["ktc"], h * 2 + 2)
                if i >= 2:
                    t = slice((r - 2) * P, (r - 1) * P)
                    pe.wait_ge(G["qs"], h + 1)
                    for v in range(2):
                        mm = pe.matmul(psum[6 + v][:, t], gst[:, d, v * P:(v + 1) * P], qd[h % 2][:, d, t], start=False,
                                       stop=s == 11, skip_group_check=True)
                if i < 5:
                    mm = pe.matmul(psum[4 + d][:, 0:GV], kdT[h % 2][:, d, r, :], head_values(h, r), start=True, stop=True)
                mm.then_inc(G["st_p"], 1)

        def states_dve(dve, h, first, last):
            for s in range(first, last):
                i, d = s // 2, s % 2
                r = pair_of(d, i)
                dve.wait_ge(G["st_p"], h * 12 + s + 1)
                if i == 0:
                    dve.tensor_copy(gst[:, d, :], psum[4 + d][:, 0:GV]).then_inc(G["st_d"], 1)
                else:
                    dve.scalar_tensor_tensor(gst[:, d, :], gst[:, d, :], gld[:, h % 2, d, 12 + r:13 + r],
                                             psum[4 + d][:, 0:GV], ALU.mult, ALU.add).then_inc(G["st_d"], 1)
                dve.drain()

        def out_act(act, h):
            act.wait_ge(G["st_p"], h * 12 + 12)
            for v in range(2):
                act.activation(nsq[:, v, :], psum[6 + v][:], ACT.Square)
            act.drain().then_inc(G["o_sq"], 1)
            act.wait_ge(G["o_sum"], h + 1)
            act.activation(nrs[:], psum[0][:], ACT.Ln, scale=1.0 / GV, bias=eps)
            act.drain().then_inc(G["o_ln"], 1)
            act.activation(nrs[:], nrs[:], ACT.Exp, scale=-0.5).then_inc(G["o_rs"], 1)

        def out_hi_act(act, h):
            act.wait_ge(G["o_n"], h + 1)
            act.activation(uhi[:, 2 * h:2 * h + 2, :], nt[:], ACT.Copy).then_inc(G["o_hi"], 1)

        def out_pe(pe, h):
            pe.wait_ge(G["o_sq"], h + 1)
            pe.wait_ge(G["att_d"], h * 4 + 4)
            for v in range(2):
                mm = pe.matmul(psum[0][:], ones, nsq[:, v, :], start=v == 0, stop=v == 1)
            mm.then_inc(G["o_sum"], 1)

        def out_gated_dve(dve, h):
            dve.wait_ge(G["o_rs"], h + 1)
            for v in range(2):
                dve.scalar_tensor_tensor(nt[:, v, :], psum[6 + v][:], pc("g_head", h * 2 + v), nrs[:], ALU.mult, ALU.mult)
            dve.drain()
            dve.tensor_tensor(nt[:], nt[:], rf[:, 2 * h:2 * h + 2, :], ALU.mult)
            dve.drain().then_inc(G["o_n"], 1)

        def out_lo_dve(dve, h):
            at = slice(2 * h, 2 * h + 2)
            dve.wait_ge(G["o_hi"], h + 1)
            dve.tensor_tensor(ulo[:, at, :], nt[:], uhi[:, at, :].bitcast(f32), ALU.subtract)
            dve.drain().then_inc(G["o_lo"], 1)

        def head_pe(pe, h):
            more = h + 1 < NGLA
            states_pe(pe, h, 0, 2)
            if h > 0:
                out_pe(pe, h - 1)
            if more:
                gate_pe(pe, h + 1, 0)
            states_pe(pe, h, 2, 4)
            att_pe(pe, h)
            states_pe(pe, h, 4, 5)
            if more:
                keys_pe(pe, h + 1, 0)
                gate_pe(pe, h + 1, 1)
            states_pe(pe, h, 5, 12)
            if more:
                keys_pe(pe, h + 1, 1)

        def head_act(act, h):
            more = h + 1 < NGLA
            if h > 0:
                out_act(act, h - 1)
            if more:
                gate_act(act, h + 1, 0)
            if h > 0:
                out_hi_act(act, h - 1)
            if more:
                decay_act(act, h + 1, 0)
                keys_act(act, h + 1, 0)
                gate_act(act, h + 1, 1)
                decay_act(act, h + 1, 1)
                keys_act(act, h + 1, 1)

        def head_dve(dve, h):
            more = h + 1 < NGLA
            states_dve(dve, h, 0, 4)
            att_dve(dve, h, 0)
            if h > 0:
                out_gated_dve(dve, h - 1)
            att_dve(dve, h, 1)
            att_dve(dve, h, 2)
            if more:
                logs_dve(dve, h + 1, 0)
            att_dve(dve, h, 3)
            queries_dve(dve, h)
            if more:
                keys_dve(dve, h + 1, 0)
            states_dve(dve, h, 4, 7)
            if h > 0:
                out_lo_dve(dve, h - 1)
            if more:
                logs_dve(dve, h + 1, 1)
            states_dve(dve, h, 7, 9)
            if more:
                keys_dve(dve, h + 1, 1)
            states_dve(dve, h, 9, 10)

        def both(pe, ph, k):
            p = PH[ph]
            b, s = p["banks"][k], (p["u0"] + k) % SLOTS
            pe.wait_ge(w_split, p["u0"] + k + 1)
            pe.wait_ge(bank_free[b], p["used"][b] + p["banks"][:k].count(b))
            split_products(pe, psum[b][:], whi[:, s, :], wlo[:, s, :], u_h, u_l, True, True)
            split_products(pe, psum[4 + k % 2][:, :TC], whi[:, s, :], wlo[:, s, :], lambda t: uch[:, t, :],
                           lambda t: ucl[:, t, :], True, True).then_inc(unit_done, 1)

        block = ctx.enter_context(nc.Block())

        @block.sync
        def _(sp):
            sp.dma_start(par[:], params).then_inc(in_ld, 16)
            sp.dma_start(con[:], consts).then_inc(in_ld, 16)
            for j in range(2):
                sp.dma_start(x0[:, 4 * j:4 * j + 4, :],
                             xT[512 * j:512 * j + 512, :].rearrange("(k p) t -> p k t", p=P)).then_inc(x_ld, 16)
            for j in range(8):
                sp.dma_start(slabs[j][:], ada1[j * P:(j + 1) * P, 0:2 * D]).then_inc(slab_ld[j], 16)
            sp.dma_start(dw[:], w_dt).then_inc(S["dw_ld"], 16)
            for s in range(RAW):
                sp.dma_start(wraw[:, s, :], units[s]).then_inc(w_loaded[s], 16)
            with sp.Fori(1, UNITS // RAW) as i:
                for s in range(RAW):
                    sp.wait_ge(w_split, i * RAW + s - RAW + 1)
                    sp.dma_start(wraw[:, s, :], units[bass.ds(i * RAW + s, 1)].rearrange("a p n -> (a p) n")
                                 ).then_inc(w_loaded[s], 16)
            for j in range(KT):
                norm_f2.ready(sp, j + 1)
                sp.dma_start(outT[j * P:(j + 1) * P, :], xr[:, j, :]).then_inc(N2["out_st"], 16)
            sp.wait_ge(N2["out_st"], KT * 16)

        @block.gpsimd
        def _(pool):
            pool.memset(pads[:, :, 0:3], 0.0).then_inc(S["pad0"], 1)
            norm_a.pool(pool)
            pool.wait_ge(S["scr_st"], 32)
            pool.wait_ge(S["dt_done"], 1)
            pool_group(pool, 0)
            with pool.Fori(1, SSM_GROUPS) as g:
                pool_group(pool, g)
            pool_squares(pool, SSM_GROUPS)
            pool.wait_ge(S["f_fin"], SSM_GROUPS)
            k8 = list(range(KT))
            ada_load(pool, 0, ada1, 2048, k8, 8)
            norm_b.pool(pool)
            norm_b.ready(pool, 8)
            ada_load(pool, 16, ada2, 0, k8, 4)
            ada_load(pool, 24, ada2, 2048, k8, 8)
            double_pool(pool, norm_f1)
            pool.wait_ge(N2["ada_read"], 3)
            pool.dma_start(xc[:], ctxT.rearrange("(k p) t -> p k t", p=P)).then_inc(G["xc_ld"], 16)
            pool.dma_start(gcon[:], gconsts).then_inc(G["gcon_ld"], 16)
            pool.wait_ge(N2["dn_d"], 8)
            pool.dma_start(wa1[:], w_a1).then_inc(G["wa1_ld"], 16)
            norm_c.pool(pool)
            pool.wait_ge(G["v_t"], 8)
            pool.memset(am[:], 0.0).then_inc(G["am0"], 1)

            def gates(h):
                wait(pool, G["z_d"], h * 2)
                for d in range(2):
                    pool.dma_start(wa2c[32 * d:32 * d + 16, :], w_a2[d, :, bass.ds(h * P, P)]).then_inc(G["wa2_ld"], 16)
            gates(0)
            for h in range(NGLA):
                decayed_pool(pool, h, 0)
                if h + 1 < NGLA:
                    gates(h + 1)
                decayed_pool(pool, h, 1)
            norm_m.pool(pool)
            norm_f2.pool(pool)

        @block.scalar
        def _(act):
            act.wait_ge(in_ld, 32)
            act.activation(c_act[:], par[:, PCOL["c"]:PCOL["c"] + 24], ACT.Silu).then_inc(S["cact"], 1)

            def before_modulation():
                act.wait_ge(S["dw_ld"], 16)
                act.activation(dwh[:], dw[:], ACT.Copy).then_inc(S["dw_hi"], 1)
                act.activation(nega[:], pc("a_log"), ACT.Exp).then_inc(S["dt_nega"], 1)
                hi_part(act, 0, 0)
            act.wait_ge(x_ld, 32)
            norm_a.act(act, before_modulation)
            for u in range(1, AHEAD):
                hi_part(act, u, 0)
            act.wait_ge(S["dt_ps"], 1)
            act.activation(dx[:], psum[4][:], ACT.Identity, bias=pc("dt_bias"))
            act.drain()
            act.activation(de[:], dx[:], ACT.Abs)
            act.drain()
            act.activation(de[:], de[:], ACT.Exp, scale=-1.0).then_inc(S["dt_e"], 1)
            act.wait_ge(S["dt_w"], 1)
            act.activation(dl[:], dd[:], ACT.Ln).then_inc(S["dt_ln"], 1)
            act.wait_ge(S["dt_ac"], 1)
            act.dma_start(scratch[0], dac[0:HEADS, :]).then_inc(S["scr_st"], 16)
            act.activation(dea[:], dac[:], ACT.Exp).then_inc(S["dt_ea"], 1)
            act.wait_ge(S["dt_ea"], 1)
            act.dma_start(scratch[1], dea[0:HEADS, :]).then_inc(S["scr_st"], 16)
            act.wait_ge(S["dt_tp"], 1)
            tp = psum[5][:].rearrange("p (a c h) -> p a c h", a=4, c=NCH)
            act.activation(dtT[:], tp[:, 0, :, :], ACT.Copy)
            act.activation(acT[:], tp[:, 1, :, :], ACT.Copy)
            act.drain().then_inc(S["dt_tok"], 1)
            act.wait_ge(S["dt_last"], 1)
            act.activation(decT[:], psum[4][:, 0:128].rearrange("p (c h) -> p c h", c=NCH), ACT.Exp
                           ).then_inc(S["dt_dec"], 1)
            act.wait_ge(S["dt_lastd"], 1)
            act.activation(endT[:], endT[:], ACT.Exp)
            act.drain().then_inc(S["dt_lastd"], 1)
            act.wait_ge(S["pad0"], 1)

            def ssm(it, ph, k0, g, par_, prev):
                for k in range(6):
                    split_hi(act, ph, it, k0 + k)
                    act_slot(act, k, g, par_, prev, it, ph, k0 + k, True)

            def ssm2(it):
                ssm(it, "ssm", 0, it * 2 + 1, 1, True)
                ssm(it, "ssm", 6, it * 2 + 2, 0, True)

            ssm(0, "ssm0", 0, 0, 0, False)
            run(act, 3, ssm2)
            ssm(0, "ssm7", 0, 7, 1, True)
            for k in range(8):
                split_hi(act, "gate_ssm", 0, k)
                if k < 6:
                    act_slot(act, k, 8, 0, True, 0, "gate_ssm", k, False)
                wait_unit(act, "gate_ssm", 0, k)
                act.activation(mg[:, k, :], bank("gate_ssm", k)[:], ACT.Sigmoid)
                act.drain().then_inc(freed("gate_ssm", k), 1)
            act.wait_ge(S["f_fin"], SSM_GROUPS)
            act.dma_start(xr[:], xT.rearrange("(k p) t -> p k t", p=P)).then_inc(N2["x2_ld"], 16)
            only_hi(act, "ssm_out")

            def conv(it):
                for k in range(4):
                    split_hi(act, "conv", it, k)
                    wait_unit(act, "conv", it, k)
                    if k == 0:
                        wait(act, N2["cc_x"], it)
                        act.activation(ccs[:], bank("conv", 0)[:], ACT.Copy).then_inc(N2["cc_a"], 1)
                        act.drain().then_inc(freed("conv", 0), 1)
                    if k == 3:
                        at = bass.ds(it, 1)
                        act.activation(sgs[:, at, :].rearrange("p a t -> p (a t)"), bank("conv", 3)[:], ACT.Sigmoid)
                        act.drain().then_inc(freed("conv", 3), 1)
                        act.wait_ge(N2["cc_y"], it + 1)
                        act.activation(vhi[:, at, :].rearrange("p a t -> p (a t)"), cy[:], ACT.Copy).then_inc(N2["cc_h"], 1)
            conv(0)
            with act.Fori(1, 8) as it:
                conv(it)
            act.drain().then_inc(N2["cg_a"], 1)

            def conv_out(it):
                for k in range(4):
                    split_hi(act, "conv_out", it, k)
                    act.wait_ge(N2["co_d"], it * 4 + k + 1)
                    act.activation(uhi[:, bass.ds(it * 4 + k, 1), :], mg[:, bass.ds(it * 4 + k, 1), :],
                                   ACT.Copy).then_inc(N2["mh"], 1)
            run(act, 2, conv_out)
            act.wait_ge(N2["ada_used"], ADA_PIECES[0])

            def ready_square(norm, sem_, before, square=None):
                def go(j, half):
                    act.wait_ge(sem_, j + (before + 1))
                    (square or norm.square)(act, j, half)
                return go
            w_o_hi(act, "w_o", ready_square(norm_b, N2["wo_d"], 0))
            norm_b.act(act, first=KT)
            mlp_up_act(act, "up1a", 0)
            only_hi(act, "down1a")
            mlp_up_act(act, "up1b", 16)
            out_hi(act, "down1b", ready_square(norm_f1, N2["dn_d"], 0, lambda a, j, half: double_square(a, norm_f1, j)),
                   lambda: act.wait_ge(N2["ada_used"], ADA_PIECES[2]))
            double_act(act, norm_f1, norm_g)
            for k in range(2):
                split_hi(act, "gla_q", 0, k)
            act.wait_ge(G["wa1_ld"], 16)
            act.activation(wa1h[:], wa1[:], ACT.Copy).then_inc(G["wa1_h"], 1)
            norm_g.ready(act, 8)
            act.wait_ge(G["xc_ld"], 16)
            norm_c.act(act)
            for k in range(4):
                if k >= 2:
                    split_hi(act, "gla_q", 0, k)
                wait_unit(act, "gla_q", 0, k)
                act.activation(qf[:, k, :], bank("gla_q", k)[:], ACT.Copy, scale=float(P) ** -0.5)
                act.drain().then_inc(freed("gla_q", k), 1)

            act.wait_ge(G["az_d"], 1)
            act.activation(az[:, TC:], psum[4][:], ACT.Copy)
            act.activation(az[:, :TC], psum[5][:, :TC], ACT.Copy)
            act.drain().then_inc(G["az_a"], 1)
            for k in range(4):
                split_hi(act, "gla_k", 0, k)
                wait_unit(act, "gla_k", 0, k)
                act.activation(kf[:, k, TC:], bank("gla_k", k)[:], ACT.Copy)
                act.activation(kf[:, k, :TC], psum[4 + k % 2][:, :TC], ACT.Copy).then_inc(G["g_k"], 1)
                act.drain().then_inc(freed("gla_k", k), 1)
            for k in range(8):
                split_hi(act, "gla_v", 0, k)
                wait_unit(act, "gla_v", 0, k)
                wait(act, G["v_t"], k - 1)
                act.activation(vf[:, k % 2, TC:], bank("gla_v", k)[:], ACT.Copy)
                act.activation(vf[:, k % 2, :TC], psum[4 + k % 2][:, :TC], ACT.Copy).then_inc(G["v_a"], 1)
                act.drain().then_inc(freed("gla_v", k), 1)
            act.wait_ge(G["v_t"], 8)
            for k in range(8):
                split_hi(act, "gla_r", 0, k)
                if k == 1:
                    gate_act(act, 0, 0)
                if k == 3:
                    decay_act(act, 0, 0)
                if k == 4:
                    keys_act(act, 0, 0)
                    gate_act(act, 0, 1)
                if k == 6:
                    decay_act(act, 0, 1)
                wait_unit(act, "gla_r", 0, k)
                act.activation(rf[:, k, :], bank("gla_r", k)[:], ACT.Silu)
                act.drain().then_inc(freed("gla_r", k), 1)
                if k == 7:
                    keys_act(act, 0, 1)
            for h in range(NGLA):
                head_act(act, h)
            out_act(act, NGLA - 1)
            out_hi_act(act, NGLA - 1)
            w_o_hi(act, "gla_o", ready_square(norm_m, G["go_d"], 0))
            norm_m.act(act, first=KT)
            mlp_up_act(act, "up2a", 32)
            only_hi(act, "down2a")
            mlp_up_act(act, "up2b", 48)
            out_hi(act, "down2b", ready_square(norm_f2, N2["dn_d"], 8))
            norm_f2.act(act, first=KT)

        @block.vector
        def _(dve):
            dve.wait_ge(in_ld, 32)
            dve.wait_ge(S["cact"], 1)
            for k in range(KT):
                dve.wait_ge(slab_ld[k], 16)
                if k == 0:
                    dve.tensor_scalar(macc[:], slabs[k][:], c_act[:, k:k + 1], None, ALU.mult)
                else:
                    last = dve.scalar_tensor_tensor(macc[:], slabs[k][:], c_act[:, k:k + 1], macc[:], ALU.mult, ALU.add)
                if k < KT - 1:
                    dve.drain()
            last.then_inc(S["mod_acc"], 1)
            dve.wait_ge(S["dw_hi"], 1)
            dve.tensor_tensor(dwl[:], dw[:], dwh[:].bitcast(f32), ALU.subtract).then_inc(S["dw_lo"], 1)
            dve.wait_ge(S["mod_ps"], 1)
            dve.tensor_tensor(mod[:, 0:16], psum[7][:, 256:272], par[:, PCOL["b_ada"]:PCOL["b_ada"] + 16], ALU.add)
            dve.drain()
            dve.scalar_tensor_tensor(g1s[:, 0:8], mod[:, 8:16], 1.0, par[:, PCOL["ln1"]:PCOL["ln1"] + 8],
                                     ALU.add, ALU.mult)
            dve.drain()
            lo_part(dve, 0, 0)
            norm_a.dve(dve)
            for u in range(1, AHEAD):
                lo_part(dve, u, 0)
            dve.wait_ge(S["dt_e"], 1)
            dve.tensor_scalar(dd[:], de[:], 1.0, None, ALU.add).then_inc(S["dt_w"], 1)
            dve.drain()
            dve.reciprocal(dr[:], dd[:])
            dve.tensor_scalar(dac[:], dd[:], -1.0, None, ALU.add)
            dve.drain()
            dve.tensor_tensor(de[:], de[:], dac[:], ALU.subtract)
            dve.drain()
            dve.tensor_tensor(de[:], de[:], dr[:], ALU.mult)
            dve.wait_ge(S["dt_ln"], 1)
            dve.drain()
            dve.tensor_tensor(de[:], de[:], dl[:], ALU.add)
            dve.drain()
            dve.scalar_tensor_tensor(dd[:], dx[:], 0.0, de[:], ALU.max, ALU.add)
            dve.wait_ge(S["dt_nega"], 1)
            dve.drain()
            dve.tensor_scalar(dr[:], dd[:], nega[:], -1.0, ALU.mult, ALU.mult)
            dve.drain()
            dve.tensor_tensor_scan(dac[:], resets, dr[:], 0.0, ALU.mult, ALU.add).then_inc(S["dt_ac"], 1)
            dve.wait_ge(S["dt_dec"], 1)
            dve.tensor_tensor(endT[:], psum[4][:, 0:128].rearrange("p (c h) -> p c h", c=NCH), acT[:],
                              ALU.subtract).then_inc(S["dt_lastd"], 1)
            dve.wait_ge(S["dt_lastd"], 2)
            dve.tensor_tensor(endT[:], endT[:], dtT[:], ALU.mult).then_inc(S["dt_done"], 1)
            dve.drain()
            dve.wait_ge(S["pad0"], 1)

            def ssm(it, ph, k0, g, par_, prev):
                for k in range(6):
                    split_lo(dve, ph, it, k0 + k)
                    dve_slot(dve, k, g, par_, prev, True)

            def ssm2(it):
                ssm(it, "ssm", 0, it * 2 + 1, 1, True)
                ssm(it, "ssm", 6, it * 2 + 2, 0, True)

            ssm(0, "ssm0", 0, 0, 0, False)
            run(dve, 3, ssm2)
            ssm(0, "ssm7", 0, 7, 1, True)
            for k in range(8):
                split_lo(dve, "gate_ssm", 0, k)
                if k < 6:
                    dve_slot(dve, k, 8, 0, True, False)
            dve.memset(ccx[:, 0:2], 0.0)
            dve.drain()

            def ssm_out(it):
                for k in range(4):
                    split_lo(dve, "ssm_out", it, k)
                    if k % 2:
                        m = mg[:, bass.ds(it * 2 + k // 2, 1), :].rearrange("p a t -> p (a t)")
                        wait_unit(dve, "ssm_out", it, k)
                        dve.tensor_tensor(m, m, bank("ssm_out", k // 2)[:], ALU.mult)
                        dve.drain().then_inc(freed("ssm_out", k // 2), 1)
            run(dve, 4, ssm_out)

            k8 = list(range(KT))

            def conv(it):
                for k in range(4):
                    split_lo(dve, "conv", it, k)
                    for n in (2 * k, 2 * k + 1):
                        ada_piece(dve, 0, it, k8, n, [(0, 0)])
                    if k == 1:
                        dve.wait_ge(N2["cc_a"], it + 1)
                        wait_unit(dve, "conv", it, 1)
                        dve.tensor_tensor(ccx[:, 2:], ccs[:], bank("conv", 1)[:], ALU.mult).then_inc(N2["cc_x"], 1)
                        dve.drain().then_inc(freed("conv", 1), 1)
                        dve.tensor_scalar(ct[:], ccx[:, 2:], pcd("conv_w", it + 16), None, ALU.mult)
                        dve.drain()
                        for tap in range(2):
                            dve.scalar_tensor_tensor(ct[:], ccx[:, tap:tap + T], pcd("conv_w", it + 8 * tap), ct[:],
                                                     ALU.mult, ALU.add)
                            dve.drain()
                    if k == 2:
                        wait_unit(dve, "conv", it, 2)
                        wait(dve, N2["cc_h"], it)
                        dve.tensor_tensor(cy[:], ct[:], bank("conv", 2)[:], ALU.mult).then_inc(N2["cc_y"], 1)
                        dve.drain().then_inc(freed("conv", 2), 1)
                    if k == 3:
                        at = bass.ds(it, 1)
                        dve.wait_ge(N2["cc_h"], it + 1)
                        dve.tensor_tensor(vlo[:, at, :].rearrange("p a t -> p (a t)"), cy[:],
                                          vhi[:, at, :].rearrange("p a t -> p (a t)").bitcast(f32),
                                          ALU.subtract).then_inc(N2["cc_l"], 1)
                        dve.drain()
            conv(0)
            with dve.Fori(1, 8) as it:
                conv(it)
            dve.wait_ge(N2["cg_a"], 1)

            def conv_out(it):
                for k in range(4):
                    at = bass.ds(it * 4 + k, 1)
                    m = mg[:, at, :].rearrange("p a t -> p (a t)")
                    split_lo(dve, "conv_out", it, k)
                    wait_unit(dve, "conv_out", it, k)
                    dve.tensor_tensor(ct[:], sgs[:, at, :].rearrange("p a t -> p (a t)"), bank("conv_out", k)[:], ALU.mult)
                    dve.drain().then_inc(freed("conv_out", k), 1)
                    dve.tensor_tensor(m, m, ct[:], ALU.add).then_inc(N2["co_d"], 1)
                    dve.drain()
                    dve.wait_ge(N2["mh"], it * 4 + k + 1)
                    dve.tensor_tensor(ulo[:, at, :].rearrange("p a t -> p (a t)"), m,
                                      uhi[:, at, :].rearrange("p a t -> p (a t)").bitcast(f32),
                                      ALU.subtract).then_inc(N2["ml"], 1)
                    dve.drain()
            run(dve, 2, conv_out)
            b1 = PCOL["b_ada"]
            ada_dve(dve, 1, [(16, 0, 32, b1 + 16)])
            dve.scalar_tensor_tensor(g1s[:, 8:16], mod[:, 32:40], 1.0, par[:, PCOL["ln2"]:PCOL["ln2"] + 8],
                                     ALU.add, ALU.mult)
            dve.wait_ge(N2["x2_ld"], 16)
            dve.drain()

            def w_o(it):
                for k in range(4):
                    at = bass.ds(it * 4 + k, 1)
                    x = xr[:, at, :].rearrange("p a t -> p (a t)")
                    split_lo(dve, "w_o", it, k)
                    wait_unit(dve, "w_o", it, k)
                    dve.scalar_tensor_tensor(x, bank("w_o", k)[:], mod[:, bass.ds(it * 4 + 16 + k, 1)], x,
                                             ALU.mult, ALU.add).then_inc(N2["wo_d"], 1)
                    dve.drain().then_inc(freed("w_o", k), 1)
            run(dve, 2, w_o)
            norm_b.dve(dve)
            def two_pieces(laps, accs):
                def beside(it, k):
                    for n in (2 * k, 2 * k + 1):
                        ada_piece(dve, laps, it, k8, n, accs)
                return beside
            mlp_up_dve(dve, "up1a", 0, two_pieces(16, [(8, 0), (16, 2048)]))
            b2 = PCOL["b_ada_2"]
            beside = two_pieces(22, [(8, -512)])
            mlp_down_dve(dve, "down1a", False, 0, peel_first=True,
                         beside=lambda it, k: None if isinstance(it, int) else beside(it, k),
                         after_first=lambda: ada_dve(dve, 2, [(48, 0, 16, b2), (96, 16, 16, b2)]))
            mlp_up_dve(dve, "up1b", 16, two_pieces(30, [(8, 1536)]))
            beside_last = two_pieces(38, [(8, 3584)])
            mlp_down_dve(dve, "down1b", True, 40, peel_first=True,
                         beside=lambda it, k: beside_last(it, k) if isinstance(it, int) else None)
            ada_dve(dve, 3, [(64, 0, 32, b2 + 16)])
            for at, scale, gain in ((16, 104, "norm1"), (24, 56, "norm1"), (32, 80, "norm2")):
                dve.scalar_tensor_tensor(g1s[:, at:at + 8], mod[:, scale:scale + 8], 1.0,
                                         par[:, PCOL[gain]:PCOL[gain] + 8], ALU.add, ALU.mult)
            dve.drain()
            norm_g.dve(dve, norm_f1.one + 1, norm_f1.gain)
            for k in range(2):
                split_lo(dve, "gla_q", 0, k)
            dve.wait_ge(G["wa1_h"], 1)
            dve.tensor_tensor(wa1l[:], wa1[:], wa1h[:].bitcast(f32), ALU.subtract).then_inc(G["wa1_l"], 1)
            norm_f1.dve(dve, norm_f1.one + 2)
            norm_c.dve(dve)
            for k in (2, 3):
                split_lo(dve, "gla_q", 0, k)
            def only_lo(ph):
                p = PH[ph]

                def step(it):
                    for k in range(p["n"]):
                        split_lo(dve, ph, it, k)
                run(dve, p["steps"], step)
            only_lo("gla_k")
            for k in range(9):
                if k < 8:
                    split_lo(dve, "gla_v", 0, k)
                if k >= 1:
                    j = k - 1
                    dve.wait_ge(G["v_t"], j + 1)
                    dve.tensor_copy(vt[:, 0:4, j * P:(j + 1) * P], psum[6][:].rearrange("p (i v) -> p i v", i=4))
                    dve.tensor_copy(vt[:, 4:6, j * P:(j + 1) * P], psum[7][:, :TC].rearrange("p (i v) -> p i v", i=2))
                    dve.drain().then_inc(G["v_d"], 1)
            dve.wait_ge(G["gcon_ld"], 16)
            dve.wait_ge(G["am0"], 1)
            for k in range(8):
                split_lo(dve, "gla_r", 0, k)
                if k == 2:
                    logs_dve(dve, 0, 0)
                if k == 3:
                    keys_dve(dve, 0, 0)
                if k == 5:
                    logs_dve(dve, 0, 1)
                if k == 6:
                    keys_dve(dve, 0, 1)
            for h in range(NGLA):
                head_dve(dve, h)
            out_gated_dve(dve, NGLA - 1)
            out_lo_dve(dve, NGLA - 1)

            def gla_o(it):
                for k in range(4):
                    x = xr[:, bass.ds(it * 4 + k, 1), :].rearrange("p a t -> p (a t)")
                    split_lo(dve, "gla_o", it, k)
                    wait_unit(dve, "gla_o", it, k)
                    dve.scalar_tensor_tensor(x, bank("gla_o", k)[:], mod[:, bass.ds(it * 4 + 64 + k, 1)], x,
                                             ALU.mult, ALU.add).then_inc(G["go_d"], 1)
                    dve.drain().then_inc(freed("gla_o", k), 1)
            run(dve, 2, gla_o)
            norm_m.dve(dve)
            mlp_up_dve(dve, "up2a", 32)
            mlp_down_dve(dve, "down2a", False, 0)
            mlp_up_dve(dve, "up2b", 48)
            mlp_down_dve(dve, "down2b", True, 88, peel_last=True)
            norm_f2.dve(dve)

        @block.tensor
        def _(pe):
            pe.wait_ge(in_ld, 32)
            norm_a.pe(pe)
            pe.wait_ge(S["mod_acc"], 1)
            for j in range(16):
                mm = pe.matmul(psum[7][:, 256 + j:257 + j], macc[:, j * P:(j + 1) * P], ones[:, 0:1], start=True, stop=True)
            mm.then_inc(S["mod_ps"], 1)
            pe.wait_ge(S["dw_lo"], 1)
            pe_first_units(pe, "ssm0", norm_a.ready, 1, (psum[4], dwh, dwl, S["dt_ps"]))

            def ssm(it, ph, k0, g, par_, prev):
                for k in range(6):
                    if prev or k > 0:
                        pe_unit(pe, ph, it, k0 + k, u_h, u_l)
                    if not prev and k == 1:
                        pe.wait_ge(S["dt_ac"], 1)
                        for a, src in ((0, dd), (1, dac)):
                            for c in range(NCH):
                                mm = pe.transpose(psum[5][:, a * 128 + c * 32:a * 128 + c * 32 + 32],
                                                  src[0:HEADS, c * CH:(c + 1) * CH], ident[0:HEADS, 0:HEADS])
                        mm.then_inc(S["dt_tp"], 1)
                    if not prev and k == 2:
                        pe.wait_ge(S["dt_tok"], 1)
                        pe.matmul(psum[4][:, 0:128], last_row, acT[:].rearrange("p c h -> p (c h)"),
                                  start=True, stop=True).then_inc(S["dt_last"], 1)
                    if not prev and k == 4:
                        pe.wait_ge(S["dt_done"], 1)
                    pe_slot(pe, k, g, par_, prev)

            def ssm2(it):
                ssm(it, "ssm", 0, it * 2 + 1, 1, True)
                ssm(it, "ssm", 6, it * 2 + 2, 0, True)

            ssm(0, "ssm0", 0, 0, 0, False)
            run(pe, 3, ssm2)
            ssm(0, "ssm7", 0, 7, 1, True)
            for k in range(8):
                pe_unit(pe, "gate_ssm", 0, k, u_h, u_l)
                if k < 6:
                    pe_slot(pe, k, 8, 0, True)
            pe.wait_ge(S["f_fin"], SSM_GROUPS)

            def ssm_out(it):
                for k in range(4):
                    half = k % 2
                    pe_unit(pe, "ssm_out", it, k, lambda t: v_h(t + 8 * half), lambda t: v_l(t + 8 * half),
                            out_i=k // 2, first=half == 0, last=half == 1)
            run(pe, 4, ssm_out)

            def plain(ph, hi, lo, ready=None):
                p = PH[ph]

                def step(it):
                    first = ready is not None and isinstance(it, int) and it == 0
                    if first:
                        pe_first_units(pe, ph, ready, rhs_hi=hi, rhs_lo=lo)
                    for k in range(2 if first else 0, p["n"]):
                        pe_unit(pe, ph, it, k, hi, lo)
                run(pe, p["steps"], step, peel_first=ready is not None)
            plain("conv", u_h, u_l)
            plain("conv_out", v_h, v_l, lambda e, n: e.wait_ge(N2["cc_l"], n))
            ada_pe(pe, 1)
            plain("w_o", u_h, u_l, lambda e, n: e.wait_ge(N2["ml"], n))
            norm_b.pe(pe)
            plain("up1a", u_h, u_l, norm_b.ready)
            mlp_down_pe(pe, "down1a", 0, peel_first=True, after_first=lambda: ada_pe(pe, 2))
            plain("up1b", u_h, u_l)
            mlp_down_pe(pe, "down1b", 16, peel_last=True, before_last=lambda: ada_pe(pe, 3))
            double_pe(pe, norm_f1, norm_g)
            pe_first_units(pe, "gla_q", norm_g.ready)
            for k in (2, 3):
                pe_unit(pe, "gla_q", 0, k, u_h, u_l)
            norm_c.pe(pe)
            pe.wait_ge(G["wa1_l"], 1)
            split_products(pe, psum[4][:], wa1h[:], wa1l[:], u_h, u_l, True, True)
            split_products(pe, psum[5][:, :TC], wa1h[:], wa1l[:], lambda t: uch[:, t, :], lambda t: ucl[:, t, :],
                           True, True, lambda t: norm_c.ready(pe, t + 1)).then_inc(G["az_d"], 1)
            for k in range(4):
                if k == 0:
                    pe.wait_ge(G["az_a"], 1)
                wait(pe, G["g_k"], k - 1)
                both(pe, "gla_k", k)
            for k in range(9):
                if k < 8:
                    if k < 2:
                        pe.wait_ge(G["g_k"], 3 + k)
                    wait(pe, G["v_a"], k - 1)
                    both(pe, "gla_v", k)
                if k >= 1:
                    j = k - 1
                    pe.wait_ge(G["v_a"], j + 1)
                    wait(pe, G["v_d"], j)
                    for i in range(TA // P):
                        b = psum[6] if i < 4 else psum[7]
                        mm = pe.transpose(b[:, (i % 4) * P:(i % 4 + 1) * P], vf[:, j % 2, i * P:(i + 1) * P], ident)
                    mm.then_inc(G["v_t"], 1)
            pe.wait_ge(G["v_d"], 8)
            for k in range(8):
                pe_unit(pe, "gla_r", 0, k, u_h, u_l)
                if k == 0:
                    gate_pe(pe, 0, 0)
                if k == 3:
                    gate_pe(pe, 0, 1)
                    keys_pe(pe, 0, 0)
                if k == 6:
                    keys_pe(pe, 0, 1)
            for b in range(4):
                pe.wait_ge(bank_free[b], PH["gla_o"]["used"][b])
            for h in range(NGLA):
                head_pe(pe, h)
            out_pe(pe, NGLA - 1)
            pe.wait_ge(G["o_ln"], NGLA)
            plain("gla_o", u_h, u_l, lambda e, n: e.wait_ge(G["o_lo"], (n + 1) // 2))
            norm_m.pe(pe)
            plain("up2a", u_h, u_l, norm_m.ready)
            mlp_down_pe(pe, "down2a", 32)
            plain("up2b", u_h, u_l)
            mlp_down_pe(pe, "down2b", 48)
            norm_f2.pe(pe)


def weight_units(i):
    import numpy as np

    def unit(w, row, col):
        return w[row:row + D, col:col + P].reshape(KT, P, P).transpose(1, 0, 2).reshape(P, KT * P)

    w_in, inner = i["w_in"][0], 2048
    gates, cb, cc, cx, z, xbc = 0, 2048, 3072, 4096, 5120, 7168
    b0, c0 = xbc + inner, xbc + inner + SSM_GROUPS * P
    out = []
    for g in range(SSM_GROUPS):
        cols = [b0 + g * P, c0 + g * P, xbc + 2 * g * P, xbc + (2 * g + 1) * P, z + 2 * g * P, z + (2 * g + 1) * P]
        out += [unit(w_in, 0, c) for c in cols]
    out += [unit(w_in, 0, gates + D + j * P) for j in range(KT)]
    out += [unit(i["w_ssm_out"][0], h * D, j * P) for j in range(KT) for h in range(2)]
    out += [unit(w_in, 0, c + j * P) for j in range(KT) for c in (cc, cx, cb, gates)]
    out += [unit(i["w_conv_out"][0], 0, j * P) for j in range(KT)]
    out += [unit(i["w_o"][0], 0, j * P) for j in range(KT)]

    def mlp(up, down):
        for half in range(2):
            for j in range(16):
                yield unit(up, 0, (16 * half + j) * P)
            for j in range(KT):
                for h in range(2):
                    yield unit(down, (2 * half + h) * D, j * P)
    out += mlp(i["w_up"][0], i["w_down"][0])
    gla = i["gla_w_in_2"][0]
    for at, n in ((0, 4), (512, 4), (1024, 8), (2048, 8)):
        out += [unit(gla, 0, at + j * P) for j in range(n)]
    out += [unit(i["gla_w_o_2"][0], 0, j * P) for j in range(KT)]
    out += mlp(i["mlp_w1_2"][0], i["mlp_w2_2"][0])
    assert len(out) == UNITS
    return np.stack(out)


def packed_params(i):
    import numpy as np

    def cols(v):
        return np.asarray(v).reshape(-1, P).T

    inner = 2048
    conv = np.asarray(i["ssm_conv_w"][0])
    bias = np.asarray(i["ssm_conv_b"][0])
    tiles = []
    for g in range(SSM_GROUPS):
        tiles += [inner + g * P, inner + SSM_GROUPS * P + g * P, 2 * g * P, (2 * g + 1) * P]
    ssm_w = np.stack([conv[tap, t:t + P] for tap in range(4) for t in tiles], axis=1)
    ssm_b = np.stack([bias[t:t + P] for t in tiles], axis=1)
    skip = np.repeat(i["d_skip"][0], 64)
    parts = {
        "b_ada": cols(i["b_ada"][0]), "ln1": cols(i["ln1"][0]), "ln2": cols(i["ln2"][0]),
        "conv_w": cols(i["conv_w"][0]), "ssm_w": ssm_w, "ssm_b": ssm_b, "ssm_norm": cols(i["ssm_norm_w"][0]),
        "d_skip": cols(skip), "dt_bias": np.tile(i["dt_bias"][0], 4)[:, None], "a_log": np.tile(i["a_log"][0], 4)[:, None],
        "final_norm": cols(i["final_norm"]), "c": cols(i["c"][0]), "c_2": cols(i["c_2"][0]), "c_ctx": cols(i["c_ctx_2"]),
        "b_ada_2": cols(i["ada_b_2"][0]), "norm1": cols(i["norm1_g_2"][0]), "norm2": cols(i["norm2_g_2"][0]),
        "b_a": cols(i["gla_b_a_2"][0]), "g_head": cols(i["gla_g_head_2"][0]), "final_2": cols(i["final_g_2"]),
    }
    for name, width in PARAMS:
        assert parts[name].shape == (P, width), (name, parts[name].shape)
    return np.ascontiguousarray(np.concatenate([parts[n] for n, _ in PARAMS], axis=1))


def constants():
    import numpy as np
    f = np.float32
    s, t = np.arange(P)[:, None], np.arange(P)[None, :]
    last = np.zeros((P, P), f)
    last[P - 1] = 1.0
    con = [np.eye(P, dtype=f), np.ones((P, P), f), last, np.where(t >= s, 0.0, -1e30).astype(f),
           np.broadcast_to((np.arange(T) % CH != 0).astype(f), (P, T)), np.full((P, 1), EPS, f),
           np.full((P, 1), EPS * EPS, f), np.full((P, P), EPS, f)]
    same = s // GC == t // GC
    at = np.arange(TA) % GC
    gcon = [np.broadcast_to((at != 0).astype(f), (P, TA)), np.broadcast_to((at != GC - 1).astype(f), (P, TA)),
            (same & (t >= s)).astype(f), (same & (t <= s)).astype(f)]
    return np.concatenate(con, axis=1), np.concatenate(gcon, axis=1)


def kernel(**inputs):
    import numpy as np
    import concourse.bacc as bacc
    from concourse.bass_utils import run_bass_kernel_spmd

    i = {k: np.asarray(v) for k, v in inputs.items()}

    def tiles(w):
        return np.ascontiguousarray(w.reshape(KT, P, P).transpose(1, 0, 2).reshape(P, KT * P))

    a1 = np.zeros((D, P), np.float32)
    for d in range(2):
        a1[:, 32 * d:32 * d + 16] = i["gla_w_a1_2"][0, d]
    con, gcon = constants()
    arrays = {
        "xT": np.ascontiguousarray(i["x"][0].T),
        "ctxT": np.ascontiguousarray(i["ctx_2"][0].T),
        "units": weight_units(i),
        "w_dt": tiles(np.concatenate([i["w_in"][0][:, 11264:11296]] * 4, axis=1)),
        "w_a1": tiles(a1),
        "w_a2": np.ascontiguousarray(i["gla_w_a2_2"][0]),
        "ada1": np.ascontiguousarray(i["w_ada"][0]),
        "ada2": np.ascontiguousarray(i["ada_w_2"][0]),
        "params": packed_params(i),
        "consts": con,
        "gconsts": gcon,
    }
    nc = bacc.Bacc("TRN2", target_bir_lowering=False, num_devices=1)
    args = [nc.dram_tensor(f"in_{n}", a.shape, mybir.dt.from_np(a.dtype), kind="ExternalInput").ap()
            for n, a in arrays.items()]
    out = nc.dram_tensor("outT", (D, T), mybir.dt.float32, kind="ExternalOutput").ap()
    build(nc, *args, out)
    r = run_bass_kernel_spmd(nc, [{f"in_{n}": a for n, a in arrays.items()}], core_ids=[0])
    return np.ascontiguousarray(r.results[0]["outT"].T)[None]
```
